# Optimizing a Trainium2 kernel written in Bass

```python
import math
import jax, jax.numpy as jnp
from jax import lax
import numpy as np

D_MODEL = 1024
BATCH = 1
SEQ = 2048
DEPTH = 1
DEC_BATCH = 8
DEC_SEQ = 16
PAST_LEN = 256

CHUNK = 64
CONV_WIDTH = 4
RMS_EPS = 1e-6
MIX_WIDTH = D_MODEL
LRU_WIDTH = MIX_WIDTH // 4
LRU_BLOCKS = 4
LRU_BLOCK = LRU_WIDTH // LRU_BLOCKS
LRU_C = 8.0
SSD_INNER = MIX_WIDTH // 4
SSD_HEAD_DIM = 64
SSD_HEADS = SSD_INNER // SSD_HEAD_DIM
SSD_GROUPS = 2
SSD_STATE = 128
SSD_CONV_DIM = SSD_INNER + 2 * SSD_GROUPS * SSD_STATE
GDN_WIDTH = MIX_WIDTH // 4
GDN_HEAD_DIM = 64
GDN_HEADS = GDN_WIDTH // GDN_HEAD_DIM
GDN_CONV_DIM = 3 * GDN_WIDTH
S5_WIDTH = MIX_WIDTH - LRU_WIDTH - SSD_INNER - GDN_WIDTH
S5_GROUP_CH = 16
S5_GROUPS = S5_WIDTH // S5_GROUP_CH
S5_STATE = 64
MEM_TOKENS = 256
MEM_HEADS = 4
MEM_HEAD_DIM = D_MODEL // MEM_HEADS
FFN_HIDDEN = ((8 * D_MODEL + 3 * 256 - 1) // (3 * 256)) * 256
IN_SIZES = (LRU_WIDTH, LRU_WIDTH, SSD_INNER, SSD_CONV_DIM, SSD_HEADS,
            GDN_CONV_DIM, GDN_WIDTH, GDN_HEADS, GDN_HEADS, S5_WIDTH)
IN_COLS = sum(IN_SIZES)

kernel_name = "hybrid_streaming_encoder_step"

def rmsnorm(x, g, eps=RMS_EPS):
    xf = x.astype(jnp.float32)
    y = xf * lax.rsqrt(jnp.mean(xf * xf, axis=-1, keepdims=True) + eps)
    return (y * g.astype(jnp.float32)).astype(x.dtype)

def l2norm(x, eps=1e-6):
    return x * lax.rsqrt(jnp.sum(x * x, axis=-1, keepdims=True) + eps)

def _split_cols(u):
    outs, start = [], 0
    for size in IN_SIZES:
        outs.append(u[..., start:start + size])
        start += size
    return outs

def _pad_time(t, pad):
    if pad == 0:
        return t
    widths = [(0, 0)] * t.ndim
    widths[1] = (0, pad)
    return jnp.pad(t, widths)

def causal_conv(x, buf, w, b=None):
    T = x.shape[1]
    xp = jnp.concatenate([buf.astype(x.dtype), x], axis=1)
    y = xp[:, 0:T] * w[0]
    for j in range(1, CONV_WIDTH):
        y = y + xp[:, j:j + T] * w[j]
    if b is not None:
        y = y + b
    return y, xp[:, T:]

def _linear_combine(e1, e2):
    a1, b1 = e1
    a2, b2 = e2
    return a2 * a1, a2 * b1 + b2

def _complex_linear_combine(e1, e2):
    ar1, ai1, br1, bi1 = e1
    ar2, ai2, br2, bi2 = e2
    return (ar2 * ar1 - ai2 * ai1, ar2 * ai1 + ai2 * ar1,
            ar2 * br1 - ai2 * bi1 + br2, ar2 * bi1 + ai2 * br1 + bi2)

def rglru_mixer(gate_in, x_in, h0, buf, conv_w, conv_b, w_r, b_r, w_i, b_i, lam):
    xc, new_buf = causal_conv(x_in, buf, conv_w, conv_b)
    B_, T, _ = xc.shape
    xb = xc.reshape(B_, T, LRU_BLOCKS, LRU_BLOCK)
    r = jax.nn.sigmoid(jnp.einsum('btnc,ncd->btnd', xb, w_r).reshape(B_, T, LRU_WIDTH) + b_r)
    i = jax.nn.sigmoid(jnp.einsum('btnc,ncd->btnd', xb, w_i).reshape(B_, T, LRU_WIDTH) + b_i)
    log_a = -LRU_C * r * jax.nn.softplus(-lam)
    a = jnp.exp(log_a)
    bt = jnp.sqrt(-jnp.expm1(2.0 * log_a)) * (i * xc)
    bt = bt.at[:, 0].add(a[:, 0] * h0)
    _, hs = lax.associative_scan(_linear_combine, (a, bt), axis=1)
    y = hs * jax.nn.gelu(gate_in)
    return y, hs[:, -1], new_buf

def ssd_scan(x, dt, a, bm, cm, h0):
    B_, T, H, P = x.shape
    cs = min(CHUNK, T)
    nc = -(-T // cs)
    pad = nc * cs - T
    rep = H // SSD_GROUPS
    bh = jnp.repeat(bm, rep, axis=2)
    ch = jnp.repeat(cm, rep, axis=2)
    x, dt, bh, ch = [_pad_time(t, pad).reshape((B_, nc, cs) + t.shape[2:]) for t in (x, dt, bh, ch)]
    g = jnp.cumsum(dt * a, axis=2)
    causal = jnp.tril(jnp.ones((cs, cs), bool))
    seg = jnp.exp(jnp.where(causal[None, None, :, :, None],
                            g[:, :, :, None, :] - g[:, :, None, :, :], -jnp.inf))
    scores = jnp.einsum('bcthn,bcshn->bctsh', ch, bh) * seg
    xdt = x * dt[..., None]
    y_diag = jnp.einsum('bctsh,bcshp->bcthp', scores, xdt)
    to_end = jnp.exp(g[:, :, -1:, :] - g)
    chunk_states = jnp.einsum('bcsh,bcshp,bcshn->bchpn', to_end, xdt, bh)
    chunk_decay = jnp.exp(g[:, :, -1, :])

    def step(h, inp):
        st, dec = inp
        return dec[..., None, None] * h + st, h

    h_last, h_start = lax.scan(step, h0.astype(jnp.float32),
                               (jnp.moveaxis(chunk_states, 1, 0), jnp.moveaxis(chunk_decay, 1, 0)))
    h_start = jnp.moveaxis(h_start, 0, 1)
    y_off = jnp.einsum('bcthn,bchpn->bcthp', ch * jnp.exp(g)[..., None], h_start)
    y = (y_diag + y_off).reshape(B_, nc * cs, H, P)[:, :T]
    return y, h_last

def ssd_mixer(z, xbc, dt_raw, h0, buf, conv_w, conv_b, dt_bias, a_log, d_skip, norm_g):
    xbc, new_buf = causal_conv(xbc, buf, conv_w, conv_b)
    xbc = jax.nn.silu(xbc)
    B_, T, _ = xbc.shape
    gn = SSD_GROUPS * SSD_STATE
    xs = xbc[..., :SSD_INNER].reshape(B_, T, SSD_HEADS, SSD_HEAD_DIM)
    bm = xbc[..., SSD_INNER:SSD_INNER + gn].reshape(B_, T, SSD_GROUPS, SSD_STATE)
    cm = xbc[..., SSD_INNER + gn:].reshape(B_, T, SSD_GROUPS, SSD_STATE)
    dt = jax.nn.softplus(dt_raw + dt_bias)
    a = -jnp.exp(a_log.astype(jnp.float32))
    y, h_last = ssd_scan(xs, dt, a, bm, cm, h0)
    y = y + d_skip[:, None] * xs
    gs = SSD_INNER // SSD_GROUPS
    yg = (y.reshape(B_, T, SSD_INNER) * jax.nn.silu(z)).reshape(B_, T, SSD_GROUPS, gs)
    yg = rmsnorm(yg, norm_g.reshape(SSD_GROUPS, gs))
    return yg.reshape(B_, T, SSD_INNER), h_last, new_buf

def gated_delta_scan(q, k, v, g, beta, s0):
    B_, T, H, DK = q.shape
    DV = v.shape[-1]
    cs = min(CHUNK, T)
    nc = -(-T // cs)
    pad = nc * cs - T

    def blk(t):
        t = _pad_time(t, pad).reshape((B_, nc, cs) + t.shape[2:])
        return jnp.swapaxes(t, 2, 3)

    q, k, v, g, beta = [blk(t) for t in (q, k, v, g, beta)]
    gc = jnp.cumsum(g, axis=-1)
    diff = gc[..., :, None] - gc[..., None, :]
    incl = jnp.tril(jnp.ones((cs, cs), bool))
    strict = jnp.tril(jnp.ones((cs, cs), bool), -1)
    decay = jnp.exp(jnp.where(incl, diff, -jnp.inf))
    kk = jnp.einsum('bnhtd,bnhsd->bnhts', k, k)
    lower = jnp.where(strict, beta[..., :, None] * kk * decay, 0.0)
    m = lower + jnp.eye(cs, dtype=lower.dtype)
    rhs = jnp.concatenate([beta[..., None] * v, (beta * jnp.exp(gc))[..., None] * k], axis=-1)
    sol = lax.linalg.triangular_solve(m, rhs, left_side=True, lower=True, unit_diagonal=True)
    u, w = sol[..., :DV], sol[..., DV:]
    qk = jnp.einsum('bnhtd,bnhsd->bnhts', q, k) * decay
    q_dec = q * jnp.exp(gc)[..., None]
    k_dec = k * jnp.exp(gc[..., -1:] - gc)[..., None]
    chunk_decay = jnp.exp(gc[..., -1])

    def step(s, inp):
        qd, kd, uc, wc, qkc, dec = inp
        delta = uc - jnp.einsum('bhsk,bhkv->bhsv', wc, s)
        o = jnp.einsum('bhtk,bhkv->bhtv', qd, s) + jnp.einsum('bhts,bhsv->bhtv', qkc, delta)
        s = dec[..., None, None] * s + jnp.einsum('bhsk,bhsv->bhkv', kd, delta)
        return s, o

    xs = tuple(jnp.moveaxis(t, 1, 0) for t in (q_dec, k_dec, u, w, qk, chunk_decay))
    s_last, o = lax.scan(step, s0.astype(jnp.float32), xs)
    o = jnp.swapaxes(jnp.moveaxis(o, 0, 1), 2, 3).reshape(B_, nc * cs, H, DV)[:, :T]
    return o, s_last

def gdn_mixer(qkv, z, beta_raw, a_raw, s0, buf, conv_w, dt_bias, a_log, norm_g):
    qkv, new_buf = causal_conv(qkv, buf, conv_w)
    qkv = jax.nn.silu(qkv)
    B_, T, _ = qkv.shape
    q, k, v = [qkv[..., j * GDN_WIDTH:(j + 1) * GDN_WIDTH].reshape(B_, T, GDN_HEADS, GDN_HEAD_DIM)
               for j in range(3)]
    q = l2norm(q) * GDN_HEAD_DIM ** -0.5
    k = l2norm(k)
    beta = jax.nn.sigmoid(beta_raw)
    g = -jnp.exp(a_log) * jax.nn.softplus(a_raw + dt_bias)
    o, s_last = gated_delta_scan(q, k, v, g, beta, s0)
    o = rmsnorm(o, norm_g) * jax.nn.silu(z.reshape(B_, T, GDN_HEADS, GDN_HEAD_DIM))
    return o.reshape(B_, T, GDN_WIDTH), s_last, new_buf

def s5_mixer(u_in, s0_re, s0_im, a_re, a_im, log_dt, b_re, b_im, c_re, c_im, d_skip, w_glu, b_glu):
    B_, T, _ = u_in.shape
    u = u_in.reshape(B_, T, S5_GROUPS, S5_GROUP_CH)
    a_re = a_re.astype(jnp.float32)
    a_im = a_im.astype(jnp.float32)
    step = jnp.exp(log_dt.astype(jnp.float32))[:, None]
    mag = jnp.exp(a_re * step)
    ang = a_im * step
    lb_re, lb_im = mag * jnp.cos(ang), mag * jnp.sin(ang)
    den = a_re * a_re + a_im * a_im
    f_re = ((lb_re - 1.0) * a_re + lb_im * a_im) / den
    f_im = (lb_im * a_re - (lb_re - 1.0) * a_im) / den
    b_re = b_re.astype(jnp.float32)
    b_im = b_im.astype(jnp.float32)
    bb_re = f_re[..., None] * b_re - f_im[..., None] * b_im
    bb_im = f_re[..., None] * b_im + f_im[..., None] * b_re
    bu_re = jnp.einsum('btgc,gnc->btgn', u, bb_re)
    bu_im = jnp.einsum('btgc,gnc->btgn', u, bb_im)
    bu_re = bu_re.at[:, 0].add(lb_re * s0_re - lb_im * s0_im)
    bu_im = bu_im.at[:, 0].add(lb_re * s0_im + lb_im * s0_re)
    shape = bu_re.shape
    _, _, x_re, x_im = lax.associative_scan(
        _complex_linear_combine,
        (jnp.broadcast_to(lb_re, shape), jnp.broadcast_to(lb_im, shape), bu_re, bu_im), axis=1)
    y = jnp.einsum('btgn,gcn->btgc', x_re, c_re) - jnp.einsum('btgn,gcn->btgc', x_im, c_im)
    y = y.reshape(B_, T, S5_WIDTH) + d_skip * u_in
    y = jax.nn.gelu(y)
    y = y * jax.nn.sigmoid(jnp.einsum('btc,cd->btd', y, w_glu) + b_glu)
    return y, x_re[:, -1], x_im[:, -1]

def memory_kv(mem, g, w_k, w_v):
    m = rmsnorm(mem, g)
    B_, M, _ = m.shape
    k = jnp.einsum('bmd,de->bme', m, w_k).reshape(B_, M, MEM_HEADS, MEM_HEAD_DIM)
    v = jnp.einsum('bmd,de->bme', m, w_v).reshape(B_, M, MEM_HEADS, MEM_HEAD_DIM)
    return k, v

def cross_attend(h, k, v, w_q, w_o):
    B_, T, _ = h.shape
    q = jnp.einsum('btd,de->bte', h, w_q).reshape(B_, T, MEM_HEADS, MEM_HEAD_DIM)
    s = jnp.einsum('bthe,bmhe->bhtm', q, k.astype(q.dtype)).astype(jnp.float32) * (MEM_HEAD_DIM ** -0.5)
    p = jax.nn.softmax(s, axis=-1).astype(h.dtype)
    o = jnp.einsum('bhtm,bmhe->bthe', p, v.astype(h.dtype)).reshape(B_, T, D_MODEL)
    return jnp.einsum('btd,de->bte', o, w_o)

def swiglu(h, w_gate, w_up, w_down):
    a = jnp.einsum('btd,df->btf', h, w_gate)
    b = jnp.einsum('btd,df->btf', h, w_up)
    return jnp.einsum('btf,fd->btd', jax.nn.silu(a) * b, w_down)

def setup_inputs(seed: int = 0) -> dict:
    key = jax.random.key(seed)
    ks = iter(list(jax.random.split(key, 64)))
    f32 = jnp.float32

    def nrm(shape, scale):
        return jax.random.normal(next(ks), shape, f32) * scale

    def unif(shape, lo, hi):
        return jax.random.uniform(next(ks), shape, f32, lo, hi)

    def gain(shape):
        return 1.0 + nrm(shape, 0.02)

    def inv_softplus_dt(shape):
        dt = jnp.exp(unif(shape, math.log(1e-3), math.log(1e-1)))
        return dt + jnp.log(-jnp.expm1(-dt))

    L = DEPTH
    K1 = CONV_WIDTH - 1
    d = {}
    d["x_prompt"] = nrm((BATCH, SEQ, D_MODEL), 1.0)
    d["x_sample"] = nrm((DEC_BATCH, DEC_SEQ, D_MODEL), 1.0)
    d["mem_prompt"] = nrm((BATCH, MEM_TOKENS, D_MODEL), 1.0)
    d["state_lru_h"] = nrm((L, DEC_BATCH, LRU_WIDTH), 0.5)
    d["cache_lru_conv"] = nrm((L, DEC_BATCH, K1, LRU_WIDTH), 1.0)
    d["state_ssd"] = nrm((L, DEC_BATCH, SSD_HEADS, SSD_HEAD_DIM, SSD_STATE), 0.1)
    d["cache_ssd_conv"] = nrm((L, DEC_BATCH, K1, SSD_CONV_DIM), 1.0)
    d["state_gdn"] = nrm((L, DEC_BATCH, GDN_HEADS, GDN_HEAD_DIM, GDN_HEAD_DIM), 0.1)
    d["cache_gdn_conv"] = nrm((L, DEC_BATCH, K1, GDN_CONV_DIM), 1.0)
    d["state_s5_re"] = nrm((L, DEC_BATCH, S5_GROUPS, S5_STATE), 0.05)
    d["state_s5_im"] = nrm((L, DEC_BATCH, S5_GROUPS, S5_STATE), 0.05)
    d["cache_mem_k"] = nrm((L, DEC_BATCH, MEM_TOKENS, MEM_HEADS, MEM_HEAD_DIM), 1.0)
    d["cache_mem_v"] = nrm((L, DEC_BATCH, MEM_TOKENS, MEM_HEADS, MEM_HEAD_DIM), 1.0)
    d["norm_mix_g"] = gain((L, D_MODEL))
    d["w_in"] = nrm((L, D_MODEL, IN_COLS), D_MODEL ** -0.5)
    d["w_out"] = nrm((L, MIX_WIDTH, D_MODEL), 0.5 * MIX_WIDTH ** -0.5)
    d["lru_conv_w"] = nrm((L, CONV_WIDTH, LRU_WIDTH), CONV_WIDTH ** -0.5)
    d["lru_conv_b"] = nrm((L, LRU_WIDTH), 0.02)
    d["lru_w_r"] = nrm((L, LRU_BLOCKS, LRU_BLOCK, LRU_BLOCK), LRU_BLOCK ** -0.5)
    d["lru_b_r"] = nrm((L, LRU_WIDTH), 0.1)
    d["lru_w_i"] = nrm((L, LRU_BLOCKS, LRU_BLOCK, LRU_BLOCK), LRU_BLOCK ** -0.5)
    d["lru_b_i"] = nrm((L, LRU_WIDTH), 0.1)
    s_lru = unif((L, LRU_WIDTH), 0.9, 0.999) ** (1.0 / LRU_C)
    d["lru_lambda"] = jnp.log(s_lru) - jnp.log1p(-s_lru)
    d["ssd_conv_w"] = nrm((L, CONV_WIDTH, SSD_CONV_DIM), CONV_WIDTH ** -0.5)
    d["ssd_conv_b"] = nrm((L, SSD_CONV_DIM), 0.02)
    d["ssd_dt_bias"] = inv_softplus_dt((L, SSD_HEADS))
    d["ssd_a_log"] = jnp.log(unif((L, SSD_HEADS), 1.0, 16.0))
    d["ssd_d"] = gain((L, SSD_HEADS))
    d["ssd_norm_g"] = gain((L, SSD_INNER))
    d["gdn_conv_w"] = nrm((L, CONV_WIDTH, GDN_CONV_DIM), CONV_WIDTH ** -0.5)
    d["gdn_dt_bias"] = inv_softplus_dt((L, GDN_HEADS))
    d["gdn_a_log"] = jnp.log(unif((L, GDN_HEADS), 1.0, 16.0))
    d["gdn_norm_g"] = gain((L, GDN_HEAD_DIM))
    d["s5_a_re"] = -0.5 + nrm((L, S5_GROUPS, S5_STATE), 0.01)
    d["s5_a_im"] = jnp.pi * jnp.arange(S5_STATE, dtype=f32) + nrm((L, S5_GROUPS, S5_STATE), 0.01)
    d["s5_log_dt"] = unif((L, S5_GROUPS), math.log(1e-3), math.log(1e-1))
    d["s5_b_re"] = nrm((L, S5_GROUPS, S5_STATE, S5_GROUP_CH), (2 * S5_GROUP_CH) ** -0.5)
    d["s5_b_im"] = nrm((L, S5_GROUPS, S5_STATE, S5_GROUP_CH), (2 * S5_GROUP_CH) ** -0.5)
    d["s5_c_re"] = nrm((L, S5_GROUPS, S5_GROUP_CH, S5_STATE), S5_STATE ** -0.5)
    d["s5_c_im"] = nrm((L, S5_GROUPS, S5_GROUP_CH, S5_STATE), S5_STATE ** -0.5)
    d["s5_d"] = gain((L, S5_WIDTH))
    d["s5_w_glu"] = nrm((L, S5_WIDTH, S5_WIDTH), S5_WIDTH ** -0.5)
    d["s5_b_glu"] = nrm((L, S5_WIDTH), 0.02)
    d["norm_mem_g"] = gain((L, D_MODEL))
    d["norm_cross_g"] = gain((L, D_MODEL))
    d["w_cq"] = nrm((L, D_MODEL, D_MODEL), D_MODEL ** -0.5)
    d["w_ck"] = nrm((L, D_MODEL, D_MODEL), D_MODEL ** -0.5)
    d["w_cv"] = nrm((L, D_MODEL, D_MODEL), D_MODEL ** -0.5)
    d["w_co"] = nrm((L, D_MODEL, D_MODEL), 0.5 * D_MODEL ** -0.5)
    d["norm_ffn_g"] = gain((L, D_MODEL))
    d["w_ffn_gate"] = nrm((L, D_MODEL, FFN_HIDDEN), D_MODEL ** -0.5)
    d["w_ffn_up"] = nrm((L, D_MODEL, FFN_HIDDEN), D_MODEL ** -0.5)
    d["w_ffn_down"] = nrm((L, FFN_HIDDEN, D_MODEL), 0.5 * FFN_HIDDEN ** -0.5)
    d["norm_final_g"] = gain((D_MODEL,))
    return d

def reference(x_prompt, x_sample, mem_prompt,
              state_lru_h, cache_lru_conv, state_ssd, cache_ssd_conv, state_gdn, cache_gdn_conv,
              state_s5_re, state_s5_im, cache_mem_k, cache_mem_v,
              norm_mix_g, w_in, w_out,
              lru_conv_w, lru_conv_b, lru_w_r, lru_b_r, lru_w_i, lru_b_i, lru_lambda,
              ssd_conv_w, ssd_conv_b, ssd_dt_bias, ssd_a_log, ssd_d, ssd_norm_g,
              gdn_conv_w, gdn_dt_bias, gdn_a_log, gdn_norm_g,
              s5_a_re, s5_a_im, s5_log_dt, s5_b_re, s5_b_im, s5_c_re, s5_c_im, s5_d, s5_w_glu, s5_b_glu,
              norm_mem_g, norm_cross_g, w_cq, w_ck, w_cv, w_co,
              norm_ffn_g, w_ffn_gate, w_ffn_up, w_ffn_down, norm_final_g):
    f32 = jnp.float32

    def layer(l, x, mem_k, mem_v, st):
        lru_h0, lru_buf0, ssd_h0, ssd_buf0, gdn_s0, gdn_buf0, s5_re0, s5_im0 = st
        h = rmsnorm(x, norm_mix_g[l])
        u = jnp.einsum('btd,dc->btc', h, w_in[l]).astype(f32)
        a_gate, a_x, b_z, b_xbc, b_dt, c_qkv, c_z, c_beta, c_a, d_u = _split_cols(u)
        y_a, lru_h, lru_buf = rglru_mixer(a_gate, a_x, lru_h0, lru_buf0, lru_conv_w[l], lru_conv_b[l],
                                          lru_w_r[l], lru_b_r[l], lru_w_i[l], lru_b_i[l], lru_lambda[l])
        y_b, ssd_h, ssd_buf = ssd_mixer(b_z, b_xbc, b_dt, ssd_h0, ssd_buf0, ssd_conv_w[l], ssd_conv_b[l],
                                        ssd_dt_bias[l], ssd_a_log[l], ssd_d[l], ssd_norm_g[l])
        y_c, gdn_s, gdn_buf = gdn_mixer(c_qkv, c_z, c_beta, c_a, gdn_s0, gdn_buf0, gdn_conv_w[l],
                                        gdn_dt_bias[l], gdn_a_log[l], gdn_norm_g[l])
        y_d, s5_re, s5_im = s5_mixer(d_u, s5_re0, s5_im0, s5_a_re[l], s5_a_im[l], s5_log_dt[l],
                                     s5_b_re[l], s5_b_im[l], s5_c_re[l], s5_c_im[l], s5_d[l],
                                     s5_w_glu[l], s5_b_glu[l])
        mix = jnp.concatenate([y_a, y_b, y_c, y_d], axis=-1).astype(x.dtype)
        x = x + jnp.einsum('btc,cd->btd', mix, w_out[l])
        x = x + cross_attend(rmsnorm(x, norm_cross_g[l]), mem_k, mem_v, w_cq[l], w_co[l])
        x = x + swiglu(rmsnorm(x, norm_ffn_g[l]), w_ffn_gate[l], w_ffn_up[l], w_ffn_down[l])
        return x, (lru_h, lru_buf, ssd_h, ssd_buf, gdn_s, gdn_buf, s5_re, s5_im)

    bp = x_prompt.shape[0]
    k1 = CONV_WIDTH - 1
    zero_states = (jnp.zeros((bp, LRU_WIDTH), f32),
                   jnp.zeros((bp, k1, LRU_WIDTH), f32),
                   jnp.zeros((bp, SSD_HEADS, SSD_HEAD_DIM, SSD_STATE), f32),
                   jnp.zeros((bp, k1, SSD_CONV_DIM), f32),
                   jnp.zeros((bp, GDN_HEADS, GDN_HEAD_DIM, GDN_HEAD_DIM), f32),
                   jnp.zeros((bp, k1, GDN_CONV_DIM), f32),
                   jnp.zeros((bp, S5_GROUPS, S5_STATE), f32),
                   jnp.zeros((bp, S5_GROUPS, S5_STATE), f32))

    xp, xs = x_prompt, x_sample
    p_states, s_states, p_mk, p_mv = [], [], [], []
    for l in range(DEPTH):
        mk, mv = memory_kv(mem_prompt, norm_mem_g[l], w_ck[l], w_cv[l])
        xp, sp = layer(l, xp, mk, mv, zero_states)
        s_in = (state_lru_h[l], cache_lru_conv[l], state_ssd[l], cache_ssd_conv[l],
                state_gdn[l], cache_gdn_conv[l], state_s5_re[l], state_s5_im[l])
        xs, ss = layer(l, xs, cache_mem_k[l], cache_mem_v[l], s_in)
        p_states.append(sp)
        s_states.append(ss)
        p_mk.append(mk)
        p_mv.append(mv)

    y_prompt = rmsnorm(xp, norm_final_g)
    y_sample = rmsnorm(xs, norm_final_g)

    def stack(states, j):
        return jnp.stack([st[j] for st in states], axis=0)

    p_lru_h, p_lru_conv, p_ssd, p_ssd_conv = stack(p_states, 0), stack(p_states, 1), stack(p_states, 2), stack(p_states, 3)
    p_gdn, p_gdn_conv, p_s5_re, p_s5_im = stack(p_states, 4), stack(p_states, 5), stack(p_states, 6), stack(p_states, 7)
    p_mem_k = jnp.stack(p_mk, axis=0)
    p_mem_v = jnp.stack(p_mv, axis=0)
    s_lru_h, s_lru_conv, s_ssd, s_ssd_conv = stack(s_states, 0), stack(s_states, 1), stack(s_states, 2), stack(s_states, 3)
    s_gdn, s_gdn_conv, s_s5_re, s_s5_im = stack(s_states, 4), stack(s_states, 5), stack(s_states, 6), stack(s_states, 7)
    return (y_prompt, y_sample,
            p_lru_h, p_lru_conv, p_ssd, p_ssd_conv, p_gdn, p_gdn_conv, p_s5_re, p_s5_im, p_mem_k, p_mem_v,
            s_lru_h, s_lru_conv, s_ssd, s_ssd_conv, s_gdn, s_gdn_conv, s_s5_re, s_s5_im)


_drawn_inputs = setup_inputs


def setup_inputs(seed=0):
    import zlib

    import numpy as np

    out = dict(_drawn_inputs(seed))
    spreads = {}
    factors = {'ssd_d': 8.0,
     'ssd_norm_g': 8.0,
     'gdn_norm_g': 8.0,
     's5_a_re': 4.098,
     's5_c_re': 8.0,
     's5_c_im': 8.0,
     's5_d': 8.0,
     's5_b_glu': 8.0,
     'norm_mem_g': 2.82,
     'norm_cross_g': 8.0,
     'norm_ffn_g': 7.242,
     'norm_final_g': 2.892}
    for name, (base, spread) in spreads.items():
        noise = np.random.default_rng([zlib.crc32(name.encode()), seed]).standard_normal(out[name].shape)
        drawn = base * np.exp(spread * noise) if base else spread * noise
        out[name] = __import__('jax').numpy.asarray(drawn.astype(out[name].dtype))
    for name, factor in factors.items():
        out[name] = (out[name] * factor).astype(out[name].dtype)
    return out
```

```python
from contextlib import ExitStack

import numpy as np

import concourse.bass as bass
from concourse import mybir

F32 = mybir.dt.float32
F32R = mybir.dt.float32r
ACT = mybir.ActivationFunctionType
ALU = mybir.AluOpType
AX_X = mybir.AxisListType.X

P = 128
D = 1024
KD = D // P
PROMPT, SEQS, SEQ_LEN = 2048, 8, 16
TOKENS = PROMPT + SEQS * SEQ_LEN
TILES = TOKENS // P
PASSES = ((0, 6), (6, 12), (12, 17))
CMAX = 6 * P
MEM = 256
HEADS, HD = 4, 256
FFN = 2816
ROUNDS = FFN // 256
EPS = 1e-6
SLAB = 2048

U_TILES, GATE, CONV, DU = 18, 0, 2, 16
N_CONV = 14
N_SMALL = 12
SLABS_IN = 11
LEVELS = (1, 2, 4, 8, 16, 32, 64)

_MIX = [("U", 128), ("L", 128), ("strict", 128), ("Us", 128), ("Ls", 128), ("stricts", 128),
        ("ident", 128), ("ones", 128), ("levels", 7 * 128), ("seqsel", 8),
        ("ct_re", 1024), ("ct_im", 1024), ("glu", 512), ("w_r", 256), ("w_i", 256),
        ("ssd_norm", 256), ("gdn_norm", 256), ("ssd_d", 256)]
MIX, _n = {}, 0
for _name, _w in _MIX:
    MIX[_name] = (_n, _w)
    _n += _w
MIX_COLS = _n
_PAR = [("conv_w", 4 * N_CONV), ("conv_b", N_CONV), ("s5_d", 2), ("b_glu", 2), ("b_r", 2), ("b_i", 2),
        ("lam", 2), ("bias8", 8), ("alog8", 8), ("g_mix", 8), ("g_mem", 8), ("g_cross", 8), ("g_ffn", 8),
        ("g_final", 8)]
PAR, _n = {}, 0
for _name, _w in _PAR:
    PAR[_name] = (_n, _w)
    _n += _w
PAR_COLS = _n
EGC, EGE, ETOT, BETA, DT, G8 = 0, 8, 16, 24, 28, 32
TS_COLS = 40
TWO_PI_HI, TWO_PI_MID = 6.28125, 0.0019353071693331003
TWO_PI_LO = 2 * np.pi - TWO_PI_HI - TWO_PI_MID
LN2_HI = 0.693359375
LN2_LO = float(np.log(2) - LN2_HI)
ROUND_MAGIC = 12582912.0


class Count:

    def __init__(self, sem, unit=1):
        self.sem, self.unit, self.n, self.i, self.per = sem, unit, 0, None, 0

    def begin(self, i, per):
        self.i, self.per, self.start = i, per, self.n

    def end(self, times):
        assert self.n - self.start == self.per, (self.n, self.start, self.per)
        self.n, self.i = self.start + self.per * times, None

    def next(self):
        self.n += 1
        return self.value()

    def value(self, back=0):
        v = (self.n - back) * self.unit
        return v if self.i is None else self.i * (self.per * self.unit) + v


class Loop:

    def __init__(self, eng, times, counts):
        self.eng, self.times, self.counts = eng, times, counts

    def __enter__(self):
        self.cm = self.eng.Fori(0, self.times)
        i = self.cm.__enter__()
        for c, per in self.counts:
            c.begin(i, per)
        return i

    def __exit__(self, *a):
        r = self.cm.__exit__(*a)
        if a[0] is None:
            for c, _ in self.counts:
                c.end(self.times)
        return r


def groups(p):
    n = (PASSES[p][1] - PASSES[p][0]) * P
    return ((0, 384), (384, n - 384))


def program(nc, t):
    ctx = ExitStack()
    with ctx:
        names = iter(range(10000))

        def sb(stack, name, shape, dt=F32):
            return stack.enter_context(nc.sbuf_tensor(f"{name}_sb{next(names)}", shape, dt))

        def sem(name):
            return ctx.enter_context(nc.semaphore(name))

        banks = ctx.enter_context(nc.psum_tensor("banks", [P, 8, 512], F32))

        par = sb(ctx, "par", [P, PAR_COLS])
        ones = sb(ctx, "ones", [P, P])
        ssd_h = sb(ctx, "ssd_h", [P, 256])
        gdn_s = sb(ctx, "gdn_s", [P, 2, P])
        s5_x = sb(ctx, "s5_x", [P, 2, 8])
        lru_h = sb(ctx, "lru_h", [P, 2])
        mag = sb(ctx, "mag", [P, 8])
        lru_c = sb(ctx, "lru_c", [P, 4])
        half_b = sb(ctx, "half_b", [P, 6])
        nea8 = sb(ctx, "nea8", [P, 8])
        eps = sb(ctx, "eps", [P, 1])
        raw12 = sb(ctx, "raw12", [P, 6, N_SMALL])
        tsc = sb(ctx, "tsc", [P, 6, TS_COLS])

        def pcol(name, k=0, n=1):
            return par[:, PAR[name][0] + k:PAR[name][0] + k + n]

        with ExitStack() as st:
            W5 = 1032
            s5p = sb(st, "s5p", [P, 3, W5])
            s5b = sb(st, "s5b", [P, 2, 1024])
            sw = [sb(st, f"sw{i}", [P, W5]) for i in range(14)]
            prep = sb(st, "prep", [P, 4, 8, P])
            sm = sb(st, "sm", [P, 12])
            ex = sb(st, "ex", [P, 5, 8])
            exi = sb(st, "exi", [P, 8], mybir.dt.int32)
            zero3 = sb(st, "zero3", [P, U_TILES, 3])

        with ExitStack() as st:
            x = sb(st, "x", [P, KD, CMAX])
            hh = sb(st, "hh", [P, KD, CMAX], F32R)
            hl = sb(st, "hl", [P, KD, CMAX], F32R)
            a_raw = sb(st, "a_raw", [P, SLAB])
            a_hi = [sb(st, f"a_hi{s}", [P, SLAB], F32R) for s in range(2)]
            a_lo = [sb(st, f"a_lo{s}", [P, SLAB], F32R) for s in range(2)]
            b_raw = sb(st, "b_raw", [P, SLAB])
            b_hi = sb(st, "b_hi", [P, SLAB], F32R)
            b_lo = sb(st, "b_lo", [P, SLAB], F32R)
            g_hi = sb(st, "g_hi", [P, 2, CMAX], F32R)
            g_lo = sb(st, "g_lo", [P, 2, CMAX], F32R)
            stage = [sb(st, f"stage{s}", [P, 2, CMAX]) for s in range(2)]
            hf = sb(st, "hf", [P, 2, 384])
            sq = sb(st, "sq", [P, 2, 384])
            rms = sb(st, "rms", [P, 384])
            rstd = sb(st, "rstd", [P, 384])
            kv = sb(st, "kv", [P, 2, 2, 512])
            pr = sb(st, "pr", [P, 2, MEM])
            soft = sb(st, "soft", [P, 2, 4])
            kvs = sb(st, "kvs", [P, 2, 512])
            prs = sb(st, "prs", [P, SEQS, MEM])
            softs = sb(st, "softs", [P, 3, SEQS])
            prs_t = sb(st, "prs_t", [P, SEQS, 2, SEQ_LEN])
            ident = sb(st, "ident", [P, P])
            ws = sb(st, "ws", [P, KD * N_SMALL])
            ws_hi = sb(st, "ws_hi", [P, KD, N_SMALL], F32R)
            ws_lo = sb(st, "ws_lo", [P, KD, N_SMALL], F32R)

        with ExitStack() as st:
            mixc = sb(st, "mixc", [P, MIX_COLS])
            mprep = sb(st, "mprep", [P, 4, 8, P])
            m = {}
            for name, cols in dict(
                    u=U_TILES * 152, cv=N_CONV * P, z=512, sz=512, cur=TS_COLS, lg=8 * P, dec=8 * P, decs=512,
                    tok_x=512, tok_qk=512, tok_v=256, xdt=256, xw=256, xsd=256, sc=512, yo=256, ys=256,
                    ytm=512, sqk=512, n8=16, qkn=512, kb=256, qd=256, wk=256, kd=256, vb=256, chT=8 * P,
                    MT=512, ML=7 * 512, S=512, T=512, X=512, qkd=512, uu=256, wT=256, delta=256, gz=256,
                    th=512, la=256, lt=256, lb=256, hs=256, gg=256, bre=1024, bim=1024, p1=1024, p2=1024,
                    p3=1024, p4=1024, s5y=256, s5t=256, ych=1024, tmp8=128, tk=8 * 64, decay5=8 * P, c5=4 * 64,
                    ssd_hs=SEQS * 256, gdn_ss=SEQS * 256, s5_xs=2 * 8 * SEQS, lru_hs=2 * SEQS, etotb=8 * SEQS,
                    tail=N_CONV * SEQS * 3).items():
                m[name] = sb(st, "m_" + name, [P, cols])
            ssd_hs = m["ssd_hs"][:].rearrange("p (s c) -> p s c", s=SEQS)
            gdn_ss = m["gdn_ss"][:].rearrange("p (s j c) -> p s j c", s=SEQS, j=2)
            s5_xs = m["s5_xs"][:].rearrange("p (r t s) -> p r t s", r=2, t=8)
            lru_hs = m["lru_hs"][:].rearrange("p (t s) -> p t s", t=2)
            etotb = m["etotb"][:].rearrange("p (s h) -> p s h", s=SEQS)
        u_dram = nc.dram_tensor("u_dram", [P, U_TILES, 3 + TOKENS], F32, kind="Internal").ap()
        z_dram = nc.dram_tensor("z_dram", [TOKENS, 512], F32, kind="Internal").ap()
        y_dram = nc.dram_tensor("y_dram", [P, KD, TOKENS], F32, kind="Internal").ap()
        prep_dram = nc.dram_tensor("prep_dram", [P, 4 * 8 * P], F32, kind="Internal").ap()

        meet_s = sem("all_engines_met")
        a_loaded = sem("a_slab_loaded")
        a_hi_s = [sem(f"a_hi_done{s}") for s in range(2)]
        a_lo_s = [sem(f"a_lo_done{s}") for s in range(2)]
        a_used_s = [sem(f"a_slab_used{s}") for s in range(2)]
        b_loaded, b_hi_s, b_lo_s, b_used_s = sem("b_slab_loaded"), sem("b_hi_done"), sem("b_lo_done"), sem("b_slab_used")
        full_s = [sem(f"bank_full{b}") for b in range(8)]
        free_s = [sem(f"bank_free{b}") for b in range(8)]
        x_loaded = sem("x_loaded")
        par_loaded = sem("par_loaded")
        sq_done, sq_used = sem("square_done"), sem("square_used")
        rms_done, rstd_done = sem("rms_done"), sem("rstd_done")
        hf_done, hh_done, hl_done = sem("h_float_done"), sem("h_hi_done"), sem("h_lo_done")
        x_summed = sem("x_summed")
        stage_full = [sem(f"stage_full{s}") for s in range(2)]
        stage_stored = [sem(f"stage_stored{s}") for s in range(2)]
        y_stored = sem("y_stored")
        y_loaded = sem("y_loaded")
        q_done, p_done, pt_done = sem("q_done"), sem("p_done"), sem("p_transposed")
        p_max, p_exp = sem("p_max"), sem("p_exp")
        kv_loaded = [sem(f"kv_loaded{s}") for s in range(2)]
        av_done, g_hi_done, g_lo_done, gate_done = sem("av_done"), sem("g_hi_done"), sem("g_lo_done"), sem("gate_done")
        kvs_loaded = [sem(f"kvs_loaded{s}") for s in range(2)]
        kvs_used = [sem(f"kvs_used{s}") for s in range(2)]
        qs_used = sem("q_sample_used")
        ws_loaded, ws_hi_done, ws_lo_done, ident_loaded = (
            sem("ws_loaded"), sem("ws_hi_done"), sem("ws_lo_done"), sem("ident_loaded"))
        up_done, out_ready, out_stored = sem("up_done"), sem("out_ready"), sem("out_stored")
        setup_act, setup_dve = sem("setup_by_scalar"), sem("setup_by_vector")

        class Counts:

            def __init__(self, eng):
                self.eng = eng
                self.met = Count(meet_s, 5)
                self.full = [Count(s) for s in full_s]
                self.free = [Count(s) for s in free_s]
                for f in self.free:
                    f.n = 1
                self.a_loaded = Count(a_loaded, 16)
                self.a_hi = [Count(s) for s in a_hi_s]
                self.a_lo = [Count(s) for s in a_lo_s]
                self.a_used = [Count(s) for s in a_used_s]
                self.b_loaded, self.b_hi, self.b_lo, self.b_used = (
                    Count(b_loaded, 16), Count(b_hi_s), Count(b_lo_s), Count(b_used_s))
                self.sq, self.sq_used, self.rms, self.rstd = Count(sq_done), Count(sq_used), Count(rms_done), Count(rstd_done)
                self.hf, self.hh, self.hl = Count(hf_done), Count(hh_done), Count(hl_done)
                self.summed = Count(x_summed)
                self.x_loaded, self.y_loaded = Count(x_loaded, 16), Count(y_loaded, 16)
                self.stage = [Count(s) for s in stage_full]
                self.stage_stored = [Count(s, 16) for s in stage_stored]
                self.y_stored = Count(y_stored, 16)
                self.q, self.p, self.pt, self.p_max, self.p_exp = Count(q_done), Count(p_done), Count(pt_done), Count(p_max), Count(p_exp)
                self.kv = [Count(s, 16) for s in kv_loaded]
                self.av, self.g_hi, self.g_lo, self.gate = Count(av_done), Count(g_hi_done), Count(g_lo_done), Count(gate_done)
                self.kvs = [Count(s, 16) for s in kvs_loaded]
                self.kvs_used = [Count(s) for s in kvs_used]
                self.up = Count(up_done)
                self.slab_a = 0

            def meet(self):
                self.eng.drain().then_inc(meet_s, 1)
                self.eng.wait_ge(meet_s, self.met.next())

        def load_a(eng, c, slot, src):
            c.a_lo[slot].next()
            if c.slab_a:
                other = c.a_lo[1 - slot]
                eng.wait_ge(other.sem, other.value())
            c.slab_a += 1
            eng.dma_start(a_raw[:], src).then_inc(a_loaded, 16)

        def split_hi_a(eng, c, slot):
            eng.wait_ge(a_loaded, c.a_loaded.next())
            c.a_used[slot].next()
            eng.wait_ge(a_used_s[slot], c.a_used[slot].value(1))
            eng.activation(a_hi[slot][:], a_raw[:], ACT.Copy).then_inc(a_hi_s[slot], 1)

        def split_lo_a(eng, c, slot):
            eng.wait_ge(a_hi_s[slot], c.a_hi[slot].next())
            eng.tensor_tensor(a_lo[slot][:], a_raw[:], a_hi[slot][:].bitcast(F32),
                              ALU.subtract).then_inc(a_lo_s[slot], 1)

        def load_b(eng, c, src):
            c.b_lo.next()
            eng.wait_ge(b_lo_s, c.b_lo.value(1))
            eng.dma_start(b_raw[:], src).then_inc(b_loaded, 16)

        def split_hi_b(eng, c):
            eng.wait_ge(b_loaded, c.b_loaded.next())
            c.b_used.next()
            eng.wait_ge(b_used_s, c.b_used.value(1))
            eng.activation(b_hi[:], b_raw[:], ACT.Copy).then_inc(b_hi_s, 1)

        def split_lo_b(eng, c):
            eng.wait_ge(b_hi_s, c.b_hi.next())
            eng.tensor_tensor(b_lo[:], b_raw[:], b_hi[:].bitcast(F32), ALU.subtract).then_inc(b_lo_s, 1)

        def three(eng, out, whi, wlo, rhi, rlo, first, last):
            eng.matmul(out, whi, rhi, start=first, stop=False)
            eng.matmul(out, wlo, rhi, start=False, stop=False)
            return eng.matmul(out, whi, rlo, start=False, stop=last)

        def bank_for(eng, c, b):
            c.free[b].next()
            eng.wait_ge(free_s[b], c.free[b].value(1))

        def bank_in(eng, c, b):
            eng.wait_ge(full_s[b], c.full[b].next())

        def pe_columns(eng, c, slot, grp):
            eng.wait_ge(a_lo_s[slot], c.a_lo[slot].next())
            hi = a_hi[slot][:].rearrange("p (k c) -> p k c", k=KD)
            lo = a_lo[slot][:].rearrange("p (k c) -> p k c", k=KD)
            for g, (c0, n) in enumerate(grp):
                for mt in range(2):
                    b = 2 * g + mt
                    bank_for(eng, c, b)
                    for k in range(KD):
                        w = slice(mt * P, mt * P + P)
                        last = three(eng, banks[:, b, 0:n], hi[:, k, w], lo[:, k, w], hh[:, k, c0:c0 + n],
                                     hl[:, k, c0:c0 + n], k == 0, k == KD - 1)
                    if g == len(grp) - 1 and mt == 1:
                        eng.drain().then_inc(a_used_s[slot], 1)
                    last.then_inc(full_s[b], 1)

        def pe_tokens(eng, c, slot, tiles):
            eng.wait_ge(a_lo_s[slot], c.a_lo[slot].next())
            hi = a_hi[slot][:].rearrange("p (k c) -> p k c", k=KD)
            lo = a_lo[slot][:].rearrange("p (k c) -> p k c", k=KD)
            for i in range(tiles):
                b = i % 4
                bank_for(eng, c, b)
                w = slice(i * P, i * P + P)
                for k in range(KD):
                    last = three(eng, banks[:, b, 0:256], hh[:, k, w], hl[:, k, w], hi[:, k, :], lo[:, k, :],
                                 k == 0, k == KD - 1)
                if i == tiles - 1:
                    eng.drain().then_inc(a_used_s[slot], 1)
                last.then_inc(full_s[b], 1)

        def pe_rows(eng, c, grp):
            eng.wait_ge(b_lo_s, c.b_lo.next())
            hi = b_hi[:].rearrange("p (k d) -> p k d", k=2)
            lo = b_lo[:].rearrange("p (k d) -> p k d", k=2)
            for g, (c0, n) in enumerate(grp):
                eng.wait_ge(g_hi_done, c.g_hi.next())
                eng.wait_ge(g_lo_done, c.g_lo.next())
                for d in range(KD):
                    b = 4 + d % 4
                    bank_for(eng, c, b)
                    for k in range(2):
                        w = slice(d * P, d * P + P)
                        last = three(eng, banks[:, b, 0:n], hi[:, k, w], lo[:, k, w], g_hi[:, k, c0:c0 + n],
                                     g_lo[:, k, c0:c0 + n], k == 0, k == 1)
                    if g == len(grp) - 1 and d == KD - 1:
                        eng.drain().then_inc(b_used_s, 1)
                    last.then_inc(full_s[b], 1)

        def pe_norm(eng, c, grp):
            for g, (c0, n) in enumerate(grp):
                bank_for(eng, c, 4)
                for k in range(KD):
                    eng.wait_ge(sq_done, c.sq.next())
                    last = eng.matmul(banks[:, 4, 0:n], ones[:], sq[:, k % 2, 0:n], start=k == 0, stop=k == KD - 1)
                    if k < KD - 1:
                        last.then_inc(sq_used, 1)
                last.then_inc(full_s[4], 1)

        def pe_small(eng, c, tiles):
            for i in range(tiles):
                b = i % 4
                bank_for(eng, c, b)
                w = slice(i * P, i * P + P)
                for k in range(KD):
                    last = three(eng, banks[:, b, 0:N_SMALL], hh[:, k, w], hl[:, k, w], ws_hi[:, k, :],
                                 ws_lo[:, k, :], k == 0, k == KD - 1)
                last.then_inc(full_s[b], 1)

        def prompt_tiles(p):
            return min(PASSES[p][1], TILES - 1) - PASSES[p][0]

        def pe_attend(eng, c, p, slot, grp):
            q, pt = stage[0], stage[1]
            nt = prompt_tiles(p)
            c.kv[slot].n += 1
            eng.wait_ge(kv_loaded[slot], c.kv[slot].next())
            eng.wait_ge(ident_loaded, 16 * (p + 1))
            eng.wait_ge(q_done, c.q.next())

            def scores(i):
                b = 4 + i % 2
                bank_for(eng, c, b)
                for e in range(2):
                    last = eng.matmul(banks[:, b, 0:MEM], q[:, e, i * P:i * P + P], kv[:, slot, 0, e * MEM:(e + 1) * MEM],
                                      start=e == 0, stop=e == 1)
                last.then_inc(full_s[b], 1)

            def turn(i):
                b = 6 + i % 2
                eng.wait_ge(p_done, c.p.next())
                bank_for(eng, c, b)
                for mt in range(2):
                    last = eng.transpose(banks[:, b, mt * P:mt * P + P], pr[:, i % 2, mt * P:mt * P + P], ident[:])
                last.then_inc(full_s[b], 1)

            for i in range(nt + 1):
                if i < nt:
                    scores(i)
                if i > 0:
                    turn(i - 1)
            sample = p == len(PASSES) - 1
            if sample:
                s0 = nt * P
                for s in range(SEQS):
                    b = 4 + s // 2
                    if s % 2 == 0:
                        bank_for(eng, c, b)
                    eng.wait_ge(kvs_loaded[s % 2], c.kvs[s % 2].next())
                    for e in range(2):
                        last = eng.matmul(banks[0:SEQ_LEN, b, s % 2 * MEM:s % 2 * MEM + MEM],
                                          q[:, e, s0 + s * SEQ_LEN:s0 + (s + 1) * SEQ_LEN],
                                          kvs[:, s % 2, e * MEM:(e + 1) * MEM], start=e == 0, stop=e == 1)
                    eng.drain().then_inc(kvs_used[s % 2], 1)
                    if s % 2:
                        last.then_inc(full_s[b], 1)
                eng.wait_ge(p_done, c.p.next())
                bank_for(eng, c, 4)
                for s in range(SEQS):
                    for mt in range(2):
                        j = (s * 2 + mt) * SEQ_LEN
                        last = eng.transpose(banks[:, 4, j:j + SEQ_LEN], prs[0:SEQ_LEN, s, mt * P:mt * P + P],
                                             ident[0:SEQ_LEN, 0:SEQ_LEN])
                last.then_inc(full_s[4], 1)
            eng.wait_ge(pt_done, c.pt.next())
            for g, (c0, n) in enumerate(grp):
                n1 = min(n, nt * P - c0)
                for e in range(2):
                    b = 2 * g + e
                    bank_for(eng, c, b)
                    for mt in range(2):
                        last = eng.matmul(banks[:, b, 0:n1], kv[:, slot, 1, mt * MEM + e * P:mt * MEM + e * P + P],
                                          pt[:, mt, c0:c0 + n1], start=mt == 0, stop=mt == 1)
                    if n1 == n:
                        last.then_inc(full_s[b], 1)
            if sample:
                for s in range(SEQS):
                    eng.wait_ge(kvs_loaded[s % 2], c.kvs[s % 2].next())
                    for e in range(2):
                        j = n1 + s * SEQ_LEN
                        for mt in range(2):
                            last = eng.matmul(banks[:, 2 + e, j:j + SEQ_LEN],
                                              kvs[:, s % 2, mt * MEM + e * P:mt * MEM + e * P + P],
                                              prs_t[:, s, mt, :], start=mt == 0, stop=mt == 1)
                        if s == SEQS - 1:
                            last.then_inc(full_s[2 + e], 1)
                    eng.drain().then_inc(kvs_used[s % 2], 1)
            eng.drain().then_inc(av_done, 1)

        def pe_stage_kv(eng, c):
            grp = ((0, MEM),)
            pe_norm(eng, c, grp)
            pe_h(eng, c, grp)
            for n in range(4):
                pe_columns(eng, c, n % 2, grp)
            for n in range(4):
                pe_tokens(eng, c, n % 2, 2)

        def pe_h(eng, c, grp):
            c.hl.n += KD * len(grp)
            eng.wait_ge(hl_done, c.hl.value())

        def pe_stage_a(eng, c, p):
            grp, nt = groups(p), PASSES[p][1] - PASSES[p][0]
            pe_norm(eng, c, grp)
            pe_h(eng, c, grp)
            with Loop(eng, 4, [(x, 2) for x in c.free[0:4]] + [(x, 1) for x in c.a_lo]):
                for s in range(2):
                    pe_columns(eng, c, s, grp)
            pe_columns(eng, c, 0, grp)
            pe_tokens(eng, c, 1, nt)
            pe_tokens(eng, c, 0, nt)
            eng.wait_ge(ws_lo_done, p + 1)
            pe_small(eng, c, nt)

        def pe_stage_b(eng, c, p):
            grp = groups(p)
            pe_h(eng, c, grp)
            with Loop(eng, 2, [(x, 2) for x in c.free[0:4]] + [(x, 1) for x in c.a_lo]):
                for s in range(2):
                    pe_columns(eng, c, s, grp)
            pe_norm(eng, c, grp)
            pe_h(eng, c, grp)
            for h in range(HEADS):
                pe_columns(eng, c, h % 2, grp)
                pe_attend(eng, c, p, h % 2, grp)
                pe_rows(eng, c, grp)
            pe_norm(eng, c, grp)
            pe_h(eng, c, grp)
            pe_columns(eng, c, 0, grp)
            pe_columns(eng, c, 1, grp)
            with Loop(eng, ROUNDS - 1, [(x, 2) for x in c.free[0:4]] + [(x, 4) for x in c.free[4:8]]
                      + [(x, 1) for x in c.a_lo] + [(c.b_lo, 1), (c.g_hi, 2), (c.g_lo, 2)]):
                pe_columns(eng, c, 0, grp)
                pe_rows(eng, c, grp)
                pe_columns(eng, c, 1, grp)
            pe_rows(eng, c, grp)
            pe_norm(eng, c, grp)

        def act_norm(eng, c, grp, need, final=False):
            for g, (c0, n) in enumerate(grp):
                for k in range(KD):
                    if need:
                        eng.wait_ge(x_summed, need[g][k])
                    if k >= 2:
                        eng.wait_ge(sq_used, c.sq_used.next())
                    eng.activation(sq[:, k % 2, 0:n], x[:, k, c0:c0 + n], ACT.Square).then_inc(sq_done, 1)
                c.sq_used.n += 1
                bank_in(eng, c, 4)
                if g:
                    eng.wait_ge(rstd_done, c.rstd.value())
                c.rstd.n += 1
                eng.activation(rms[:, 0:n], banks[:, 4, 0:n], ACT.Sqrt, bias=eps[:], scale=1.0 / D).then_inc(rms_done, 1)
                eng.drain().then_inc(free_s[4], 1)
                if final:
                    continue
                for k in range(KD):
                    eng.wait_ge(hf_done, c.hf.next())
                    eng.activation(hh[:, k, c0:c0 + n], hf[:, k % 2, 0:n], ACT.Copy).then_inc(hh_done, 1)

        def skip(counts, which):
            for b in which:
                counts[b].n += 1

        def banks_of_columns(grp):
            return [2 * g + mt for g in range(len(grp)) for mt in range(2)]

        def banks_of_rows(grp):
            return [4 + d % 4 for _ in grp for d in range(KD)]

        def sums_by_rows(c, grp, sets):
            c.summed.n += sets * KD * len(grp)
            base = c.summed.n - KD * len(grp)
            return [[base + g * KD + k + 1 for k in range(KD)] for g in range(len(grp))]

        def sums_by_columns(c, grp):
            c.summed.n += 4 * 2 * len(grp)
            base = c.summed.n - 2 * len(grp)
            return [[base + 2 * g + 2] * KD for g in range(len(grp))]

        def act_out_columns(eng, c, slot, grp):
            eng.wait_ge(stage_stored[slot], c.stage_stored[slot].value())
            c.stage_stored[slot].n += 1
            for g, (c0, n) in enumerate(grp):
                for mt in range(2):
                    b = 2 * g + mt
                    bank_in(eng, c, b)
                    eng.activation(stage[slot][:, mt, c0:c0 + n], banks[:, b, 0:n], ACT.Copy).then_inc(free_s[b], 1)
            eng.drain().then_inc(stage_full[slot], 1)

        def act_out_tokens(eng, c, slot, tiles):
            out = stage[slot][:].rearrange("p a b -> p (a b)")
            eng.wait_ge(stage_stored[slot], c.stage_stored[slot].value())
            c.stage_stored[slot].n += 1
            for i in range(tiles):
                bank_in(eng, c, i % 4)
                eng.activation(out[:, i * 256:i * 256 + 256], banks[:, i % 4, 0:256], ACT.Copy).then_inc(free_s[i % 4], 1)
            eng.drain().then_inc(stage_full[slot], 1)

        def act_stage_kv(eng, c):
            grp = ((0, MEM),)
            for s in range(2):
                split_hi_a(eng, c, s)
            eng.wait_ge(x_loaded, c.x_loaded.next())
            act_norm(eng, c, grp, None)
            for n in range(8):
                if n < 4:
                    act_out_columns(eng, c, n % 2, grp)
                else:
                    act_out_tokens(eng, c, n % 2, 2)
                if n + 2 < 8:
                    split_hi_a(eng, c, n % 2)

        def act_stage_a(eng, c, p):
            grp, nt = groups(p), PASSES[p][1] - PASSES[p][0]
            for s in range(2):
                split_hi_a(eng, c, s)
            eng.wait_ge(x_loaded, c.x_loaded.next())
            act_norm(eng, c, grp, None)
            eng.wait_ge(ws_loaded, 16 * (p + 1))
            eng.activation(ws_hi[:].rearrange("p k c -> p (k c)"), ws[:], ACT.Copy).then_inc(ws_hi_done, 1)
            with Loop(eng, 4, [(x, 2) for x in c.full[0:4]] + [(x, 1) for x in c.a_used]
                      + [(c.a_loaded, 2)] + [(x, 1) for x in c.stage_stored]):
                for s in range(2):
                    act_out_columns(eng, c, s, grp)
                    split_hi_a(eng, c, s)
            act_out_columns(eng, c, 0, grp)
            split_hi_a(eng, c, 0)
            act_out_tokens(eng, c, 1, nt)
            act_out_tokens(eng, c, 0, nt)
            skip(c.full, [i % 4 for i in range(nt)])

        def act_attend(eng, c, p, slot, grp):
            q, pt = stage[0], stage[1]
            nt = prompt_tiles(p)
            sample = p == len(PASSES) - 1

            def weights(i):
                eng.wait_ge(p_max, c.p_max.next())
                eng.activation(pr[:, i % 2, :], banks[:, 4 + i % 2, 0:MEM], ACT.Exp, bias=soft[:, i % 2, 1:2],
                               accum_out=soft[:, i % 2, 2:3])
                eng.drain().then_inc(free_s[4 + i % 2], 1)
                eng.drain().then_inc(p_exp, 1)

            def turned(i):
                bank_in(eng, c, 6 + i % 2)
                out = pt[:, :, i * P:i * P + P]
                eng.activation(out, banks[:, 6 + i % 2, 0:MEM].rearrange("p (a b) -> p a b", a=2),
                               ACT.Copy).then_inc(free_s[6 + i % 2], 1)

            for i in range(nt + 1):
                if i < nt:
                    weights(i)
                if i > 0:
                    turned(i - 1)
            skip(c.full, [4 + i % 2 for i in range(nt)])
            if sample:
                skip(c.full, [4, 5, 6, 7])
                eng.wait_ge(p_max, c.p_max.next())
                eng.activation(prs[0:SEQ_LEN], prs[0:SEQ_LEN], ACT.Exp).then_inc(p_exp, 1)
                bank_in(eng, c, 4)
                eng.activation(prs_t[:].rearrange("p a b c -> p (a b c)"), banks[:, 4, 0:SEQS * 2 * SEQ_LEN],
                               ACT.Copy).then_inc(free_s[4], 1)
            eng.drain().then_inc(pt_done, 1)

        def act_stage_b(eng, c, p):
            grp = groups(p)
            for s in range(2):
                split_hi_a(eng, c, s)
            eng.wait_ge(y_loaded, c.y_loaded.next())
            c.x_loaded.n += 1
            for g, (c0, n) in enumerate(grp):
                for k in range(KD):
                    eng.activation(hh[:, k, c0:c0 + n], x[:, k, c0:c0 + n], ACT.Copy).then_inc(hh_done, 1)
            skip(c.full, banks_of_columns(grp) * 4)
            for n in range(4):
                split_hi_a(eng, c, n % 2)
            split_hi_b(eng, c)
            act_norm(eng, c, grp, sums_by_columns(c, grp))
            q = stage[0]
            for h in range(HEADS):
                for g, (c0, n) in enumerate(grp):
                    for mt in range(2):
                        b = 2 * g + mt
                        bank_in(eng, c, b)
                        eng.activation(q[:, mt, c0:c0 + n], banks[:, b, 0:n], ACT.Copy,
                                       scale=HD ** -0.5).then_inc(free_s[b], 1)
                eng.drain().then_inc(q_done, 1)
                split_hi_a(eng, c, h % 2)
                act_attend(eng, c, p, h % 2, grp)
                for g, (c0, n) in enumerate(grp):
                    for e in range(2):
                        b = 2 * g + e
                        bank_in(eng, c, b)
                        eng.activation(g_hi[:, e, c0:c0 + n], banks[:, b, 0:n], ACT.Copy)
                    eng.drain().then_inc(g_hi_done, 1)
                skip(c.full, banks_of_rows(grp))
                split_hi_b(eng, c)
            act_norm(eng, c, grp, sums_by_rows(c, grp, HEADS))

            def gate():
                for g, (c0, n) in enumerate(grp):
                    for mt in range(2):
                        b = 2 * g + mt
                        bank_in(eng, c, b)
                        if g == 0 and mt == 0:
                            eng.wait_ge(g_lo_done, c.g_lo.value())
                        eng.activation(stage[0][:, mt, c0:c0 + n], banks[:, b, 0:n], ACT.Silu).then_inc(free_s[b], 1)
                    eng.drain().then_inc(gate_done, 1)
                skip(c.full, banks_of_columns(grp))

            def up():
                for g, (c0, n) in enumerate(grp):
                    eng.wait_ge(up_done, c.up.next())
                    eng.activation(g_hi[:, :, c0:c0 + n], stage[0][:, :, c0:c0 + n], ACT.Copy).then_inc(g_hi_done, 1)

            c.g_lo.n += HEADS * len(grp)
            gate()
            split_hi_a(eng, c, 0)
            up()
            split_hi_a(eng, c, 1)
            c.g_lo.n += len(grp)
            with Loop(eng, ROUNDS - 2, [(x, 2) for x in c.full[0:4]] + [(x, 1) for x in c.a_used]
                      + [(c.a_loaded, 2), (c.b_loaded, 1), (c.b_used, 1), (c.g_lo, 2), (c.up, 2)]):
                gate()
                split_hi_a(eng, c, 0)
                split_hi_b(eng, c)
                up()
                split_hi_a(eng, c, 1)
                c.g_lo.n += len(grp)
            gate()
            split_hi_b(eng, c)
            up()
            c.g_lo.n += len(grp)
            skip(c.full, banks_of_rows(grp) * ROUNDS)
            act_norm(eng, c, grp, sums_by_rows(c, grp, ROUNDS), final=True)

        def dve_norm(eng, c, grp, gain, final=False):
            for g, (c0, n) in enumerate(grp):
                eng.wait_ge(rms_done, c.rms.next())
                eng.drain()
                eng.reciprocal(rstd[:, 0:n], rms[:, 0:n]).then_inc(rstd_done, 1)
                eng.drain()
                for k in range(KD):
                    if final:
                        eng.scalar_tensor_tensor(x[:, k, c0:c0 + n], x[:, k, c0:c0 + n], pcol(gain, k), rstd[:, 0:n],
                                                 ALU.mult, ALU.mult)
                        continue
                    if k >= 2 or g:
                        eng.wait_ge(hh_done, c.hh.value() + g * KD + k - 1)
                        eng.wait_ge(hl_done, c.hl.value() + g * KD + k - 1)
                    eng.scalar_tensor_tensor(hf[:, k % 2, 0:n], x[:, k, c0:c0 + n], pcol(gain, k), rstd[:, 0:n],
                                             ALU.mult, ALU.mult).then_inc(hf_done, 1)
            if not final:
                c.hh.n += KD * len(grp)
                c.hl.n += KD * len(grp)
            skip(c.full, [4] * len(grp))

        def dve_add_columns(eng, c, n0, grp):
            for g, (c0, n) in enumerate(grp):
                for mt in range(2):
                    b = 2 * g + mt
                    bank_in(eng, c, b)
                    dst = x[:, n0 + mt, c0:c0 + n]
                    eng.tensor_tensor(dst, dst, banks[:, b, 0:n], ALU.add).then_inc(free_s[b], 1)
                    eng.drain().then_inc(x_summed, 1)

        def dve_add_rows(eng, c, grp):
            for g, (c0, n) in enumerate(grp):
                for d in range(KD):
                    b = 4 + d % 4
                    bank_in(eng, c, b)
                    dst = x[:, d, c0:c0 + n]
                    eng.tensor_tensor(dst, dst, banks[:, b, 0:n], ALU.add).then_inc(free_s[b], 1)
                    eng.drain().then_inc(x_summed, 1)

        def dve_stage_kv(eng, c):
            grp = ((0, MEM),)
            dve_norm(eng, c, grp, "g_mem")
            skip(c.full, [0, 1] * 8)

        def dve_stage_a(eng, c, p):
            grp, nt = groups(p), PASSES[p][1] - PASSES[p][0]
            dve_norm(eng, c, grp, "g_mix")
            eng.wait_ge(ws_hi_done, p + 1)
            eng.tensor_tensor(ws_lo[:].rearrange("p k c -> p (k c)"), ws[:],
                              ws_hi[:].rearrange("p k c -> p (k c)").bitcast(F32), ALU.subtract).then_inc(ws_lo_done, 1)
            skip(c.full, banks_of_columns(grp) * 9 + [i % 4 for i in range(nt)] * 2)
            for i in range(nt):
                bank_in(eng, c, i % 4)
                eng.tensor_copy(raw12[:, i, :], banks[:, i % 4, 0:N_SMALL]).then_inc(free_s[i % 4], 1)

        def dve_attend(eng, c, p, grp):
            nt = prompt_tiles(p)

            def row_max(i):
                bank_in(eng, c, 4 + i % 2)
                eng.tensor_reduce(soft[:, i % 2, 0:1], banks[:, 4 + i % 2, 0:MEM], AX_X, ALU.max)
                eng.drain()
                eng.tensor_scalar(soft[:, i % 2, 1:2], soft[:, i % 2, 0:1], -1.0, None, ALU.mult).then_inc(p_max, 1)

            def normalise(i):
                eng.wait_ge(p_exp, c.p_exp.next())
                eng.reciprocal(soft[:, i % 2, 3:4], soft[:, i % 2, 2:3])
                eng.drain()
                eng.tensor_scalar(pr[:, i % 2, :], pr[:, i % 2, :], soft[:, i % 2, 3:4], None, ALU.mult)
                eng.drain().then_inc(p_done, 1)

            for i in range(nt + 1):
                if i < nt:
                    row_max(i)
                if i > 0:
                    normalise(i - 1)
            skip(c.full, [6 + i % 2 for i in range(nt)])
            if p == len(PASSES) - 1:
                for b in range(4, 8):
                    bank_in(eng, c, b)
                s = banks[0:SEQ_LEN, 4:8, :].rearrange("p b (s m) -> p (b s) m", s=2)
                w = prs[0:SEQ_LEN]
                top, total, inv = (softs[0:SEQ_LEN, j, :] for j in range(3))
                eng.tensor_reduce(top, s, AX_X, ALU.max)
                eng.drain()
                eng.tensor_tensor(w, s, top.unsqueeze(2).to_broadcast([SEQ_LEN, SEQS, MEM]), ALU.subtract)
                for b in range(4, 8):
                    eng.drain().then_inc(free_s[b], 1)
                eng.drain().then_inc(p_max, 1)
                eng.wait_ge(p_exp, c.p_exp.next())
                eng.tensor_reduce(total, w, AX_X, ALU.add)
                eng.drain()
                eng.reciprocal(inv, total)
                eng.drain()
                eng.tensor_tensor(w, w, inv.unsqueeze(2).to_broadcast([SEQ_LEN, SEQS, MEM]), ALU.mult)
                eng.drain().then_inc(p_done, 1)
                skip(c.full, [4])

        def dve_stage_b(eng, c, p):
            grp = groups(p)
            for g, (c0, n) in enumerate(grp):
                for k in range(KD):
                    eng.wait_ge(hh_done, c.hh.next())
                    eng.tensor_tensor(hl[:, k, c0:c0 + n], x[:, k, c0:c0 + n], hh[:, k, c0:c0 + n].bitcast(F32),
                                      ALU.subtract).then_inc(hl_done, 1)
            c.hl.n += KD * len(grp)
            eng.wait_ge(x_loaded, 16 * (3 + 2 * p))
            for n in range(4):
                dve_add_columns(eng, c, 2 * n, grp)
            dve_norm(eng, c, grp, "g_cross")
            for h in range(HEADS):
                skip(c.full, banks_of_columns(grp))
                dve_attend(eng, c, p, grp)
                for g, (c0, n) in enumerate(grp):
                    eng.wait_ge(g_hi_done, c.g_hi.next())
                    for e in range(2):
                        b = 2 * g + e
                        bank_in(eng, c, b)
                        eng.tensor_tensor(g_lo[:, e, c0:c0 + n], banks[:, b, 0:n], g_hi[:, e, c0:c0 + n].bitcast(F32),
                                          ALU.subtract).then_inc(free_s[b], 1)
                    eng.drain().then_inc(g_lo_done, 1)
                dve_add_rows(eng, c, grp)
            dve_norm(eng, c, grp, "g_ffn")

            def times_up():
                skip(c.full, banks_of_columns(grp))
                for g, (c0, n) in enumerate(grp):
                    eng.wait_ge(gate_done, c.gate.next())
                    for mt in range(2):
                        b = 2 * g + mt
                        bank_in(eng, c, b)
                        dst = stage[0][:, mt, c0:c0 + n]
                        eng.tensor_tensor(dst, dst, banks[:, b, 0:n], ALU.mult).then_inc(free_s[b], 1)
                    eng.drain().then_inc(up_done, 1)

            times_up()
            with Loop(eng, ROUNDS - 1, [(x, 2) for x in c.full[0:4]] + [(x, 4) for x in c.full[4:8]] + [(c.gate, 2)]):
                dve_add_rows(eng, c, grp)
                times_up()
            dve_add_rows(eng, c, grp)
            c.g_hi.n += 2 * ROUNDS
            dve_norm(eng, c, grp, "g_final", final=True)
            eng.drain().then_inc(out_ready, 1)

        def pool_norm(eng, c, grp):
            for g, (c0, n) in enumerate(grp):
                for k in range(KD):
                    eng.wait_ge(hh_done, c.hh.next())
                    eng.tensor_tensor(hl[:, k, c0:c0 + n], hf[:, k % 2, 0:n], hh[:, k, c0:c0 + n].bitcast(F32),
                                      ALU.subtract).then_inc(hl_done, 1)

        def pool_stage_kv(eng, c):
            for s in range(2):
                split_lo_a(eng, c, s)
            pool_norm(eng, c, ((0, MEM),))
            for n in range(6):
                split_lo_a(eng, c, n % 2)

        def pool_stage_a(eng, c, p):
            for s in range(2):
                split_lo_a(eng, c, s)
            pool_norm(eng, c, groups(p))
            with Loop(eng, 4, [(x, 1) for x in c.a_hi]):
                for s in range(2):
                    split_lo_a(eng, c, s)
            split_lo_a(eng, c, 0)

        def pool_stage_b(eng, c, p):
            grp = groups(p)
            for s in range(2):
                split_lo_a(eng, c, s)
            c.hh.n += KD * len(grp)
            for n in range(4):
                split_lo_a(eng, c, n % 2)
            split_lo_b(eng, c)
            pool_norm(eng, c, grp)
            for h in range(HEADS):
                split_lo_a(eng, c, h % 2)
                split_lo_b(eng, c)
            pool_norm(eng, c, grp)
            c.g_hi.n += HEADS * len(grp)

            def up():
                for g, (c0, n) in enumerate(grp):
                    eng.wait_ge(g_hi_done, c.g_hi.next())
                    eng.tensor_tensor(g_lo[:, :, c0:c0 + n], stage[0][:, :, c0:c0 + n],
                                      g_hi[:, :, c0:c0 + n].bitcast(F32), ALU.subtract).then_inc(g_lo_done, 1)

            split_lo_a(eng, c, 0)
            up()
            split_lo_a(eng, c, 1)
            with Loop(eng, ROUNDS - 2, [(x, 1) for x in c.a_hi] + [(c.b_hi, 1), (c.g_hi, 2)]):
                split_lo_a(eng, c, 0)
                split_lo_b(eng, c)
                up()
                split_lo_a(eng, c, 1)
            split_lo_b(eng, c)
            up()

        def sp_stage_kv(eng, c):
            eng.dma_start(x[:, :, 0:MEM], t["mem_t"]).then_inc(x_loaded, 16)

            def store(n):
                slot = n % 2
                eng.wait_ge(stage_full[slot], c.stage[slot].next())
                c.stage_stored[slot].n += 1
                if n < 4:
                    dst = t["p_mem_kt"].rearrange("(t p) m -> p t m", p=P)[:, 2 * n:2 * n + 2, :]
                    eng.dma_start(dst, stage[slot][:, :, 0:MEM]).then_inc(stage_stored[slot], 16)
                else:
                    j = (n - 4) * 256
                    dst = t["p_mem_v"].rearrange("(t p) e -> p t e", p=P)[:, :, j:j + 256]
                    src = stage[slot][:].rearrange("p a b -> p (a b)")[:, 0:512].rearrange("p (t e) -> p t e", t=2)
                    eng.dma_start(dst, src).then_inc(stage_stored[slot], 16)

            for n in range(8):
                load_a(eng, c, n % 2, t["w_kv"][n])
                if n >= 3:
                    store(n - 3)
            for n in range(5, 8):
                store(n)
            for s in range(2):
                eng.wait_ge(stage_stored[s], c.stage_stored[s].value())

        def sp_stage_a(eng, c, p):
            t0, nt = PASSES[p][0] * P, PASSES[p][1] - PASSES[p][0]
            n = nt * P
            eng.dma_start(x[:, :, 0:n], t["x_t"][:, :, t0:t0 + n]).then_inc(x_loaded, 16)
            load_a(eng, c, 0, t["w_in"][0])
            eng.dma_start(ws[:], t["w_small"]).then_inc(ws_loaded, 16)
            load_a(eng, c, 1, t["w_in"][1])

            def store(i, slot, tokens=None):
                eng.wait_ge(stage_full[slot], c.stage[slot].next())
                c.stage_stored[slot].n += 1
                if tokens is None:
                    dst = u_dram[:, bass.ds(i * 2, 2), 3 + t0:3 + t0 + n]
                    src = stage[slot][:, :, 0:n]
                else:
                    dst = z_dram[t0:t0 + n, tokens * 256:tokens * 256 + 256].rearrange("(t p) c -> p t c", p=P)
                    src = stage[slot][:].rearrange("p a b -> p (a b)")[:, 0:nt * 256].rearrange("p (t c) -> p t c", t=nt)
                eng.dma_start(dst, src).then_inc(stage_stored[slot], 16)

            load_a(eng, c, 0, t["w_in"][2])
            with Loop(eng, 4, [(x, 1) for x in c.a_lo + c.stage + c.stage_stored]) as i:
                for s in range(2):
                    store(i * 2 + s, s)
                    load_a(eng, c, 1 - s, t["w_in"][bass.ds(i * 2 + (s + 3), 1)].rearrange("a p n -> p (a n)"))
            store(8, 0)
            store(None, 1, tokens=0)
            store(None, 0, tokens=1)
            for s in range(2):
                eng.wait_ge(stage_stored[s], c.stage_stored[s].value())

        def sp_stage_b(eng, c, p):
            t0, nt = PASSES[p][0] * P, PASSES[p][1] - PASSES[p][0]
            n = nt * P
            sample = p == len(PASSES) - 1
            eng.wait_ge(ms["y_out"], 1 + 16 * PASSES[p][1])
            eng.dma_start(x[:, :, 0:n], y_dram[:, :, t0:t0 + n]).then_inc(y_loaded, 16)
            load_a(eng, c, 0, t["w_a"][0])
            eng.dma_start(ident[:], t["mixc"][:, MIX["ident"][0]:MIX["ident"][0] + P]).then_inc(ident_loaded, 16)
            load_a(eng, c, 1, t["w_a"][1])
            c.hl.n = KD + (2 * KD) * (p + 1) + 3 * (2 * KD) * p + 2 * KD
            c.hh.n = c.hl.n
            eng.wait_ge(hl_done, c.hl.value())
            eng.wait_ge(hh_done, c.hh.value())
            eng.dma_start(x[:, :, 0:n], t["x_t"][:, :, t0:t0 + n]).then_inc(x_loaded, 16)

            def load_kv(h):
                slot = h % 2
                if h >= 2:
                    eng.wait_ge(av_done, HEADS * p + h - 1)
                k = t["p_mem_kt"].rearrange("(h e p) m -> h p e m", h=HEADS, p=P)[h]
                v = t["p_mem_v"].rearrange("(t p) (h e) -> h p t e", p=P, h=HEADS)[h]
                eng.dma_start(kv[:, slot, 0, :].rearrange("p (e m) -> p e m", e=2), k).then_inc(kv_loaded[slot], 16)
                eng.dma_start(kv[:, slot, 1, :].rearrange("p (t e) -> p t e", t=2), v).then_inc(kv_loaded[slot], 16)

            for s in (2, 3, 4, 5):
                load_a(eng, c, s % 2, t["w_a"][s])
            for h in range(HEADS):
                load_kv(h)
                load_b(eng, c, t["w_b"][h])
                load_a(eng, c, h % 2, t["w_a"][6 + h])
                if sample:
                    for name in ("k_cache_t", "v_cache"):
                        for s in range(SEQS):
                            c.kvs_used[s % 2].next()
                            eng.wait_ge(kvs_used[s % 2], c.kvs_used[s % 2].value(1))
                            eng.dma_start(kvs[:, s % 2, :], t[name][h, s]).then_inc(kvs_loaded[s % 2], 16)
            load_b(eng, c, t["w_b"][4])
            with Loop(eng, ROUNDS - 1, [(x, 1) for x in c.a_lo] + [(c.b_lo, 1)]) as i:
                for s in range(2):
                    load_a(eng, c, s, t["w_a"][bass.ds(i * 2 + (10 + s), 1)].rearrange("a p n -> p (a n)"))
                load_b(eng, c, t["w_b"][bass.ds(i + 5, 1)].rearrange("a p n -> p (a n)"))
            eng.wait_ge(out_ready, p + 1)
            eng.dma_start(t["y_t"][:, :, t0:t0 + n], x[:, :, 0:n]).then_inc(out_stored, 16)
            eng.wait_ge(out_stored, 16 * (p + 1))

        per_chunk = dict(
            u_in=1, z_in=1, turned=3, turned_sb=4, kq=1, kq_dec=2, share=2, share_sb=2, tap0=3, conv=3, sz=1,
            bu=2, bu_sb=2, cs=2,
            lg=1, dec_g=1, dec_s=1, dec_x=2, dec_m=2, score=1,
            gates=1, th=1, n2=1, nr=1, scaled=1, ch=2, cht=2, ml=7, cur=1,
            rot_p=1, sc=1, ssdy=1, yo=1, xw=1, ssdst=1, xsd=1, la=1, lm=1, lsq=1, gg=1,
            xs5=1, s5yb=1, s5ys=1, gys=1, glu=1, glut=1, uw=1, uw_sb=1, ws_b=1, delta=1, ob=1, gst=1,
            rot_z=1, rot_q=1, y3=1, ss=1, rs=1, gz=1, gsq=1, grs=1, ytm=2, ytr=2, ych=2, y_out=1, s5done=1,
            lruy=1, osum=1, sel=8, stp=8, x0=6, x1=6, y0=6, y1=6, t0=6, t1=6, sx0=6, sx1=6, ss0=7, ss1=7, st0=6, st1=6)
        ms = {k: sem("m_" + k) for k in per_chunk}
        prep_in, tok_pe, tok_act, tok_dve = sem("prep_in"), sem("tok_pe"), sem("tok_act"), sem("tok_dve")
        sample_in = sem("sample_in")
        SAMPLE_LOADS = U_TILES + 5
        SAMPLE_ONLY = ("sel", "stp", "share", "share_sb", "osum")
        finals_stored = sem("finals_stored")

        def v3(ap, a):
            return ap.rearrange("p (a b) -> p a b", a=a)

        def mc(name, j=0, w=None):
            o, n = MIX[name]
            return mixc[:, o + j:o + j + (n if w is None else w)]

        class Chunk:

            def __init__(self, eng, base, i, sample):
                self.eng, self.base, self.i, self.sample = eng, base, i, sample
                self.seqs, self.len = (SEQS, SEQ_LEN) if sample else (1, P)

            def need(self, name, k=1):
                if self.sample and name == "u_in":
                    self.eng.wait_ge(sample_in, 16 * SAMPLE_LOADS)
                    return
                n, unit = per_chunk[name], 16 if name in ("u_in", "z_in", "y_out") else 1
                v = (k if name in SAMPLE_ONLY else self.base * n + k) * unit
                if name == "y_out":
                    v += 1
                self.eng.wait_ge(ms[name], v if self.i is None else self.i * (n * unit) + v)

            def window(self, tile, j=3):
                w = self.len + 3
                return u_buf[:, tile, 0:self.seqs * w].rearrange("p (s w) -> p s w", w=w)[:, :, j:j + self.len]

            def by_seq(self, ap):
                return v3(ap, self.seqs)

        u_buf = m["u"][:].rearrange("p (t w) -> p t w", t=U_TILES)
        cv = v3(m["cv"][:], N_CONV)
        cur = m["cur"]
        dec, lg = v3(m["dec"][:], 8), v3(m["lg"][:], 8)
        chT = v3(m["chT"][:], 8)
        bre, bim, p1, p2, p3, p4 = (m[k] for k in ("bre", "bim", "p1", "p2", "p3", "p4"))
        ych = v3(m["ych"][:], 8)
        levels_of = lambda sample: 3 if sample else 6
        GROUPS = ((8, 14), (2, 8), (0, 2))

        def heads(ap, n=4):
            return v3(ap, n)

        def per_head(ap, n, w=64):
            return ap.unsqueeze(2).to_broadcast([P, n, w])

        def pe_tokens_scalars(eng, c, p):
            npr = prompt_tiles(p)
            eng.wait_ge(tok_dve, 2 * p + 2)
            g = m["tmp8"][:, 0:npr * 8]
            eng.matmul(banks[:, 0, 0:npr * 8], mc("U"), g, start=True, stop=True)
            eng.matmul(banks[:, 0, 64:64 + npr * 8], mc("L"), g, start=True, stop=True)
            last = eng.matmul(banks[:, 0, 128:128 + npr * 8], mc("ones"), g, start=True, stop=True)
            if p == len(PASSES) - 1:
                g = m["tmp8"][:, npr * 8:npr * 8 + 8]
                eng.matmul(banks[:, 1, 0:8], mc("Us"), g, start=True, stop=True)
                eng.matmul(banks[:, 1, 8:16], mc("Ls"), g, start=True, stop=True)
                last = eng.matmul(banks[:, 1, 64:128], mc("ones"), m["tmp8"][:, 64:128], start=True, stop=True)
            last.then_inc(tok_pe, 1)

        def pe_chunk(eng, k):
            s_ = k.sample

            k.need("u_in")
            for part in range(2):
                for s in range(8):
                    b = 3 + 2 * part + s // 4
                    last = eng.matmul(k.by_seq(banks[:, b, s % 4 * P:s % 4 * P + P]), mprep[:, part, s, :],
                                      k.window(DU + s // 4), start=True, stop=True)
                last.then_inc(ms["bu"], 1)

            def turn(bank, col, tiles):
                for j, src in enumerate(tiles):
                    last = eng.transpose(banks[:, bank, col + j * P:col + j * P + P], src, mc("ident"))
                return last

            k.need("cs", 1)
            turn(1, 0, [cv[:, j, :] for j in (8, 9, 10, 11)]).then_inc(ms["turned"], 1)
            turn(2, 0, [cv[:, j, :] for j in (12, 13)]).then_inc(ms["turned"], 1)
            k.need("cs", 2)
            turn(0, 0, [cv[:, j, :] for j in (2, 3, 4, 5)]).then_inc(ms["turned"], 1)
            k.need("lg")
            k.need("bu_sb", 2)
            for h in range(8):
                b = 3 if h < 4 else 4
                last = eng.matmul(banks[:, b, h % 4 * P:h % 4 * P + P], lg[:, h, :], mc("Us" if s_ else "U"),
                                  start=True, stop=True)
                if h % 4 == 3:
                    last.then_inc(ms["dec_s" if h < 4 else "dec_g"], 1)
            k.need("turned_sb", 3)
            for g in range(2):
                last = eng.matmul(banks[:, 2, 256 + g * P:256 + g * P + P], cv[:, 4 + g, :], cv[:, 6 + g, :],
                                  start=True, stop=True)
            last.then_inc(ms["score"], 1)
            k.need("conv", 3)
            for w, name in enumerate(("w_r", "w_i")):
                for j in range(2):
                    last = eng.matmul(banks[:, 7, (2 * w + j) * P:(2 * w + j + 1) * P], mc(name, j * P, P), cv[:, j, :],
                                      start=True, stop=True)
            last.then_inc(ms["gates"], 1)
            k.need("scaled")
            k.need("turned_sb", 4)
            qkn = m["qkn"]
            turn(0, 0, [qkn[:, j * P:j * P + P] for j in range(4)]).then_inc(ms["ch"], 1)
            turn(1, 0, [m["kb"][:, 0:P], m["kb"][:, P:256], m["qd"][:, 0:P], m["qd"][:, P:256]]).then_inc(ms["ch"], 1)
            k.need("cht", 2)
            for o, right in ((0, 4), (2, 0)):
                for h in range(4):
                    r = slice(h % 2 * 64, h % 2 * 64 + 64)
                    j = (o + h // 2) * P
                    eng.matmul(banks[:, 5 + h % 2, j:j + P], chT[r, 2 + h // 2, :], chT[r, right + h // 2, :],
                               start=True, stop=True)
            eng.drain().then_inc(ms["kq"], 1)
            k.need("sc")
            k.need("th")
            for h in range(4):
                last = eng.matmul(banks[:, 7, h * 64:h * 64 + 64], m["sc"][:, h * P:h * P + P],
                                  m["xdt"][:, h * 64:h * 64 + 64], start=True, stop=True)
            if s_:
                for g in range(2):
                    for s in range(SEQS):
                        cols = slice(s * SEQ_LEN, (s + 1) * SEQ_LEN)
                        last = eng.matmul(banks[:, 7, 256 + g * P + s * SEQ_LEN:256 + g * P + (s + 1) * SEQ_LEN],
                                          ssd_hs[:, s, g * P:g * P + P], cv[:, 6 + g, cols], start=True, stop=True)
            else:
                for g in range(2):
                    last = eng.matmul(banks[:, 7, 256 + g * P:256 + g * P + P], cv[:, 6 + g, :],
                                      ssd_h[:, g * P:g * P + P], start=True, stop=True)
            last.then_inc(ms["ssdy"], 1)
            k.need("cht", 2)
            top = levels_of(s_)
            for lv in range(top):
                for pr_ in range(2):
                    bx, by = (0, 1) if pr_ == 0 else (2, 3)
                    if lv == 0:
                        if pr_ == 1:
                            k.need("sc")
                            k.need("turned_sb", 3)
                    k.need(f"ss{pr_}", lv + 1)
                    for h in range(2):
                        o = (2 * pr_ + h) * P
                        last = eng.transpose(banks[:, bx, 256 + h * P:256 + h * P + P], m["S"][:, o:o + P], mc("ident"))
                    last.then_inc(ms[f"t{pr_}"], 1)
                for pr_ in range(2):
                    bx, by = (0, 1) if pr_ == 0 else (2, 3)
                    k.need(f"st{pr_}", lv + 1)
                    k.need("ml", lv + 2)
                    for h in range(2):
                        o = (2 * pr_ + h) * P
                        last = eng.matmul(banks[:, bx, h * P:h * P + P],
                                          m["ML"][:, (lv + 1) * 512 + o:(lv + 1) * 512 + o + P],
                                          m["T"][:, o:o + P], start=True, stop=True)
                    last.then_inc(ms[f"x{pr_}"], 1)
                for pr_ in range(2):
                    bx, by = (0, 1) if pr_ == 0 else (2, 3)
                    k.need(f"sx{pr_}", lv + 1)
                    if lv == 0 and pr_ == 1:
                        k.need("dec_x", 2)
                    for h in range(2):
                        o = (2 * pr_ + h) * P
                        last = eng.matmul(banks[:, by, h * P:h * P + P], m["X"][:, o:o + P], m["S"][:, o:o + P],
                                          start=True, stop=True)
                    last.then_inc(ms[f"y{pr_}"], 1)
            k.need("kq_dec", 2)
            k.need("xw")
            if not s_:
                for g in range(2):
                    last = eng.matmul(banks[:, 6, g * P:g * P + P], m["tok_x"][:, 256 + g * P:256 + g * P + P],
                                      m["xw"][:, g * P:g * P + P], start=True, stop=True)
                last.then_inc(ms["ssdst"], 1)
            else:
                k.need("share_sb", 1)
                turn(6, 0, [m["yo"][:, 0:P], m["yo"][:, P:256]]).then_inc(ms["share"], 1)
            k.need("xs5")
            k.need("dec_x", 2)
            for j in range(2):
                for n in range(8):
                    s, part = 4 * j + n // 2, n % 2
                    src = (p1, p3)[part]
                    last = eng.matmul(banks[:, 4, j * P:j * P + P], mc(("ct_re", "ct_im")[part], s * P, P),
                                      src[:, s * P:s * P + P], start=n == 0, stop=n == 7)
            last.then_inc(ms["s5yb"], 1)
            k.need("kq_dec", 1)
            k.need("ss0", top + 1)
            k.need("ss1", top + 1)
            for h in range(4):
                S = m["S"][:, h * P:h * P + P]
                eng.matmul(banks[:, 5, h * 64:h * 64 + 64], S, m["vb"][:, h * 64:h * 64 + 64], start=True, stop=True)
            for h in range(4):
                r = slice(h % 2 * 64, h % 2 * 64 + 64)
                last = eng.matmul(banks[r, 5, 256 + h // 2 * P:256 + h // 2 * P + P], m["wk"][:, h * 64:h * 64 + 64],
                                  m["S"][:, h * P:h * P + P], start=True, stop=True)
            last.then_inc(ms["uw"], 1)
            wT, delta = m["wT"], m["delta"]
            k.need("uw_sb")
            if s_:
                pe_gdn_sample(eng, k)
                return
            for j in range(2):
                last = eng.matmul(banks[:, 3, 256 + j * P:256 + j * P + P], wT[:, j * P:j * P + P], gdn_s[:, j, :],
                                  start=True, stop=True)
            last.then_inc(ms["ws_b"], 1)
            k.need("delta")
            for j in range(2):
                eng.matmul(banks[:, 6, 256 + j * P:256 + j * P + P], chT[:, 6 + j, :], gdn_s[:, j, :],
                           start=True, stop=False, skip_group_check=True)
                for h in (2 * j, 2 * j + 1):
                    last = eng.matmul(banks[:, 6, 256 + h * 64:256 + h * 64 + 64], m["qkd"][:, h * P:h * P + P],
                                      delta[:, h * 64:h * 64 + 64], start=False, stop=h == 2 * j + 1, skip_group_check=True)
            last.then_inc(ms["ob"], 1)
            k.need("yo")
            k.need("y3")
            for j in range(2):
                last = eng.matmul(banks[:, 7, j * P:j * P + P], m["kd"][:, j * P:j * P + P], delta[:, j * P:j * P + P],
                                  start=True, stop=True)
            last.then_inc(ms["gst"], 1)
            pe_glu(eng, k)
            pe_chunk_end(eng, k)

        def pe_gdn_sample(eng, k):
            for j in range(2):
                for s in range(SEQS):
                    cols = slice(j * P + s * SEQ_LEN, j * P + (s + 1) * SEQ_LEN)
                    out = slice(256 + cols.start, 256 + cols.stop)
                    eng.matmul(banks[:, 3, out], gdn_ss[:, s, j, :], m["wT"][:, cols], start=True, stop=True)
                    last = eng.matmul(banks[:, 6, out], gdn_ss[:, s, j, :],
                                      chT[:, 6 + j, s * SEQ_LEN:(s + 1) * SEQ_LEN], start=True, stop=True)
            last.then_inc(ms["share"], 1)
            k.need("share_sb", 2)
            for j in range(4):
                last = eng.transpose(banks[:, 0, j * P:j * P + P], m["X"][:, j * P:j * P + P], mc("ident"))
            last.then_inc(ms["ws_b"], 1)
            k.need("delta")
            for h in range(4):
                last = eng.matmul(banks[:, 6, 256 + h * 64:256 + h * 64 + 64], m["qkd"][:, h * P:h * P + P],
                                  m["delta"][:, h * 64:h * 64 + 64], start=True, stop=True)
            last.then_inc(ms["ob"], 1)
            pe_glu(eng, k)
            k.need("yo")
            k.need("y3")
            for s in range(SEQS):
                k.need("sel", s + 1)
                for j in range(2):
                    eng.matmul(banks[:, 7, j * P:j * P + P], m["kb"][:, j * P:j * P + P],
                               m["delta"][:, j * P:j * P + P], start=True, stop=True)
                for g in range(2):
                    last = eng.matmul(banks[:, 7, 256 + g * P:256 + g * P + P],
                                      m["tok_x"][:, 256 + g * P:256 + g * P + P], m["qd"][:, g * P:g * P + P],
                                      start=True, stop=True)
                last.then_inc(ms["stp"], 1)
            pe_chunk_end(eng, k)

        def pe_glu(eng, k):
            k.need("gys")
            for d in range(2):
                for j in range(2):
                    last = eng.matmul(banks[:, 4, 256 + d * P:256 + d * P + P], mc("glu", j * 256 + d * P, P),
                                      m["s5t"][:, j * P:j * P + P], start=j == 0, stop=j == 1)
            last.then_inc(ms["glu"], 1)

        def pe_chunk_end(eng, k):
            for n in range(2):
                k.need("ytm", n + 1)
                for j in range(2):
                    last = eng.transpose(banks[:, n, j * P:j * P + P], m["ytm"][:, (2 * n + j) * P:(2 * n + j + 1) * P],
                                         mc("ident"))
                last.then_inc(ms["ytr"], 1)

        def pe_stage_m(eng, c, p):
            eng.wait_ge(prep_in, 32 * (p + 1))
            pe_tokens_scalars(eng, c, p)
            chunks(eng, c, p, pe_chunk)

        def chunks(eng, c, p, body):
            first, n = PASSES[p][0], prompt_tiles(p)
            eng.wait_ge(prep_in, 32 * (p + 1))
            with Loop(eng, n, [(c.met, 1)]) as i:
                c.meet()
                body(eng, Chunk(eng, first, i, False))
            if p == len(PASSES) - 1:
                c.meet()
                body(eng, Chunk(eng, TILES - 1, None, True))
                c.meet()

        def act_chunk(eng, k):
            s_ = k.sample
            top = levels_of(s_)
            k.need("u_in")
            for grp in GROUPS:
                for j in range(*grp):
                    w = pcol("conv_w", j)
                    last = eng.activation(k.by_seq(cv[:, j, :]), k.window(CONV + j, 0), ACT.Identity,
                                          bias=pcol("conv_b", j), scale=w)
                last.then_inc(ms["tap0"], 1)
            for part, dst in enumerate((bre, bim)):
                k.need("bu", part + 1)
                src = banks[:, 3 + 2 * part:5 + 2 * part, :].rearrange("p b c -> p (b c)")
                eng.activation(dst[:], src, ACT.Copy).then_inc(ms["bu_sb"], 1)
            k.need("conv", 1)
            eng.activation(cv[:, 8:14, :], cv[:, 8:14, :], ACT.Silu).then_inc(ms["cs"], 1)
            k.need("z_in")
            eng.activation(m["sz"][:], m["z"][:], ACT.Silu).then_inc(ms["sz"], 1)
            k.need("conv", 2)
            eng.activation(cv[:, 2:8, :], cv[:, 2:8, :], ACT.Silu).then_inc(ms["cs"], 1)
            k.need("turned", 1)
            eng.activation(m["tok_qk"][:], banks[:, 1, :], ACT.Copy).then_inc(ms["turned_sb"], 1)
            eng.activation(m["sqk"][:], banks[:, 1, :], ACT.Square).then_inc(ms["turned_sb"], 1)
            k.need("turned", 2)
            eng.activation(m["tok_v"][:], banks[:, 2, 0:256], ACT.Copy).then_inc(ms["turned_sb"], 1)
            k.need("turned", 3)
            eng.activation(m["tok_x"][:], banks[:, 0, :], ACT.Copy).then_inc(ms["turned_sb"], 1)
            k.need("gates")
            for j in range(4):
                eng.activation(m["th"][:, j * P:j * P + P], banks[:, 7, j * P:j * P + P], ACT.Tanh,
                               bias=half_b[:, j:j + 1], scale=0.5)
            eng.drain().then_inc(ms["th"], 1)
            k.need("n2")
            eng.activation(m["n8"][:, 0:8], m["n8"][:, 0:8], ACT.Sqrt, bias=eps[:]).then_inc(ms["nr"], 1)
            for b, name, o in ((4, "dec_g", 4), (3, "dec_s", 0)):
                k.need(name)
                eng.activation(dec[:, o:o + 4, :].rearrange("p h t -> p (h t)"), banks[:, b, :],
                               ACT.Exp).then_inc(ms["dec_x"], 1)
            for j in range(2):
                th = m["th"][:, j * P:j * P + P]
                for dst, o, f in ((m["la"], 0, ACT.Exp), (m["lt"], 2, ACT.Tanh)):
                    eng.activation(dst[:, j * P:j * P + P], th, f, bias=lru_c[:, o + j:o + j + 1],
                                   scale=lru_c[:, o + j:o + j + 1])
            eng.drain().then_inc(ms["la"], 1)
            for b in range(2):
                k.need("ch", b + 1)
                eng.activation(chT[:, 4 * b:4 * b + 4, :].rearrange("p a t -> p (a t)"), banks[:, b, :],
                               ACT.Copy).then_inc(ms["cht"], 1)

            def yo():
                if s_:
                    k.need("share", 1)
                else:
                    k.need("ssdy")
                b, o = (6, 0) if s_ else (7, 256)
                for h in range(4):
                    eng.activation(m["yo"][:, h * 64:h * 64 + 64], banks[:, b, o + h * 64:o + h * 64 + 64], ACT.Copy,
                                   scale=cur[:, EGC + h:EGC + h + 1])
                eng.drain().then_inc(ms["yo"], 1)

            for lv in range(top):
                for pr_, b in ((0, 0), (1, 2)):
                    k.need(f"t{pr_}", lv + 1)
                    eng.activation(m["T"][:, pr_ * 256:pr_ * 256 + 256], banks[:, b, 256:512],
                                   ACT.Copy).then_inc(ms[f"st{pr_}"], 1)
                for pr_, b in ((0, 0), (1, 2)):
                    k.need(f"x{pr_}", lv + 1)
                    eng.activation(m["X"][:, pr_ * 256:pr_ * 256 + 256], banks[:, b, 0:256],
                                   ACT.Copy).then_inc(ms[f"sx{pr_}"], 1)
                if lv == 0:
                    if s_:
                        k.need("ssdy")
                        eng.activation(m["yo"][:], banks[:, 7, 256:512], ACT.Copy).then_inc(ms["share_sb"], 1)
                    else:
                        yo()
                if lv == 1:
                    k.need("lm")
                    eng.activation(m["lb"][:], m["lb"][:], ACT.Sqrt, scale=0.25).then_inc(ms["lsq"], 1)
            if s_:
                yo()
            k.need("y3")
            for g in range(2):
                eng.activation(m["sqk"][:, g * P:g * P + P], m["ys"][:, g * P:g * P + P], ACT.Square,
                               accum_out=m["n8"][:, g:g + 1])
            eng.drain()
            eng.activation(m["n8"][:, 0:2], m["n8"][:, 0:2], ACT.Sqrt, bias=eps[:], scale=1.0 / P).then_inc(ms["rs"], 1)
            k.need("uw")
            eng.activation(m["uu"][:], banks[:, 5, 0:256], ACT.Copy)
            eng.activation(m["wT"][:], banks[:, 5, 256:512], ACT.Copy)
            eng.drain().then_inc(ms["uw_sb"], 1)
            if s_:
                k.need("share", 2)
                eng.activation(m["X"][:, 0:256], banks[:, 3, 256:512], ACT.Copy)
                eng.activation(m["X"][:, 256:512], banks[:, 6, 256:512], ACT.Copy)
                eng.drain().then_inc(ms["share_sb"], 1)
            eng.activation(k.by_seq(m["gg"][:, 0:P]), k.window(GATE), ACT.Gelu_apprx_tanh)
            eng.activation(k.by_seq(m["gg"][:, P:256]), k.window(GATE + 1), ACT.Gelu_apprx_tanh)
            eng.drain().then_inc(ms["gg"], 1)
            k.need("s5ys")
            eng.activation(m["s5t"][:], m["s5y"][:], ACT.Gelu_apprx_tanh).then_inc(ms["gys"], 1)
            k.need("osum" if s_ else "ob")
            o = m["uu"][:] if s_ else banks[:, 6, 256:512]
            eng.activation(m["sqk"][:, 0:256], o, ACT.Square).then_inc(ms["gsq"], 1)
            k.need("glu")
            for d in range(2):
                eng.activation(m["sqk"][:, 256 + d * P:256 + d * P + P], banks[:, 4, 256 + d * P:256 + d * P + P],
                               ACT.Tanh, bias=half_b[:, 4 + d:5 + d], scale=0.5)
            eng.drain().then_inc(ms["glut"], 1)
            k.need("ss")
            eng.activation(m["n8"][:, 8:12], m["n8"][:, 8:12], ACT.Sqrt, bias=eps[:], scale=1.0 / 64).then_inc(ms["grs"], 1)
            k.need("y_out", 0)
            for n in range(2):
                k.need("ytr", n + 1)
                eng.activation(ych[:, 2 + 2 * n:4 + 2 * n, :], v3(banks[:, n, 0:256], 2), ACT.Copy).then_inc(ms["ych"], 1)

        def act_stage_m(eng, c, p):
            n, npr = PASSES[p][1] - PASSES[p][0], prompt_tiles(p)
            eng.wait_ge(tok_dve, 2 * p + 1)
            tk = m["tk"]
            eng.activation(tk[:, 2 * 64:2 * 64 + n * 8], tk[:, 64:64 + n * 8], ACT.Exp)
            eng.activation(v3(tk[:, 4 * 64:4 * 64 + n * 4], n), raw12[:, 0:n, 8:12], ACT.Tanh, scale=0.5)
            eng.drain().then_inc(tok_act, 1)
            eng.wait_ge(tok_pe, p + 1)
            for o, col in ((EGC, 0), (EGE, 64), (ETOT, 128)):
                eng.activation(tsc[:, 0:npr, o:o + 8], v3(banks[:, 0, col:col + npr * 8], npr), ACT.Exp)
            if npr < n:
                eng.activation(tsc[:, npr, EGC:EGC + 16], banks[:, 1, 0:16], ACT.Exp)
                eng.activation(m["etotb"][:], banks[:, 1, 64:128], ACT.Exp)
            chunks(eng, c, p, act_chunk)

        def dve_tokens_scalars(eng, p):
            n, npr = PASSES[p][1] - PASSES[p][0], prompt_tiles(p)
            w = n * 8
            tk = m["tk"]
            x8, na, e, sp, th, z, z2, acc = (tk[:, j * 64:j * 64 + w] for j in range(8))
            th = tk[:, 4 * 64:4 * 64 + n * 4]
            eng.tensor_tensor(v3(x8, n), raw12[:, 0:n, 0:8], pcol("bias8", 0, 8).unsqueeze(1).to_broadcast([P, n, 8]), ALU.add)
            eng.drain()
            eng.scalar_tensor_tensor(na, x8, -1.0, x8, ALU.mult, ALU.min)
            eng.drain().then_inc(tok_dve, 1)
            eng.wait_ge(tok_act, p + 1)
            eng.tensor_scalar(z, e, 2.0, None, ALU.add)
            eng.drain()
            eng.reciprocal(z, z)
            eng.drain()
            eng.tensor_tensor(z, z, e, ALU.mult)
            eng.drain()
            eng.tensor_tensor(z2, z, z, ALU.mult)
            artanh(eng, acc, z2)
            eng.drain()
            eng.tensor_tensor(acc, acc, z, ALU.mult)
            eng.drain()
            eng.tensor_scalar(acc, acc, 2.0, None, ALU.mult)
            eng.drain()
            eng.scalar_tensor_tensor(sp, x8, 0.0, acc, ALU.max, ALU.add)
            eng.drain()
            sp3 = v3(sp, n)
            eng.tensor_tensor(tsc[:, 0:n, G8:G8 + 8], sp3, nea8[:].unsqueeze(1).to_broadcast([P, n, 8]), ALU.mult)
            eng.tensor_tensor(v3(m["tmp8"][:, 0:w], n), sp3, nea8[:].unsqueeze(1).to_broadcast([P, n, 8]), ALU.mult)
            eng.tensor_copy(tsc[:, 0:n, DT:DT + 4], sp3[:, :, 0:4])
            eng.tensor_scalar(tsc[:, 0:n, BETA:BETA + 4], v3(th, n), 0.5, 0.5, ALU.mult, ALU.add)
            if npr < n:
                eng.drain()
                g = m["tmp8"][:, npr * 8:npr * 8 + 8]
                eng.tensor_tensor(v3(m["tmp8"][:, 64:128], SEQS), mc("seqsel").unsqueeze(2).to_broadcast([P, SEQS, 8]),
                                  g.unsqueeze(1).to_broadcast([P, SEQS, 8]), ALU.mult)
            eng.drain().then_inc(tok_dve, 1)

        def artanh(eng, acc, z2):
            eng.memset(acc, 1.0 / 17)
            for d in (15, 13, 11, 9, 7, 5, 3, 1):
                eng.drain()
                eng.tensor_tensor(acc, acc, z2, ALU.mult)
                eng.drain()
                eng.tensor_scalar(acc, acc, 1.0 / d, None, ALU.add)

        def v4(k, ap):
            return ap.rearrange("p (t s l) -> p t s l", t=8, s=k.seqs)

        def rotation(k, part):
            tab = mprep[:, 2 + part, :, 0:k.len]
            return tab.unsqueeze(2).to_broadcast([P, 8, k.seqs, k.len])

        def dve_chunk(eng, k):
            s_, top = k.sample, levels_of(k.sample)
            tt, stt = eng.tensor_tensor, eng.scalar_tensor_tensor
            s5_state = s5_xs if s_ else s5_x[:].unsqueeze(3)
            decay5, c5 = m["decay5"], m["c5"]
            tile_in_pass = TILES - 1 - PASSES[-1][0] if s_ else k.i
            eng.tensor_copy(cur[:], tsc[:, bass.ds(tile_in_pass, 1), :].rearrange("p a c -> p (a c)")).then_inc(ms["cur"], 1)
            k.need("u_in")

            def conv(n):
                k.need("tap0", n + 1)
                for tap in (1, 2, 3):
                    for j in range(*GROUPS[n]):
                        out = k.by_seq(cv[:, j, :])
                        last = stt(out, k.window(CONV + j, tap), pcol("conv_w", tap * N_CONV + j), out, ALU.mult, ALU.add)
                    if tap < 3:
                        eng.drain()
                last.then_inc(ms["conv"], 1)

            conv(0)
            conv(1)
            k.need("bu_sb", 2)
            tt(v4(k, p1[:]), v4(k, bre[:]), rotation(k, 0), ALU.mult)
            tt(v4(k, p3[:]), v4(k, bim[:]), rotation(k, 0), ALU.mult)
            for part in range(2):
                tt(v3(c5[:, part * 64:part * 64 + 8 * k.seqs], 8), s5_state[:, part],
                   mag[:].unsqueeze(2).to_broadcast([P, 8, k.seqs]), ALU.mult)
            conv(2)
            k.need("turned_sb", 2)
            eng.tensor_reduce(m["n8"][:, 0:8], v3(m["sqk"][:], 8), AX_X, ALU.add).then_inc(ms["n2"], 1)
            k.need("rot_p")
            tt(p1[:], p1[:], p2[:], ALU.add)
            tt(p3[:], p3[:], p4[:], ALU.subtract)
            if s_:
                eng.memset(v4(k, decay5[:])[:, :, :, 0:1], 0.0)
            eng.drain()
            for part, src in enumerate((p1, p3)):
                first = v4(k, src[:])[:, :, :, 0]
                tt(first, first, v3(c5[:, part * 64:part * 64 + 8 * k.seqs], 8), ALU.add)
            k.need("nr")
            eng.reciprocal(m["n8"][:, 0:8], m["n8"][:, 0:8])
            eng.drain()
            eng.tensor_scalar(m["n8"][:, 0:4], m["n8"][:, 0:4], 0.125, None, ALU.mult)
            eng.drain()
            k.need("turned_sb", 1)
            k.need("turned_sb", 3)
            qkn = m["qkn"]
            tt(v3(qkn[:], 8), v3(m["tok_qk"][:], 8), per_head(m["n8"][:, 0:8], 8), ALU.mult)
            beta, egc = cur[:, BETA:BETA + 4], cur[:, EGC + 4:EGC + 8]
            tt(heads(m["vb"][:]), heads(m["tok_v"][:]), per_head(beta, 4), ALU.mult)
            eng.drain()
            tt(heads(m["kb"][:]), heads(qkn[:, 256:512]), per_head(beta, 4), ALU.mult)
            tt(heads(m["qd"][:]), heads(qkn[:, 0:256]), per_head(egc, 4), ALU.mult)
            eng.drain().then_inc(ms["scaled"], 1)
            tt(heads(m["kd"][:]), heads(qkn[:, 256:512]), per_head(cur[:, EGE + 4:EGE + 8], 4), ALU.mult)
            tt(heads(m["wk"][:]), heads(m["kb"][:]), per_head(egc, 4), ALU.mult)
            k.need("turned_sb", 4)
            tt(heads(m["xdt"][:]), heads(m["tok_x"][:, 0:256]), per_head(cur[:, DT:DT + 4], 4), ALU.mult)
            k.need("dec_m", 2)
            k.need("score")
            for g in range(2):
                tt(v3(m["sc"][:, g * 256:g * 256 + 256], 2), dec[:, 2 * g:2 * g + 2, :],
                   banks[:, 2, 256 + g * P:256 + g * P + P].unsqueeze(1).to_broadcast([P, 2, P]), ALU.mult)
            eng.drain().then_inc(ms["sc"], 1)
            k.need("kq")

            def by_pair(ap):
                return ap.rearrange("p (j h t) -> p j h t", j=2, h=2)

            kq = banks[:, 5:7, :].rearrange("p h (w j t) -> p w j h t", w=2, j=2)
            tt(by_pair(m["MT"][:]), kq[:, 0], by_pair(m["decs"][:]), ALU.mult).then_inc(ms["kq_dec"], 1)
            tt(by_pair(m["qkd"][:]), kq[:, 1], dec[:, 4:8, :].rearrange("p (j h) t -> p j h t", j=2),
               ALU.mult).then_inc(ms["kq_dec"], 1)
            k.need("ml", 1)
            for pr_ in range(2):
                o = slice(pr_ * 256, pr_ * 256 + 256)
                tt(v3(m["S"][:, o], 2), mc("ident").unsqueeze(1).to_broadcast([P, 2, P]), v3(m["ML"][:, o], 2),
                   ALU.subtract).then_inc(ms[f"ss{pr_}"], 1)
            tt(heads(m["xw"][:]), heads(m["xdt"][:]), per_head(cur[:, EGE:EGE + 4], 4), ALU.mult).then_inc(ms["xw"], 1)
            k.need("la")
            tt(m["lb"][:], m["la"][:], m["la"][:], ALU.mult)
            eng.drain()
            stt(m["lb"][:], m["lb"][:], 1.0, m["lt"][:], ALU.add, ALU.mult).then_inc(ms["lm"], 1)

            def ssd_y():
                k.need("ssdy")
                k.need("yo")
                k.need("xsd")
                k.need("sz")
                ys = m["ys"][:]
                tt(ys, banks[:, 7, 0:256], m["yo"][:], ALU.add)
                eng.drain()
                tt(ys, ys, m["xsd"][:], ALU.add)
                eng.drain()
                tt(ys, ys, m["sz"][:, 0:256], ALU.mult).then_inc(ms["y3"], 1)

            for lv in range(top):
                if lv == 0:
                    for part, src, dst in ((0, p1, bre), (1, p3, bim)):
                        eng.tensor_tensor_scan(dst[:], decay5[:], src[:], 0.0, ALU.mult, ALU.add)
                    eng.drain().then_inc(ms["rot_z"], 1)
                if lv == 1:
                    stt(m["lt"][:], m["th"][:, 256:512], 1.0, cv[:, 0:2, :].rearrange("p a t -> p (a t)"), ALU.add, ALU.mult)
                    tt(v4(k, p1[:]), v4(k, bre[:]), rotation(k, 0), ALU.mult)
                    tt(v4(k, p3[:]), v4(k, bim[:]), rotation(k, 0), ALU.mult)
                if lv == 2:
                    eng.drain()
                    k.need("lsq")
                    tt(m["lt"][:], m["lt"][:], m["lb"][:], ALU.mult)
                    eng.drain()
                    for j in range(2):
                        for s in range(k.seqs):
                            w = slice(j * P + s * k.len, j * P + (s + 1) * k.len)
                            first = lru_hs[:, j, s:s + 1] if s_ else lru_h[:, j:j + 1]
                            eng.tensor_tensor_scan(m["hs"][:, w], m["la"][:, w], m["lt"][:, w], first, ALU.mult, ALU.add)
                    eng.drain()
                    dst = lru_hs if s_ else lru_h[:].unsqueeze(2)
                    eng.tensor_copy(dst, m["hs"][:].rearrange("p (t s l) -> p t s l", t=2, s=k.seqs)[:, :, :, k.len - 1])
                if lv == 3:
                    ssd_y()
                for pr_, b in ((0, 1), (1, 3)):
                    k.need(f"y{pr_}", lv + 1)
                    o = slice(pr_ * 256, pr_ * 256 + 256)
                    tt(m["S"][:, o], m["S"][:, o], banks[:, b, 0:256], ALU.subtract).then_inc(ms[f"ss{pr_}"], 1)
            k.need("rot_q")
            tt(p1[:], p1[:], p2[:], ALU.subtract)
            tt(p3[:], p3[:], p4[:], ALU.add)
            eng.drain().then_inc(ms["xs5"], 1)
            for part, src in enumerate((p1, p3)):
                eng.tensor_copy(s5_state[:, part], v4(k, src[:])[:, :, :, k.len - 1])
            if s_:
                ssd_y()
            if not s_:
                k.need("ssdst")
                for h in range(4):
                    o = slice(h * 64, h * 64 + 64)
                    stt(ssd_h[:, o], ssd_h[:, o], cur[:, ETOT + h:ETOT + h + 1], banks[:, 6, o], ALU.mult, ALU.add)
            k.need("s5yb")
            for j in range(2):
                stt(k.by_seq(m["s5y"][:, j * P:j * P + P]), k.window(DU + j), pcol("s5_d", j),
                    k.by_seq(banks[:, 4, j * P:j * P + P]), ALU.mult, ALU.add)
            eng.drain().then_inc(ms["s5ys"], 1)
            k.need("uw_sb")
            k.need("ws_b")
            uu = m["uu"]
            if s_:
                tt(m["delta"][:], uu[:], banks[:, 0, 0:256], ALU.subtract)
                eng.drain()
                eng.tensor_copy(uu[:], banks[:, 0, 256:512])
                eng.drain().then_inc(ms["delta"], 1)
            else:
                tt(m["delta"][:], uu[:], banks[:, 3, 256:512], ALU.subtract).then_inc(ms["delta"], 1)
            k.need("rs")
            eng.reciprocal(m["n8"][:, 0:2], m["n8"][:, 0:2])
            eng.drain()
            for g in range(2):
                o = slice(g * P, g * P + P)
                stt(m["ytm"][:, o], m["ys"][:, o], m["n8"][:, g:g + 1], mc("ssd_norm", g * P, P), ALU.mult, ALU.mult)
            eng.drain().then_inc(ms["ytm"], 1)
            k.need("gg")
            k.need("y_out", 0)
            tt(ych[:, 0:2, :].rearrange("p a t -> p (a t)"), m["hs"][:], m["gg"][:], ALU.mult).then_inc(ms["lruy"], 1)
            k.need("ob")
            if s_:
                tt(uu[:], uu[:], banks[:, 6, 256:512], ALU.add).then_inc(ms["osum"], 1)
            k.need("gsq")
            eng.tensor_reduce(m["n8"][:, 8:12], heads(m["sqk"][:, 0:256]), AX_X, ALU.add).then_inc(ms["ss"], 1)

            def gdn_state(j, state, total):
                for half in range(2):
                    r = slice(half * 64, half * 64 + 64)
                    h = 2 * j + half
                    stt(state[r, j, r], state[r, j, r], total[r, 4 + h:5 + h],
                        banks[r, 7, j * P + half * 64:j * P + half * 64 + 64], ALU.mult, ALU.add)

            if not s_:
                k.need("gst")
                for j in range(2):
                    gdn_state(j, gdn_s, cur[:, ETOT:ETOT + 8])
            s5_gate(eng, k)
            k.need("grs")
            eng.reciprocal(m["n8"][:, 8:12], m["n8"][:, 8:12])
            eng.drain()
            o = uu[:] if s_ else banks[:, 6, 256:512]
            tt(heads(m["yo"][:]), heads(o), per_head(m["n8"][:, 8:12], 4), ALU.mult)
            eng.drain()
            k.need("gz")
            tt(m["ytm"][:, 256:512], m["yo"][:], m["gz"][:], ALU.mult).then_inc(ms["ytm"], 1)
            if s_:
                for s in range(SEQS):
                    if s:
                        k.need("stp", s)
                    sel = mc("seqsel", s, 1)
                    eng.tensor_scalar(m["kb"][:], m["kd"][:], sel, None, ALU.mult)
                    eng.tensor_scalar(m["qd"][:], m["xw"][:], sel, None, ALU.mult)
                    eng.drain().then_inc(ms["sel"], 1)
                    k.need("stp", s + 1)
                    for j in range(2):
                        gdn_state(j, gdn_ss[:, s], etotb[:, s, :])
                    for h in range(4):
                        o = slice(h * 64, h * 64 + 64)
                        stt(ssd_hs[:, s, o], ssd_hs[:, s, o], etotb[:, s, h:h + 1],
                            banks[:, 7, 256 + h * 64:256 + h * 64 + 64], ALU.mult, ALU.add)
                    eng.drain()
                tails = u_buf[:, CONV:CONV + N_CONV, 0:SEQS * (SEQ_LEN + 3)].rearrange("p t (s w) -> p t s w", s=SEQS)
                eng.tensor_copy(m["tail"][:].rearrange("p (t s w) -> p t s w", t=N_CONV, s=SEQS), tails[:, :, :, SEQ_LEN:])

        def s5_gate(eng, k):
            k.need("glut")
            g = m["sqk"][:, 256:512]
            eng.tensor_scalar(g, g, 0.5, 0.5, ALU.mult, ALU.add)
            eng.drain()
            eng.tensor_tensor(ych[:, 6:8, :].rearrange("p a t -> p (a t)"), m["s5t"][:], g, ALU.mult).then_inc(ms["s5done"], 1)

        def dve_stage_m(eng, c, p):
            eng.wait_ge(prep_in, 32 * (p + 1))
            dve_tokens_scalars(eng, p)
            eng.tensor_scalar(mc("ct_im"), mc("ct_im"), -1.0, None, ALU.mult)
            eng.tensor_copy(v3(m["decay5"][:], 8), mag[:].unsqueeze(2).to_broadcast([P, 8, P]))
            eng.drain()
            eng.memset(v3(m["decay5"][:], 8)[:, :, 0:1], 0.0)
            chunks(eng, c, p, dve_chunk)

        def pool_chunk(eng, k):
            s_ = k.sample
            tt = eng.tensor_tensor
            k.need("cur")
            later = mc("Ls" if s_ else "L")
            tt(lg[:, 0, :], later, cur[:, G8:G8 + 1].to_broadcast([P, P]), ALU.mult)
            for h in range(1, 8):
                eng.tensor_scalar(lg[:, h, :], later, cur[:, G8 + h:G8 + h + 1], None, ALU.mult)
            eng.drain().then_inc(ms["lg"], 1)
            k.need("bu_sb", 2)
            tt(v4(k, p2[:]), v4(k, bim[:]), rotation(k, 1), ALU.mult)
            tt(v4(k, p4[:]), v4(k, bre[:]), rotation(k, 1), ALU.mult)
            eng.drain().then_inc(ms["rot_p"], 1)
            k.need("dec_x", 1)
            mask = mc("Us" if s_ else "U").unsqueeze(1).to_broadcast([P, 4, P])
            strict = mc("stricts" if s_ else "strict").unsqueeze(1).to_broadcast([P, 4, P])
            tt(dec[:, 4:8, :], dec[:, 4:8, :], mask, ALU.mult)
            eng.drain()
            tt(v3(m["decs"][:], 4), dec[:, 4:8, :], strict, ALU.mult)
            eng.drain().then_inc(ms["dec_m"], 1)
            k.need("dec_x", 2)
            tt(dec[:, 0:4, :], dec[:, 0:4, :], mask, ALU.mult).then_inc(ms["dec_m"], 1)
            k.need("kq_dec", 1)
            for b in range(levels_of(s_) + 1):
                lm = mc("levels", b * P, P).unsqueeze(1).to_broadcast([P, 4, P])
                tt(v3(m["ML"][:, b * 512:b * 512 + 512], 4), v3(m["MT"][:], 4), lm, ALU.mult).then_inc(ms["ml"], 1)
                if b == 2:
                    k.need("turned_sb", 4)
                    tt(m["xsd"][:], m["tok_x"][:, 0:256], mc("ssd_d"), ALU.mult).then_inc(ms["xsd"], 1)
            k.need("rot_z")
            tt(v4(k, p2[:]), v4(k, bim[:]), rotation(k, 1), ALU.mult)
            tt(v4(k, p4[:]), v4(k, bre[:]), rotation(k, 1), ALU.mult)
            eng.drain().then_inc(ms["rot_q"], 1)
            k.need("sz")
            tt(m["gz"][:], m["sz"][:, 256:512], mc("gdn_norm"), ALU.mult).then_inc(ms["gz"], 1)

        def pool_stage_m(eng, c, p):
            chunks(eng, c, p, pool_chunk)

        def sp_chunk(eng, k):
            if k.sample:
                t0 = PROMPT
                for tile in range(U_TILES):
                    eng.dma_start(k.window(tile), k.by_seq(u_dram[:, tile, 3 + t0:3 + t0 + P])).then_inc(sample_in, 16)
                halo = u_buf[:, CONV:CONV + N_CONV, 0:SEQS * (SEQ_LEN + 3)].rearrange("p t (s w) -> p (t s) w", s=SEQS)
                eng.dma_start(halo[:, :, 0:3], t["conv_caches"]).then_inc(sample_in, 16)
                for name in ("ssd_hs", "gdn_ss", "s5_xs", "lru_hs"):
                    eng.dma_start(m[name][:], t[name]).then_inc(sample_in, 16)
            else:
                t0 = k.i * P + k.base * P
                eng.dma_start(u_buf[:, :, 0:P + 3], u_dram[:, :, bass.ds(t0, P + 3)]).then_inc(ms["u_in"], 16)
            eng.dma_start(m["z"][:], z_dram[bass.ds(t0, P), :]).then_inc(ms["z_in"], 16)
            k.need("lruy")
            k.need("s5done")
            k.need("ych", 2)
            eng.dma_start(y_dram[:, :, bass.ds(t0, P)], ych).then_inc(ms["y_out"], 16)

        def sp_stage_m(eng, c, p):
            eng.dma_start(mixc[:], t["mixc"]).then_inc(prep_in, 16)
            eng.dma_start(mprep[:].rearrange("p a b c -> p (a b c)"), prep_dram).then_inc(prep_in, 16)
            chunks(eng, c, p, sp_chunk)
            if p == len(PASSES) - 1:
                outs = [("p_ssd", ssd_h[:]), ("p_gdn", gdn_s[:].rearrange("p a b -> p (a b)")),
                        ("p_s5", s5_x[:].rearrange("p a b -> p (a b)")), ("p_lru", lru_h[:]),
                        ("p_tail", u_dram[:, CONV:CONV + N_CONV, PROMPT:PROMPT + 3]),
                        ("s_tail", m["tail"][:]), ("s_ssd", m["ssd_hs"][:]), ("s_gdn", m["gdn_ss"][:]),
                        ("s_s5", m["s5_xs"][:]), ("s_lru", m["lru_hs"][:])]
                for name, src in outs:
                    eng.dma_start(t[name], src).then_inc(finals_stored, 16)
                eng.wait_ge(finals_stored, 16 * len(outs))

        are, aim, ldt = (s5p[:, j, :] for j in range(3))
        (w_step, w_mag, w_ang, w_k, w_r, w_sin, w_half, w_cos, w_den, w_fr, w_fi, w_t1, w_t2, w_t3) = (w[:] for w in sw)
        prep_flat = prep[:].rearrange("p a b c -> p (a b c)")

        def act_setup(eng):
            eng.wait_ge(par_loaded, 16 * 3)
            eng.activation(w_step, ldt, ACT.Exp)
            eng.activation(sm[:, 2:4], pcol("lam", 0, 2), ACT.Abs)
            eng.drain()
            eng.activation(sm[:, 4:6], sm[:, 2:4], ACT.Exp, scale=-1.0)
            eng.activation(nea8[:], pcol("alog8", 0, 8), ACT.Exp)
            eng.drain().then_inc(setup_act, 1)
            eng.wait_ge(setup_dve, 1)
            eng.activation(w_mag, w_t1, ACT.Exp)
            eng.drain().then_inc(setup_act, 1)
            eng.wait_ge(setup_dve, 2)
            eng.activation(w_sin, w_r, ACT.Sin)
            eng.activation(w_half, w_r, ACT.Sin, scale=0.5)
            eng.drain().then_inc(setup_act, 1)

        def exp_exact(eng, out, src):
            n, r, e = ex[:, 0], ex[:, 1], ex[:, 2]
            eng.tensor_scalar(n, src, float(1 / np.log(2)), ROUND_MAGIC, ALU.mult, ALU.add)
            eng.drain()
            eng.tensor_scalar(n, n, ROUND_MAGIC, -126.0, ALU.subtract, ALU.max)
            eng.drain()
            eng.tensor_scalar(n, n, 127.0, None, ALU.min)
            eng.drain()
            eng.scalar_tensor_tensor(r, n, -LN2_HI, src, ALU.mult, ALU.add)
            eng.drain()
            eng.scalar_tensor_tensor(r, n, -LN2_LO, r, ALU.mult, ALU.add)
            eng.memset(e, 1.0 / 9)
            for d in range(8, 0, -1):
                eng.drain()
                eng.tensor_tensor(e, e, r, ALU.mult)
                eng.drain()
                eng.tensor_scalar(e, e, 1.0, 1.0 / d, ALU.add, ALU.mult)
            eng.drain()
            eng.tensor_tensor(e, e, r, ALU.mult)
            eng.tensor_scalar(exi[:], n, 127.0, 8388608.0, ALU.add, ALU.mult)
            eng.drain()
            eng.tensor_scalar(e, e, 1.0, None, ALU.add)
            eng.drain()
            eng.tensor_tensor(out, e, exi[:].bitcast(F32), ALU.mult)

        def dve_setup(eng):
            tt, ts, stt = eng.tensor_tensor, eng.tensor_scalar, eng.scalar_tensor_tensor
            eng.memset(ones[:], 1.0)
            eng.memset(eps[:], EPS)
            eng.memset(ssd_h[:], 0.0)
            eng.memset(gdn_s[:], 0.0)
            eng.memset(s5_x[:], 0.0)
            eng.memset(lru_h[:], 0.0)
            eng.memset(zero3[:], 0.0)
            for s in free_s:
                eng.sem_inc(s, 1)
            eng.sem_inc(ms["y_out"], 1)
            eng.wait_ge(setup_act, 1)
            exp_exact(eng, w_step[:, 1024:W5], ldt[:, 1024:W5])
            eng.drain()
            tt(w_t1, are, w_step, ALU.mult).then_inc(setup_dve, 1)
            tt(w_ang, aim, w_step, ALU.mult)
            eng.drain()
            ts(w_k, w_ang, float(1 / (2 * np.pi)), ROUND_MAGIC, ALU.mult, ALU.add)
            eng.drain()
            ts(w_k, w_k, ROUND_MAGIC, None, ALU.subtract)
            eng.drain()
            stt(w_r, w_k, -TWO_PI_HI, w_ang, ALU.mult, ALU.add)
            eng.drain()
            stt(w_r, w_k, -TWO_PI_MID, w_r, ALU.mult, ALU.add)
            eng.drain()
            stt(w_r, w_k, -float(TWO_PI_LO), w_r, ALU.mult, ALU.add)
            eng.drain().then_inc(setup_dve, 1)
            tt(w_t2, are, are, ALU.mult)
            tt(w_t3, aim, aim, ALU.mult)
            eng.drain()
            tt(w_den, w_t2, w_t3, ALU.add)
            eng.drain()
            eng.reciprocal(w_den, w_den)
            z, z2, acc = sm[:, 6:8], sm[:, 8:10], sm[:, 10:12]
            e = sm[:, 4:6]
            ts(z, e, 2.0, None, ALU.add)
            eng.drain()
            eng.reciprocal(z, z)
            eng.drain()
            tt(z, z, e, ALU.mult)
            eng.drain()
            tt(z2, z, z, ALU.mult)
            artanh(eng, acc, z2)
            eng.drain()
            tt(acc, acc, z, ALU.mult)
            ts(sm[:, 0:2], pcol("lam", 0, 2), -1.0, 0.0, ALU.mult, ALU.max)
            eng.drain()
            stt(sm[:, 0:2], acc, 2.0, sm[:, 0:2], ALU.mult, ALU.add)
            eng.drain()
            ts(lru_c[:, 0:2], sm[:, 0:2], -4.0, None, ALU.mult)
            ts(lru_c[:, 2:4], sm[:, 0:2], 4.0, None, ALU.mult)
            for j, name in enumerate(("b_r", "b_i", "b_glu")):
                ts(half_b[:, 2 * j:2 * j + 2], pcol(name, 0, 2), 0.5, None, ALU.mult)
            ts(nea8[:], nea8[:], -1.0, None, ALU.mult)
            eng.wait_ge(setup_act, 3)
            tt(w_t2, w_half, w_half, ALU.mult)
            eng.drain()
            ts(w_cos, w_t2, -2.0, 1.0, ALU.mult, ALU.add)
            exp_exact(eng, mag[:], w_t1[:, 1024:W5])
            eng.drain()
            tt(w_t1, w_mag, w_cos, ALU.mult)
            tt(w_t2, w_mag, w_sin, ALU.mult)
            eng.drain()
            ts(w_t1, w_t1, -1.0, None, ALU.add)
            eng.drain()
            tt(w_fr, w_t1, are, ALU.mult)
            tt(w_t3, w_t2, aim, ALU.mult)
            eng.drain()
            tt(w_fr, w_fr, w_t3, ALU.add)
            tt(w_fi, w_t2, are, ALU.mult)
            eng.drain()
            tt(w_t3, w_t1, aim, ALU.mult)
            tt(w_fr, w_fr, w_den, ALU.mult)
            eng.drain()
            tt(w_fi, w_fi, w_t3, ALU.subtract)
            eng.drain()
            tt(w_fi, w_fi, w_den, ALU.mult)
            eng.drain()
            fr, fi, t2, t3 = w_fr[:, 0:1024], w_fi[:, 0:1024], w_t2[:, 0:1024], w_t3[:, 0:1024]
            out_re, out_im = prep_flat[:, 0:1024], prep_flat[:, 1024:2048]
            tt(out_re, fr, s5b[:, 0, :], ALU.mult)
            tt(t2, fi, s5b[:, 1, :], ALU.mult)
            tt(out_im, fr, s5b[:, 1, :], ALU.mult)
            tt(t3, fi, s5b[:, 0, :], ALU.mult)
            eng.drain()
            tt(out_re, out_re, t2, ALU.subtract)
            tt(out_im, out_im, t3, ALU.add)
            cos, sin = prep[:, 2], prep[:, 3]
            eng.tensor_copy(cos[:, :, 0], w_cos[:, 1024:W5])
            eng.tensor_copy(sin[:, :, 0], w_sin[:, 1024:W5])
            eng.drain()
            n = 1
            while n < P:
                cn = cos[:, :, n - 1:n].to_broadcast([P, 8, n])
                sn = sin[:, :, n - 1:n].to_broadcast([P, 8, n])
                ta, tb = v3(w_t2[:, 0:8 * n], 8), v3(w_t3[:, 0:8 * n], 8)
                tt(ta, sin[:, :, 0:n], sn, ALU.mult)
                tt(tb, cos[:, :, 0:n], sn, ALU.mult)
                tt(cos[:, :, n:2 * n], cos[:, :, 0:n], cn, ALU.mult)
                tt(sin[:, :, n:2 * n], sin[:, :, 0:n], cn, ALU.mult)
                eng.drain()
                tt(cos[:, :, n:2 * n], cos[:, :, n:2 * n], ta, ALU.subtract)
                tt(sin[:, :, n:2 * n], sin[:, :, n:2 * n], tb, ALU.add)
                eng.drain()
                n *= 2
            eng.drain().then_inc(setup_dve, 1)

        def sp_setup(eng):
            eng.dma_start(par[:], t["par"]).then_inc(par_loaded, 16)
            eng.dma_start(s5p[:], t["s5p"]).then_inc(par_loaded, 16)
            eng.dma_start(s5b[:], t["s5b"]).then_inc(par_loaded, 16)
            eng.wait_ge(setup_dve, 3)
            eng.dma_start(u_dram[:, :, 0:3], zero3[:]).then_inc(par_loaded, 16)
            eng.dma_start(prep_dram, prep_flat).then_inc(par_loaded, 16)
            eng.wait_ge(par_loaded, 16 * 5)

        block = ctx.enter_context(nc.Block())

        @block.tensor
        def _(pe):
            c = Counts(pe)
            c.meet()
            pe_stage_kv(pe, c)
            c.meet()
            for p in range(len(PASSES)):
                pe_stage_a(pe, c, p)
                c.meet()
                pe_stage_m(pe, c, p)
                c.meet()
                pe_stage_b(pe, c, p)
                c.meet()

        @block.scalar
        def _(act):
            c = Counts(act)
            act_setup(act)
            c.meet()
            act_stage_kv(act, c)
            c.meet()
            for p in range(len(PASSES)):
                act_stage_a(act, c, p)
                c.meet()
                act_stage_m(act, c, p)
                c.meet()
                act_stage_b(act, c, p)
                c.meet()

        @block.vector
        def _(dve):
            c = Counts(dve)
            dve_setup(dve)
            c.meet()
            dve_stage_kv(dve, c)
            c.meet()
            for p in range(len(PASSES)):
                dve_stage_a(dve, c, p)
                c.meet()
                dve_stage_m(dve, c, p)
                c.meet()
                dve_stage_b(dve, c, p)
                c.meet()

        @block.gpsimd
        def _(pool):
            c = Counts(pool)
            c.meet()
            pool_stage_kv(pool, c)
            c.meet()
            for p in range(len(PASSES)):
                pool_stage_a(pool, c, p)
                c.meet()
                pool_stage_m(pool, c, p)
                c.meet()
                pool_stage_b(pool, c, p)
                c.meet()

        @block.sync
        def _(sp):
            c = Counts(sp)
            sp_setup(sp)
            c.meet()
            sp_stage_kv(sp, c)
            c.meet()
            for p in range(len(PASSES)):
                sp_stage_a(sp, c, p)
                c.meet()
                sp_stage_m(sp, c, p)
                c.meet()
                sp_stage_b(sp, c, p)
                c.meet()


def channel_major(a, tiles):
    return np.ascontiguousarray(a.reshape(a.shape[0], tiles, P).transpose(2, 1, 0))


def column_slab(w):
    return w.reshape(KD, P, 256).transpose(1, 0, 2).reshape(P, SLAB)


def row_slab(w):
    return w.reshape(2, P, D).transpose(1, 0, 2).reshape(P, SLAB)


def by_channel(v):
    return v.reshape(-1, P).T


def rows(v):
    return np.tile(v.reshape(1, -1), (P, 1))


def lay_out(a):
    f = np.float32
    a = {k: np.asarray(v) for k, v in a.items()}
    o = {}
    tokens = np.concatenate([a["x_prompt"][0], a["x_sample"].reshape(SEQS * SEQ_LEN, D)])
    o["x_t"] = channel_major(tokens, KD)
    o["mem_t"] = channel_major(a["mem_prompt"][0], KD)
    w = a["w_in"][0]
    starts = [0, 256] + [768 + 256 * j for j in range(3)] + [1540 + 256 * j for j in range(3)] + [2572, 512, 2308]
    o["w_in"] = np.stack([column_slab(w[:, s:s + 256]) for s in starts])
    small = np.concatenate([w[:, 1536:1540], w[:, 2568:2572], w[:, 2564:2568]], axis=1)
    o["w_small"] = small.reshape(KD, P, N_SMALL).transpose(1, 0, 2).reshape(P, -1)
    cols = lambda w, n: [column_slab(w[:, j * 256:j * 256 + 256]) for j in range(n)]
    rws = lambda w, n: [row_slab(w[j * 256:j * 256 + 256]) for j in range(n)]
    o["w_kv"] = np.stack(cols(a["w_ck"][0], 4) + cols(a["w_cv"][0], 4))
    gate, up = cols(a["w_ffn_gate"][0], ROUNDS), cols(a["w_ffn_up"][0], ROUNDS)
    o["w_a"] = np.stack(cols(a["w_out"][0], 4) + cols(a["w_cq"][0], 4) + [s for pair in zip(gate, up) for s in pair])
    o["w_b"] = np.stack(rws(a["w_co"][0], 4) + rws(a["w_ffn_down"][0], ROUNDS))
    o["k_cache_t"] = (a["cache_mem_k"][0].transpose(2, 0, 3, 1).reshape(HEADS, SEQS, 2, P, MEM)
                      .transpose(0, 1, 3, 2, 4).reshape(HEADS, SEQS, P, 512))
    o["v_cache"] = (a["cache_mem_v"][0].transpose(2, 0, 1, 3).reshape(HEADS, SEQS, 2, P, HD)
                    .transpose(0, 1, 3, 2, 4).reshape(HEADS, SEQS, P, 512))

    def fill(table, parts, width):
        out = np.zeros((P, width), f)
        for name, v in parts.items():
            c0, n = table[name]
            out[:, c0:c0 + n] = v
        return out

    t_ = np.arange(P)
    same = (t_[:, None] // SEQ_LEN) == (t_[None, :] // SEQ_LEN)
    upper, strict, lower = t_[:, None] <= t_[None, :], t_[:, None] < t_[None, :], t_[:, None] > t_[None, :]
    lev = [((t_[:, None] // (2 * b)) == (t_[None, :] // (2 * b))) & (t_[None, :] // b % 2 == 1)
           & (t_[:, None] // b % 2 == 0) for b in LEVELS]
    ct = {}
    for part in ("re", "im"):
        c = np.zeros((P, 8, P), f)
        for g in range(16):
            ch = g * 16 % P
            c[g % 2 * 64:g % 2 * 64 + 64, g // 2, ch:ch + 16] = a["s5_c_" + part][0][g].T
        ct[part] = c.reshape(P, -1)
    lru = {}
    for name in ("w_r", "w_i"):
        c = np.zeros((P, 2, P), f)
        for b in range(4):
            r = slice(b % 2 * 64, b % 2 * 64 + 64)
            c[r, b // 2, r] = a["lru_" + name][0][b]
        lru[name] = c.reshape(P, -1)
    o["mixc"] = fill(MIX, dict(
        U=upper, L=lower, strict=strict, Us=upper & same, Ls=lower & same, stricts=strict & same, ident=np.eye(P),
        ones=1.0, levels=np.stack(lev, 1).reshape(P, -1), seqsel=t_[:, None] // SEQ_LEN == np.arange(SEQS)[None, :],
        ct_re=ct["re"], ct_im=ct["im"], glu=a["s5_w_glu"][0].reshape(2, P, 256).transpose(1, 0, 2).reshape(P, 512),
        w_r=lru["w_r"], w_i=lru["w_i"], ssd_norm=rows(a["ssd_norm_g"][0]), gdn_norm=rows(np.tile(a["gdn_norm_g"][0], 4)),
        ssd_d=rows(np.repeat(a["ssd_d"][0], 64))), MIX_COLS)
    conv_w = np.concatenate([a["lru_conv_w"][0], a["ssd_conv_w"][0], a["gdn_conv_w"][0]], axis=1)
    conv_b = np.concatenate([a["lru_conv_b"][0], a["ssd_conv_b"][0], np.zeros(768, f)])
    o["par"] = fill(PAR, dict(
        conv_w=np.concatenate([by_channel(conv_w[j]) for j in range(4)], axis=1), conv_b=by_channel(conv_b),
        s5_d=by_channel(a["s5_d"][0]), b_glu=by_channel(a["s5_b_glu"][0]), b_r=by_channel(a["lru_b_r"][0]),
        b_i=by_channel(a["lru_b_i"][0]), lam=by_channel(a["lru_lambda"][0]),
        bias8=rows(np.concatenate([a["ssd_dt_bias"][0], a["gdn_dt_bias"][0]])),
        alog8=rows(np.concatenate([a["ssd_a_log"][0], a["gdn_a_log"][0]])),
        g_mix=by_channel(a["norm_mix_g"][0]), g_mem=by_channel(a["norm_mem_g"][0]),
        g_cross=by_channel(a["norm_cross_g"][0]), g_ffn=by_channel(a["norm_ffn_g"][0]),
        g_final=by_channel(a["norm_final_g"])), PAR_COLS)
    states = [a["s5_a_re"][0].reshape(-1), a["s5_a_im"][0].reshape(-1), np.repeat(a["s5_log_dt"][0], 64)]
    o["s5p"] = np.stack([np.concatenate([rows(v), by_channel(v)], axis=1) for v in states], axis=1)
    s5b = np.zeros((P, 2, 1024), f)
    for part, name in enumerate(("s5_b_re", "s5_b_im")):
        for g in range(16):
            ch = g * 16 % P
            s5b[ch:ch + 16, part, g * 64:g * 64 + 64] = a[name][0][g].T
    o["s5b"] = s5b
    caches = np.concatenate([a["cache_lru_conv"][0], a["cache_ssd_conv"][0], a["cache_gdn_conv"][0]], axis=2)
    o["conv_caches"] = (caches.transpose(2, 0, 1).reshape(N_CONV, P, SEQS, 3).transpose(1, 0, 2, 3)
                        .reshape(P, N_CONV * SEQS, 3))
    o["ssd_hs"] = a["state_ssd"][0].transpose(3, 0, 1, 2).reshape(P, -1)
    g = np.zeros((2, 64, SEQS, 2, 2, 64), f)
    s = a["state_gdn"][0].reshape(SEQS, 2, 2, 64, 64)
    for half in range(2):
        g[half, :, :, :, half] = s[:, :, half].transpose(2, 0, 1, 3)
    o["gdn_ss"] = g.reshape(P, -1)
    o["s5_xs"] = np.concatenate([a["state_s5_" + part][0].reshape(SEQS, 8, P).transpose(2, 1, 0).reshape(P, -1)
                                 for part in ("re", "im")], axis=1)
    o["lru_hs"] = a["state_lru_h"][0].reshape(SEQS, 2, P).transpose(2, 1, 0).reshape(P, -1)
    return {k: np.ascontiguousarray(v, dtype=f) for k, v in o.items()}


OUTPUTS = dict(y_t=[P, KD, TOKENS], p_mem_kt=[D, MEM], p_mem_v=[MEM, D], p_ssd=[P, 256], p_gdn=[P, 256],
               p_s5=[P, 16], p_lru=[P, 2], p_tail=[P, N_CONV, 3], s_tail=[P, N_CONV * SEQS * 3],
               s_ssd=[P, SEQS * 256], s_gdn=[P, SEQS * 256], s_s5=[P, 16 * SEQS], s_lru=[P, 2 * SEQS])


def unpack(r):
    y = r["y_t"].transpose(2, 1, 0).reshape(TOKENS, D)

    def states(lru, tail, ssd, gdn, s5, n):
        conv = tail.reshape(P, N_CONV, n, 3).transpose(2, 3, 1, 0).reshape(n, 3, N_CONV * P)
        g = gdn.reshape(2, 64, n, 2, 2, 64)
        g = np.stack([g[half, :, :, :, half] for half in range(2)])
        s5 = s5.reshape(P, 2, 8, n).transpose(1, 3, 2, 0).reshape(2, n, 16, 64)
        out = (lru.reshape(P, 2, n).transpose(2, 1, 0).reshape(n, 256), conv[:, :, 0:256],
               ssd.reshape(P, n, 4, 64).transpose(1, 2, 3, 0), conv[:, :, 256:1024],
               g.transpose(2, 3, 0, 1, 4).reshape(n, 4, 64, 64), conv[:, :, 1024:1792], s5[0], s5[1])
        return tuple(np.ascontiguousarray(v)[None] for v in out)

    mem_k = np.ascontiguousarray(r["p_mem_kt"].T).reshape(1, 1, MEM, HEADS, HD)
    mem_v = r["p_mem_v"].reshape(1, 1, MEM, HEADS, HD)
    return ((np.ascontiguousarray(y[:PROMPT])[None], np.ascontiguousarray(y[PROMPT:]).reshape(SEQS, SEQ_LEN, D))
            + states(r["p_lru"], r["p_tail"], r["p_ssd"], r["p_gdn"], r["p_s5"], 1) + (mem_k, mem_v)
            + states(r["s_lru"], r["s_tail"], r["s_ssd"], r["s_gdn"], r["s_s5"], SEQS))


def kernel(**inputs):
    from concourse import bacc
    from concourse.bass_utils import run_bass_kernel_spmd

    nc = bacc.Bacc("TRN2", target_bir_lowering=False, num_devices=1)
    arrays = lay_out(inputs)
    t = {name: nc.dram_tensor(name, list(a.shape), F32, kind="ExternalInput").ap() for name, a in arrays.items()}
    t.update((name, nc.dram_tensor(name, shape, F32, kind="ExternalOutput").ap()) for name, shape in OUTPUTS.items())
    program(nc, t)
    r = run_bass_kernel_spmd(nc, [arrays], core_ids=[0])
    return unpack(r.results[0])
```

```python
from contextlib import ExitStack

import numpy as np

import concourse.bass as bass
from concourse import mybir

F32 = mybir.dt.float32
F32R = mybir.dt.float32r
ACT = mybir.ActivationFunctionType
ALU = mybir.AluOpType
AX_X = mybir.AxisListType.X

P = 128
D = 1024
KD = D // P
PROMPT, SEQS, SEQ_LEN = 2048, 8, 16
TOKENS = PROMPT + SEQS * SEQ_LEN
TILES = TOKENS // P
PASSES = ((0, 6), (6, 12), (12, 17))
CMAX = 6 * P
MEM = 256
HEADS, HD = 4, 256
KVS = 3
FFN = 2816
ROUNDS = FFN // 256
EPS = 1e-6
SLAB = 2048

U_TILES, GATE, CONV, DU = 18, 0, 2, 16
N_CONV = 14
N_SMALL = 12
SLABS_IN = 11
LEVELS = (1, 2, 4, 8, 16, 32, 64)

_MIX = [("U", 128), ("L", 128), ("strict", 128), ("Us", 128), ("Ls", 128), ("stricts", 128),
        ("ident", 128), ("ones", 128), ("levels", 7 * 128), ("seqsel", 8),
        ("ct_re", 1024), ("ct_im", 1024), ("glu", 512), ("w_r", 256), ("w_i", 256),
        ("ssd_norm", 256), ("gdn_norm", 256), ("ssd_d", 256)]
MIX, _n = {}, 0
for _name, _w in _MIX:
    MIX[_name] = (_n, _w)
    _n += _w
MIX_COLS = _n
_PAR = [("conv_w", 4 * N_CONV), ("conv_b", N_CONV), ("s5_d", 2), ("b_glu", 2), ("b_r", 2), ("b_i", 2),
        ("lam", 2), ("bias8", 8), ("alog8", 8), ("g_mix", 8), ("g_mem", 8), ("g_cross", 8), ("g_ffn", 8),
        ("g_final", 8)]
PAR, _n = {}, 0
for _name, _w in _PAR:
    PAR[_name] = (_n, _w)
    _n += _w
PAR_COLS = _n
EGC, EGE, ETOT, BETA, DT, G8 = 0, 8, 16, 24, 28, 32
TS_COLS = 40
TWO_PI_HI, TWO_PI_MID = 6.28125, 0.0019353071693331003
TWO_PI_LO = 2 * np.pi - TWO_PI_HI - TWO_PI_MID
LN2_HI = 0.693359375
LN2_LO = float(np.log(2) - LN2_HI)
ROUND_MAGIC = 12582912.0


class Count:

    def __init__(self, sem, unit=1):
        self.sem, self.unit, self.n, self.i, self.per = sem, unit, 0, None, 0

    def begin(self, i, per):
        self.i, self.per, self.start = i, per, self.n

    def end(self, times):
        assert self.n - self.start == self.per, (self.n, self.start, self.per)
        self.n, self.i = self.start + self.per * times, None

    def next(self):
        self.n += 1
        return self.value()

    def value(self, back=0):
        v = (self.n - back) * self.unit
        return v if self.i is None else self.i * (self.per * self.unit) + v


class Loop:

    def __init__(self, eng, times, counts):
        self.eng, self.times, self.counts = eng, times, counts

    def __enter__(self):
        self.cm = self.eng.Fori(0, self.times)
        i = self.cm.__enter__()
        for c, per in self.counts:
            c.begin(i, per)
        return i

    def __exit__(self, *a):
        r = self.cm.__exit__(*a)
        if a[0] is None:
            for c, _ in self.counts:
                c.end(self.times)
        return r


def groups(p):
    n = (PASSES[p][1] - PASSES[p][0]) * P
    return ((0, 384), (384, n - 384))


def program(nc, t):
    ctx = ExitStack()
    with ctx:
        names = iter(range(10000))

        def sb(stack, name, shape, dt=F32):
            return stack.enter_context(nc.sbuf_tensor(f"{name}_sb{next(names)}", shape, dt))

        def sem(name):
            return ctx.enter_context(nc.semaphore(name))

        banks = ctx.enter_context(nc.psum_tensor("banks", [P, 8, 512], F32))

        par = sb(ctx, "par", [P, PAR_COLS])
        ones = sb(ctx, "ones", [P, P])
        ssd_h = sb(ctx, "ssd_h", [P, 256])
        gdn_s = sb(ctx, "gdn_s", [P, 2, P])
        s5_x = sb(ctx, "s5_x", [P, 2, 8])
        lru_h = sb(ctx, "lru_h", [P, 2])
        mag = sb(ctx, "mag", [P, 8])
        lru_c = sb(ctx, "lru_c", [P, 4])
        half_b = sb(ctx, "half_b", [P, 6])
        nea8 = sb(ctx, "nea8", [P, 8])
        eps = sb(ctx, "eps", [P, 1])
        raw12 = sb(ctx, "raw12", [P, 6, N_SMALL])
        tsc = sb(ctx, "tsc", [P, 6, TS_COLS])

        def pcol(name, k=0, n=1):
            return par[:, PAR[name][0] + k:PAR[name][0] + k + n]

        with ExitStack() as st:
            W5 = 8
            s5p = sb(st, "s5p", [P, 3, W5])
            s5b = sb(st, "s5b", [P, 2, 1024])
            bb = sb(st, "bb", [P, 2, 8, P])
            bt = sb(st, "bt", [P, 2, 1024])
            ident_s = sb(st, "ident_s", [P, P])
            sw = [sb(st, f"sw{i}", [P, W5]) for i in range(14)]
            prep = sb(st, "prep", [P, 4, 8, P])
            sm = sb(st, "sm", [P, 12])
            ex = sb(st, "ex", [P, 5, 8])
            exi = sb(st, "exi", [P, 8], mybir.dt.int32)
            zero3 = sb(st, "zero3", [P, U_TILES, 3])

        with ExitStack() as st:
            x = sb(st, "x", [P, KD, CMAX])
            hh = sb(st, "hh", [P, KD, CMAX], F32R)
            hl = sb(st, "hl", [P, KD, CMAX], F32R)
            a_raw = sb(st, "a_raw", [P, SLAB])
            a_hi = [sb(st, f"a_hi{s}", [P, SLAB], F32R) for s in range(2)]
            a_lo = [sb(st, f"a_lo{s}", [P, SLAB], F32R) for s in range(2)]
            b_raw = sb(st, "b_raw", [P, SLAB])
            b_hi = sb(st, "b_hi", [P, SLAB], F32R)
            b_lo = sb(st, "b_lo", [P, SLAB], F32R)
            g_hi = sb(st, "g_hi", [P, 2, CMAX], F32R)
            g_lo = sb(st, "g_lo", [P, 2, CMAX], F32R)
            stage = [sb(st, f"stage{s}", [P, 2, CMAX]) for s in range(2)]
            hf = sb(st, "hf", [P, 2, 384])
            sq = sb(st, "sq", [P, 2, 384])
            rms = sb(st, "rms", [P, 384])
            rstd = sb(st, "rstd", [P, 384])
            q_odd = sb(st, "q_odd", [P, 2, CMAX])
            kv = sb(st, "kv", [P, 2, 2, 512])
            pr = sb(st, "pr", [P, 2, MEM])
            soft = sb(st, "soft", [P, 2, 4])
            kvs = sb(st, "kvs", [P, KVS, 512])
            prs = sb(st, "prs", [P, SEQS, MEM])
            softs = sb(st, "softs", [P, 3, SEQS])
            prs_t = sb(st, "prs_t", [P, SEQS, 2, SEQ_LEN])
            ident = sb(st, "ident", [P, P])
            ws = sb(st, "ws", [P, KD * N_SMALL])
            ws_hi = sb(st, "ws_hi", [P, KD, N_SMALL], F32R)
            ws_lo = sb(st, "ws_lo", [P, KD, N_SMALL], F32R)

        with ExitStack() as st:
            mixc = sb(st, "mixc", [P, MIX_COLS])
            mprep = sb(st, "mprep", [P, 4, 8, P])
            m = {}
            for name, cols in dict(
                    u=U_TILES * 152, cv=N_CONV * P, z=512, sz=512, cur=TS_COLS, lg=8 * P, dec=8 * P, decs=512,
                    tok_x=512, tok_qk=512, tok_v=256, xdt=256, xw=256, xsd=256, sc=512, yo=256, ys=256,
                    ytm=512, sqk=512, n8=16, qkn=512, kb=256, qd=256, wk=256, kd=256, vb=256, chT=8 * P,
                    MT=512, ML=7 * 512, ST=4 * 256, X=512, qkd=512, uu=256, wT=256, delta=256, gz=256,
                    th=512, la=256, lt=256, lb=256, hs=256, gg=256, bre=1024, bim=1024, p1=1024, p2=1024,
                    p3=1024, p4=1024, s5y=256, s5t=256, ych=1024, tmp8=128, tk=8 * 64, decay5=8 * P, c5=4 * 64,
                    ssd_hs=SEQS * 256, gdn_ss=SEQS * 256, s5_xs=2 * 8 * SEQS, lru_hs=2 * SEQS, etotb=8 * SEQS,
                    tail=N_CONV * SEQS * 3).items():
                m[name] = sb(st, "m_" + name, [P, cols])
            ssd_hs = m["ssd_hs"][:].rearrange("p (s c) -> p s c", s=SEQS)
            gdn_ss = m["gdn_ss"][:].rearrange("p (s j c) -> p s j c", s=SEQS, j=2)
            s5_xs = m["s5_xs"][:].rearrange("p (r t s) -> p r t s", r=2, t=8)
            lru_hs = m["lru_hs"][:].rearrange("p (t s) -> p t s", t=2)
            etotb = m["etotb"][:].rearrange("p (s h) -> p s h", s=SEQS)
        u_dram = nc.dram_tensor("u_dram", [P, U_TILES, 3 + TOKENS], F32, kind="Internal").ap()
        z_dram = nc.dram_tensor("z_dram", [TOKENS, 512], F32, kind="Internal").ap()
        y_dram = nc.dram_tensor("y_dram", [P, KD, TOKENS], F32, kind="Internal").ap()
        prep_dram = nc.dram_tensor("prep_dram", [P, 4 * 8 * P], F32, kind="Internal").ap()

        meet_s = sem("all_engines_met")
        a_loaded = sem("a_slab_loaded")
        a_hi_s = [sem(f"a_hi_done{s}") for s in range(2)]
        a_lo_s = [sem(f"a_lo_done{s}") for s in range(2)]
        a_used_s = [sem(f"a_slab_used{s}") for s in range(2)]
        b_loaded, b_hi_s, b_lo_s, b_used_s = sem("b_slab_loaded"), sem("b_hi_done"), sem("b_lo_done"), sem("b_slab_used")
        full_s = [sem(f"bank_full{b}") for b in range(8)]
        free_s = [sem(f"bank_free{b}") for b in range(8)]
        x_loaded = [sem(f"x_loaded{g}") for g in range(2)]
        par_loaded = sem("par_loaded")
        sq_done, sq_used = sem("square_done"), sem("square_used")
        rms_done, rstd_done = sem("rms_done"), sem("rstd_done")
        hf_done, hh_done = sem("h_float_done"), sem("h_hi_done")
        hl_even_done, hl_odd_done = sem("h_lo_even_done"), sem("h_lo_odd_done")
        x_summed = sem("x_summed")
        stage_full = [sem(f"stage_full{s}") for s in range(2)]
        stage_stored = [sem(f"stage_stored{s}") for s in range(2)]
        y_loaded = [sem(f"y_loaded{g}") for g in range(2)]
        q_done, p_done, pt_done = sem("q_done"), sem("p_done"), sem("p_transposed")
        p_max, p_exp = sem("p_max"), sem("p_exp")
        kv_loaded = [sem(f"kv_loaded{s}") for s in range(2)]
        av_done, g_hi_done, g_lo_done, gate_done = sem("av_done"), sem("g_hi_done"), sem("g_lo_done"), sem("gate_done")
        kvs_loaded = [sem(f"kvs_loaded{s}") for s in range(KVS)]
        kvs_used = [sem(f"kvs_used{s}") for s in range(KVS)]
        ws_loaded, ws_hi_done, ws_lo_done, ident_loaded = (
            sem("ws_loaded"), sem("ws_hi_done"), sem("ws_lo_done"), sem("ident_loaded"))
        up_done, out_ready = sem("up_done"), sem("out_ready")
        out_stored = [sem(f"out_stored{g}") for g in range(2)]
        setup_act, setup_dve = sem("setup_by_scalar"), sem("setup_by_vector")

        class Counts:

            def __init__(self, eng):
                self.eng = eng
                self.met = Count(meet_s, 5)
                self.full = [Count(s) for s in full_s]
                self.free = [Count(s) for s in free_s]
                for f in self.free:
                    f.n = 1
                self.a_loaded = Count(a_loaded, 16)
                self.a_hi = [Count(s) for s in a_hi_s]
                self.a_lo = [Count(s) for s in a_lo_s]
                self.a_used = [Count(s) for s in a_used_s]
                self.b_loaded, self.b_hi, self.b_lo, self.b_used = (
                    Count(b_loaded, 16), Count(b_hi_s), Count(b_lo_s), Count(b_used_s))
                self.sq, self.sq_used, self.rms, self.rstd = Count(sq_done), Count(sq_used), Count(rms_done), Count(rstd_done)
                self.hf, self.hh = Count(hf_done), Count(hh_done)
                self.hl_even, self.hl_odd = Count(hl_even_done), Count(hl_odd_done)
                self.summed = Count(x_summed)
                self.x_loaded, self.y_loaded = ([Count(s, 16) for s in sems] for sems in (x_loaded, y_loaded))
                self.stage = [Count(s) for s in stage_full]
                self.stage_stored = [Count(s, 16) for s in stage_stored]
                self.q, self.p, self.pt, self.p_max, self.p_exp = Count(q_done), Count(p_done), Count(pt_done), Count(p_max), Count(p_exp)
                self.kv = [Count(s, 16) for s in kv_loaded]
                self.av, self.g_hi, self.g_lo, self.gate = Count(av_done), Count(g_hi_done), Count(g_lo_done), Count(gate_done)
                self.kvs = [Count(s, 16) for s in kvs_loaded]
                self.kvs_used = [Count(s) for s in kvs_used]
                self.up = Count(up_done)
                self.slab_a = 0

            def meet(self):
                self.eng.drain().then_inc(meet_s, 1)
                self.eng.wait_ge(meet_s, self.met.next())

            def pass_by(self):
                self.eng.drain().then_inc(meet_s, 1)
                self.met.n += 1

        def load_a(eng, c, slot, src):
            c.a_lo[slot].next()
            if c.slab_a:
                other = c.a_lo[1 - slot]
                eng.wait_ge(other.sem, other.value())
            c.slab_a += 1
            eng.dma_start(a_raw[:], src).then_inc(a_loaded, 16)

        def split_hi_a(eng, c, slot):
            eng.wait_ge(a_loaded, c.a_loaded.next())
            c.a_used[slot].next()
            eng.wait_ge(a_used_s[slot], c.a_used[slot].value(1))
            eng.activation(a_hi[slot][:], a_raw[:], ACT.Copy).then_inc(a_hi_s[slot], 1)

        def split_lo_a(eng, c, slot):
            eng.wait_ge(a_hi_s[slot], c.a_hi[slot].next())
            eng.tensor_tensor(a_lo[slot][:], a_raw[:], a_hi[slot][:].bitcast(F32),
                              ALU.subtract).then_inc(a_lo_s[slot], 1)

        def load_b(eng, c, src):
            c.b_lo.next()
            eng.wait_ge(b_lo_s, c.b_lo.value(1))
            eng.dma_start(b_raw[:], src).then_inc(b_loaded, 16)

        def split_hi_b(eng, c):
            eng.wait_ge(b_loaded, c.b_loaded.next())
            c.b_used.next()
            eng.wait_ge(b_used_s, c.b_used.value(1))
            eng.activation(b_hi[:], b_raw[:], ACT.Copy).then_inc(b_hi_s, 1)

        def split_lo_b(eng, c):
            eng.wait_ge(b_hi_s, c.b_hi.next())
            eng.tensor_tensor(b_lo[:], b_raw[:], b_hi[:].bitcast(F32), ALU.subtract).then_inc(b_lo_s, 1)

        def three(eng, out, whi, wlo, rhi, rlo, first, last):
            eng.matmul(out, whi, rhi, start=first, stop=False)
            eng.matmul(out, wlo, rhi, start=False, stop=False)
            return eng.matmul(out, whi, rlo, start=False, stop=last)

        def bank_for(eng, c, b):
            c.free[b].next()
            eng.wait_ge(free_s[b], c.free[b].value(1))

        def bank_in(eng, c, b):
            eng.wait_ge(full_s[b], c.full[b].next())

        def pe_columns(eng, c, slot, grp, new_h=False):
            eng.wait_ge(a_lo_s[slot], c.a_lo[slot].next())
            for g in range(len(grp)):
                for mt in range(2):
                    pe_column(eng, c, slot, grp, g, mt, new_h and mt == 0)

        def tile_of_h(eng, c, g, k):
            even, odd = c.h_before[g]
            if c.h_by_vector_only:
                eng.wait_ge(hl_odd_done, odd + k + 1)
            elif k % 2 == 0:
                eng.wait_ge(hl_even_done, even + k // 2 + 1)
            else:
                eng.wait_ge(hl_odd_done, odd + (k + 1) // 2)

        def pe_column(eng, c, slot, grp, g, mt, new_h=False):
            hi = a_hi[slot][:].rearrange("p (k c) -> p k c", k=KD)
            lo = a_lo[slot][:].rearrange("p (k c) -> p k c", k=KD)
            b, (c0, n), w = 2 * g + mt, grp[g], slice(mt * P, mt * P + P)
            bank_for(eng, c, b)
            for k in range(KD):
                if new_h:
                    tile_of_h(eng, c, g, k)
                last = three(eng, banks[:, b, 0:n], hi[:, k, w], lo[:, k, w], hh[:, k, c0:c0 + n],
                             hl[:, k, c0:c0 + n], k == 0, k == KD - 1)
            if g == len(grp) - 1 and mt == 1:
                eng.drain().then_inc(a_used_s[slot], 1)
            last.then_inc(full_s[b], 1)

        def pe_tokens(eng, c, slot, tiles):
            eng.wait_ge(a_lo_s[slot], c.a_lo[slot].next())
            hi = a_hi[slot][:].rearrange("p (k c) -> p k c", k=KD)
            lo = a_lo[slot][:].rearrange("p (k c) -> p k c", k=KD)
            for i in range(tiles):
                b = i % 4
                bank_for(eng, c, b)
                w = slice(i * P, i * P + P)
                for k in range(KD):
                    last = three(eng, banks[:, b, 0:256], hh[:, k, w], hl[:, k, w], hi[:, k, :], lo[:, k, :],
                                 k == 0, k == KD - 1)
                if i == tiles - 1:
                    eng.drain().then_inc(a_used_s[slot], 1)
                last.then_inc(full_s[b], 1)

        def pe_rows(eng, c, grp):
            eng.wait_ge(b_lo_s, c.b_lo.next())
            hi = b_hi[:].rearrange("p (k d) -> p k d", k=2)
            lo = b_lo[:].rearrange("p (k d) -> p k d", k=2)
            for g, (c0, n) in enumerate(grp):
                eng.wait_ge(g_hi_done, c.g_hi.next())
                eng.wait_ge(g_lo_done, c.g_lo.next())
                for d in range(KD):
                    b = 4 + d % 4
                    bank_for(eng, c, b)
                    for k in range(2):
                        w = slice(d * P, d * P + P)
                        last = three(eng, banks[:, b, 0:n], hi[:, k, w], lo[:, k, w], g_hi[:, k, c0:c0 + n],
                                     g_lo[:, k, c0:c0 + n], k == 0, k == 1)
                    if g == len(grp) - 1 and d == KD - 1:
                        eng.drain().then_inc(b_used_s, 1)
                    last.then_inc(full_s[b], 1)

        def pe_norm(eng, c, grp):
            for g, (c0, n) in enumerate(grp):
                bank_for(eng, c, 4)
                for k in range(KD):
                    eng.wait_ge(sq_done, c.sq.next())
                    last = eng.matmul(banks[:, 4, 0:n], ones[:], sq[:, k % 2, 0:n], start=k == 0, stop=k == KD - 1)
                    if k < KD - 1:
                        last.then_inc(sq_used, 1)
                last.then_inc(full_s[4], 1)

        def pe_small(eng, c, tiles):
            for i in range(tiles):
                b = i % 4
                bank_for(eng, c, b)
                w = slice(i * P, i * P + P)
                for k in range(KD):
                    last = three(eng, banks[:, b, 0:N_SMALL], hh[:, k, w], hl[:, k, w], ws_hi[:, k, :],
                                 ws_lo[:, k, :], k == 0, k == KD - 1)
                last.then_inc(full_s[b], 1)

        def prompt_tiles(p):
            return min(PASSES[p][1], TILES - 1) - PASSES[p][0]

        def pe_attend(eng, c, p, slot, grp, more):
            q, pt = (stage[0], q_odd)[slot], stage[1]
            rest = [(g, mt) for g in range(len(grp)) for mt in range(2)] if more else []
            if more:
                eng.wait_ge(a_lo_s[1 - slot], c.a_lo[1 - slot].next())
            nt = prompt_tiles(p)
            c.kv[slot].n += 1
            eng.wait_ge(kv_loaded[slot], c.kv[slot].next())
            eng.wait_ge(ident_loaded, 16 * (p + 1))
            eng.wait_ge(q_done, c.q.next())

            def scores(i):
                b = 4 + i % 2
                bank_for(eng, c, b)
                for e in range(2):
                    last = eng.matmul(banks[:, b, 0:MEM], q[:, e, i * P:i * P + P], kv[:, slot, 0, e * MEM:(e + 1) * MEM],
                                      start=e == 0, stop=e == 1)
                last.then_inc(full_s[b], 1)

            def turn(i):
                b = 6 + i % 2
                eng.wait_ge(p_done, c.p.next())
                bank_for(eng, c, b)
                for mt in range(2):
                    last = eng.transpose(banks[:, b, mt * P:mt * P + P], pr[:, i % 2, mt * P:mt * P + P], ident[:])
                last.then_inc(full_s[b], 1)

            for i in range(nt + 1):
                if i < nt:
                    scores(i)
                for part in rest[i:i + 1]:
                    pe_column(eng, c, 1 - slot, grp, *part)
                if i > 0:
                    turn(i - 1)
            sample = p == len(PASSES) - 1
            if sample:
                s0 = nt * P
                for s in range(SEQS):
                    b = 4 + s // 2
                    if s % 2 == 0:
                        bank_for(eng, c, b)
                    eng.wait_ge(kvs_loaded[s % KVS], c.kvs[s % KVS].next())
                    for e in range(2):
                        last = eng.matmul(banks[0:SEQ_LEN, b, s % 2 * MEM:s % 2 * MEM + MEM],
                                          q[:, e, s0 + s * SEQ_LEN:s0 + (s + 1) * SEQ_LEN],
                                          kvs[:, s % KVS, e * MEM:(e + 1) * MEM], start=e == 0, stop=e == 1)
                    eng.drain().then_inc(kvs_used[s % KVS], 1)
                    if s % 2:
                        last.then_inc(full_s[b], 1)
            eng.wait_ge(pt_done, c.pt.next())
            for g, (c0, n) in enumerate(grp):
                n1 = min(n, nt * P - c0)
                for e in range(2):
                    b = 2 * g + e
                    bank_for(eng, c, b)
                    for mt in range(2):
                        last = eng.matmul(banks[:, b, 0:n1], kv[:, slot, 1, mt * MEM + e * P:mt * MEM + e * P + P],
                                          pt[:, mt, c0:c0 + n1], start=mt == 0, stop=mt == 1)
                    if n1 == n:
                        last.then_inc(full_s[b], 1)
            if sample:
                eng.wait_ge(p_done, c.p.next())
                bank_for(eng, c, 4)
                for s in range(SEQS):
                    for mt in range(2):
                        j = (s * 2 + mt) * SEQ_LEN
                        last = eng.transpose(banks[:, 4, j:j + SEQ_LEN], prs[0:SEQ_LEN, s, mt * P:mt * P + P],
                                             ident[0:SEQ_LEN, 0:SEQ_LEN])
                last.then_inc(full_s[4], 1)
                eng.wait_ge(pt_done, c.pt.next())
                for s in range(SEQS):
                    eng.wait_ge(kvs_loaded[s % KVS], c.kvs[s % KVS].next())
                    for e in range(2):
                        j = n1 + s * SEQ_LEN
                        for mt in range(2):
                            last = eng.matmul(banks[:, 2 + e, j:j + SEQ_LEN],
                                              kvs[:, s % KVS, mt * MEM + e * P:mt * MEM + e * P + P],
                                              prs_t[:, s, mt, :], start=mt == 0, stop=mt == 1)
                        if s == SEQS - 1:
                            last.then_inc(full_s[2 + e], 1)
                    eng.drain().then_inc(kvs_used[s % KVS], 1)
            eng.drain().then_inc(av_done, 1)

        def pe_stage_kv(eng, c):
            grp = ((0, MEM),)
            pe_norm(eng, c, grp)
            pe_h(c, grp, KD // 2, KD // 2)
            for n in range(4):
                pe_columns(eng, c, n % 2, grp, new_h=n == 0)
            for n in range(4):
                pe_tokens(eng, c, n % 2, 2)

        def pe_h(c, grp, even, odd):
            c.h_before = [(c.hl_even.n + g * even, c.hl_odd.n + g * odd) for g in range(len(grp))]
            c.h_by_vector_only = even == 0
            c.hl_even.n += len(grp) * even
            c.hl_odd.n += len(grp) * odd

        def pe_stage_a(eng, c, p):
            grp, nt = groups(p), PASSES[p][1] - PASSES[p][0]
            pe_norm(eng, c, grp)
            pe_h(c, grp, KD // 2, KD // 2)
            with Loop(eng, 4, [(x, 2) for x in c.free[0:4]] + [(x, 1) for x in c.a_lo]):
                for s in range(2):
                    pe_columns(eng, c, s, grp, new_h=s == 0)
            pe_columns(eng, c, 0, grp)
            pe_tokens(eng, c, 1, nt)
            pe_tokens(eng, c, 0, nt)
            eng.wait_ge(ws_lo_done, p + 1)
            pe_small(eng, c, nt)

        def pe_stage_b(eng, c, p):
            grp = groups(p)
            pe_h(c, grp, 0, KD)
            with Loop(eng, 2, [(x, 2) for x in c.free[0:4]] + [(x, 1) for x in c.a_lo]):
                for s in range(2):
                    pe_columns(eng, c, s, grp, new_h=s == 0)
            pe_norm(eng, c, grp)
            pe_h(c, grp, KD // 2, KD // 2)
            pe_columns(eng, c, 0, grp, new_h=True)
            for h in range(HEADS):
                pe_attend(eng, c, p, h % 2, grp, h < HEADS - 1)
                pe_rows(eng, c, grp)
            pe_norm(eng, c, grp)
            pe_h(c, grp, KD // 2, KD // 2)
            pe_columns(eng, c, 0, grp, new_h=True)
            pe_columns(eng, c, 1, grp)
            with Loop(eng, ROUNDS - 1, [(x, 2) for x in c.free[0:4]] + [(x, 4) for x in c.free[4:8]]
                      + [(x, 1) for x in c.a_lo] + [(c.b_lo, 1), (c.g_hi, 2), (c.g_lo, 2)]):
                pe_columns(eng, c, 0, grp)
                pe_rows(eng, c, grp)
                pe_columns(eng, c, 1, grp)
            pe_rows(eng, c, grp)
            pe_norm(eng, c, grp)

        def act_norm(eng, c, grp, need, final=False, split_between=False):
            for g, (c0, n) in enumerate(grp):
                if need is None:
                    eng.wait_ge(x_loaded[g], c.x_loaded[g].next())
                for k in range(KD):
                    if need:
                        eng.wait_ge(x_summed, need[g][k])
                    if k >= 2:
                        eng.wait_ge(sq_used, c.sq_used.next())
                    eng.activation(sq[:, k % 2, 0:n], x[:, k, c0:c0 + n], ACT.Square).then_inc(sq_done, 1)
                c.sq_used.n += 1
                bank_in(eng, c, 4)
                if g:
                    eng.wait_ge(rstd_done, c.rstd.value())
                c.rstd.n += 1
                eng.activation(rms[:, 0:n], banks[:, 4, 0:n], ACT.Sqrt, bias=eps[:], scale=1.0 / D).then_inc(rms_done, 1)
                eng.drain().then_inc(free_s[4], 1)
                if final:
                    continue
                for k in range(KD):
                    eng.wait_ge(hf_done, c.hf.next())
                    eng.activation(hh[:, k, c0:c0 + n], hf[:, k % 2, 0:n], ACT.Copy).then_inc(hh_done, 1)
                if split_between and g == 0:
                    split_hi_a(eng, c, 1)

        def skip(counts, which):
            for b in which:
                counts[b].n += 1

        def banks_of_columns(grp):
            return [2 * g + mt for g in range(len(grp)) for mt in range(2)]

        def banks_of_rows(grp):
            return [4 + d % 4 for _ in grp for d in range(KD)]

        def sums_by_rows(c, grp, sets):
            c.summed.n += sets * KD * len(grp)
            base = c.summed.n - KD * len(grp)
            return [[base + g * KD + k + 1 for k in range(KD)] for g in range(len(grp))]

        def sums_by_columns(c, grp):
            c.summed.n += 4 * 2 * len(grp)
            base = c.summed.n - 2 * len(grp)
            return [[base + 2 * g + 2] * KD for g in range(len(grp))]

        def act_out_columns(eng, c, slot, grp):
            eng.wait_ge(stage_stored[slot], c.stage_stored[slot].value())
            c.stage_stored[slot].n += 1
            for g, (c0, n) in enumerate(grp):
                for mt in range(2):
                    b = 2 * g + mt
                    bank_in(eng, c, b)
                    eng.activation(stage[slot][:, mt, c0:c0 + n], banks[:, b, 0:n], ACT.Copy).then_inc(free_s[b], 1)
            eng.drain().then_inc(stage_full[slot], 1)

        def act_out_tokens(eng, c, slot, tiles):
            out = stage[slot][:].rearrange("p a b -> p (a b)")
            eng.wait_ge(stage_stored[slot], c.stage_stored[slot].value())
            c.stage_stored[slot].n += 1
            for i in range(tiles):
                bank_in(eng, c, i % 4)
                eng.activation(out[:, i * 256:i * 256 + 256], banks[:, i % 4, 0:256], ACT.Copy).then_inc(free_s[i % 4], 1)
            eng.drain().then_inc(stage_full[slot], 1)

        def act_stage_kv(eng, c):
            grp = ((0, MEM),)
            for s in range(2):
                split_hi_a(eng, c, s)
            act_norm(eng, c, grp, None)
            for n in range(8):
                if n < 4:
                    act_out_columns(eng, c, n % 2, grp)
                else:
                    act_out_tokens(eng, c, n % 2, 2)
                if n + 2 < 8:
                    split_hi_a(eng, c, n % 2)

        def act_stage_a(eng, c, p):
            grp, nt = groups(p), PASSES[p][1] - PASSES[p][0]
            split_hi_a(eng, c, 0)
            act_norm(eng, c, grp, None, split_between=True)
            eng.wait_ge(ws_loaded, 16 * (p + 1))
            eng.activation(ws_hi[:].rearrange("p k c -> p (k c)"), ws[:], ACT.Copy).then_inc(ws_hi_done, 1)
            with Loop(eng, 4, [(x, 2) for x in c.full[0:4]] + [(x, 1) for x in c.a_used]
                      + [(c.a_loaded, 2)] + [(x, 1) for x in c.stage_stored]):
                for s in range(2):
                    act_out_columns(eng, c, s, grp)
                    split_hi_a(eng, c, s)
            act_out_columns(eng, c, 0, grp)
            split_hi_a(eng, c, 0)
            act_out_tokens(eng, c, 1, nt)
            act_out_tokens(eng, c, 0, nt)
            skip(c.full, [i % 4 for i in range(nt)])

        def act_q(eng, c, h, grp):
            q = (stage[0], q_odd)[h % 2]
            for g, (c0, n) in enumerate(grp):
                for mt in range(2):
                    b = 2 * g + mt
                    bank_in(eng, c, b)
                    eng.activation(q[:, mt, c0:c0 + n], banks[:, b, 0:n], ACT.Copy,
                                   scale=HD ** -0.5).then_inc(free_s[b], 1)
            eng.drain().then_inc(q_done, 1)

        def act_attend(eng, c, p, h, grp):
            pt = stage[1]
            nt = prompt_tiles(p)
            sample = p == len(PASSES) - 1

            def weights(i):
                eng.wait_ge(p_max, c.p_max.next())
                eng.activation(pr[:, i % 2, :], banks[:, 4 + i % 2, 0:MEM], ACT.Exp, bias=soft[:, i % 2, 1:2],
                               accum_out=soft[:, i % 2, 2:3])
                eng.drain().then_inc(free_s[4 + i % 2], 1)
                eng.drain().then_inc(p_exp, 1)

            def turned(i):
                bank_in(eng, c, 6 + i % 2)
                out = pt[:, :, i * P:i * P + P]
                eng.activation(out, banks[:, 6 + i % 2, 0:MEM].rearrange("p (a b) -> p a b", a=2),
                               ACT.Copy).then_inc(free_s[6 + i % 2], 1)

            for i in range(nt + 1):
                if i < nt:
                    weights(i)
                if i > 0:
                    turned(i - 1)
            skip(c.full, [4 + i % 2 for i in range(nt)])
            eng.drain().then_inc(pt_done, 1)
            if h < HEADS - 1:
                act_q(eng, c, h + 1, grp)
            if sample:
                skip(c.full, [4, 5, 6, 7])
                eng.wait_ge(p_max, c.p_max.next())
                eng.activation(prs[0:SEQ_LEN], prs[0:SEQ_LEN], ACT.Exp).then_inc(p_exp, 1)
                bank_in(eng, c, 4)
                eng.activation(prs_t[:].rearrange("p a b c -> p (a b c)"), banks[:, 4, 0:SEQS * 2 * SEQ_LEN],
                               ACT.Copy).then_inc(free_s[4], 1)
                eng.drain().then_inc(pt_done, 1)

        def act_stage_b(eng, c, p):
            grp = groups(p)
            for g in range(2):
                c.x_loaded[g].n += 1
            for g, (c0, n) in enumerate(grp):
                split_hi_a(eng, c, g)
                eng.wait_ge(y_loaded[g], c.y_loaded[g].next())
                for k in range(KD):
                    eng.activation(hh[:, k, c0:c0 + n], x[:, k, c0:c0 + n], ACT.Copy).then_inc(hh_done, 1)
            skip(c.full, banks_of_columns(grp) * 4)
            for n in range(4):
                split_hi_a(eng, c, n % 2)
            split_hi_b(eng, c)
            act_norm(eng, c, grp, sums_by_columns(c, grp))
            act_q(eng, c, 0, grp)
            for h in range(HEADS):
                split_hi_a(eng, c, h % 2)
                act_attend(eng, c, p, h, grp)
                for g, (c0, n) in enumerate(grp):
                    for e in range(2):
                        b = 2 * g + e
                        bank_in(eng, c, b)
                        eng.activation(g_hi[:, e, c0:c0 + n], banks[:, b, 0:n], ACT.Copy)
                    eng.drain().then_inc(g_hi_done, 1)
                skip(c.full, banks_of_rows(grp))
                split_hi_b(eng, c)
            act_norm(eng, c, grp, sums_by_rows(c, grp, HEADS))

            def gate():
                for g, (c0, n) in enumerate(grp):
                    for mt in range(2):
                        b = 2 * g + mt
                        bank_in(eng, c, b)
                        if g == 0 and mt == 0:
                            eng.wait_ge(g_lo_done, c.g_lo.value())
                        eng.activation(stage[0][:, mt, c0:c0 + n], banks[:, b, 0:n], ACT.Silu).then_inc(free_s[b], 1)
                    eng.drain().then_inc(gate_done, 1)
                skip(c.full, banks_of_columns(grp))

            def up():
                for g, (c0, n) in enumerate(grp):
                    eng.wait_ge(up_done, c.up.next())
                    eng.activation(g_hi[:, :, c0:c0 + n], stage[0][:, :, c0:c0 + n], ACT.Copy).then_inc(g_hi_done, 1)

            c.g_lo.n += HEADS * len(grp)
            gate()
            split_hi_a(eng, c, 0)
            up()
            split_hi_a(eng, c, 1)
            c.g_lo.n += len(grp)
            with Loop(eng, ROUNDS - 2, [(x, 2) for x in c.full[0:4]] + [(x, 1) for x in c.a_used]
                      + [(c.a_loaded, 2), (c.b_loaded, 1), (c.b_used, 1), (c.g_lo, 2), (c.up, 2)]):
                gate()
                split_hi_a(eng, c, 0)
                split_hi_b(eng, c)
                up()
                split_hi_a(eng, c, 1)
                c.g_lo.n += len(grp)
            gate()
            split_hi_b(eng, c)
            up()
            c.g_lo.n += len(grp)
            skip(c.full, banks_of_rows(grp) * ROUNDS)
            act_norm(eng, c, grp, sums_by_rows(c, grp, ROUNDS), final=True)

        def dve_norm(eng, c, grp, gain, final=False):
            def low_odd(g, k, c0, n):
                eng.wait_ge(hh_done, c.hh.value() + g * KD + k + 1)
                eng.tensor_tensor(hl[:, k, c0:c0 + n], hf[:, 1, 0:n], hh[:, k, c0:c0 + n].bitcast(F32),
                                  ALU.subtract).then_inc(hl_odd_done, 1)

            for g, (c0, n) in enumerate(grp):
                eng.wait_ge(rms_done, c.rms.next())
                eng.drain()
                eng.reciprocal(rstd[:, 0:n], rms[:, 0:n]).then_inc(rstd_done, 1)
                eng.drain()
                for k in range(KD):
                    if final:
                        eng.scalar_tensor_tensor(x[:, k, c0:c0 + n], x[:, k, c0:c0 + n], pcol(gain, k), rstd[:, 0:n],
                                                 ALU.mult, ALU.mult)
                        continue
                    if k % 2:
                        eng.drain()
                    elif k or g:
                        eng.wait_ge(hh_done, c.hh.value() + g * KD + k - 1)
                        eng.wait_ge(hl_even_done, c.hl_even.value() + (g * KD + k) // 2)
                    eng.scalar_tensor_tensor(hf[:, k % 2, 0:n], x[:, k, c0:c0 + n], pcol(gain, k), rstd[:, 0:n],
                                             ALU.mult, ALU.mult).then_inc(hf_done, 1)
                    if k and k % 2 == 0:
                        low_odd(g, k - 1, c0, n)
                if final:
                    eng.drain().then_inc(out_ready, 1)
                else:
                    low_odd(g, KD - 1, c0, n)
            if not final:
                c.hh.n += KD * len(grp)
                c.hl_even.n += KD // 2 * len(grp)
            skip(c.full, [4] * len(grp))

        def dve_add_columns(eng, c, n0, grp):
            for g, (c0, n) in enumerate(grp):
                for mt in range(2):
                    b = 2 * g + mt
                    bank_in(eng, c, b)
                    dst = x[:, n0 + mt, c0:c0 + n]
                    eng.tensor_tensor(dst, dst, banks[:, b, 0:n], ALU.add).then_inc(free_s[b], 1)
                    eng.drain().then_inc(x_summed, 1)

        def dve_add_rows(eng, c, grp):
            for g, (c0, n) in enumerate(grp):
                for d in range(KD):
                    b = 4 + d % 4
                    bank_in(eng, c, b)
                    dst = x[:, d, c0:c0 + n]
                    eng.tensor_tensor(dst, dst, banks[:, b, 0:n], ALU.add).then_inc(free_s[b], 1)
                    eng.drain().then_inc(x_summed, 1)

        def dve_stage_kv(eng, c):
            grp = ((0, MEM),)
            dve_norm(eng, c, grp, "g_mem")
            skip(c.full, [0, 1] * 8)

        def dve_stage_a(eng, c, p):
            grp, nt = groups(p), PASSES[p][1] - PASSES[p][0]
            dve_norm(eng, c, grp, "g_mix")
            eng.wait_ge(ws_hi_done, p + 1)
            eng.tensor_tensor(ws_lo[:].rearrange("p k c -> p (k c)"), ws[:],
                              ws_hi[:].rearrange("p k c -> p (k c)").bitcast(F32), ALU.subtract).then_inc(ws_lo_done, 1)
            skip(c.full, banks_of_columns(grp) * 9 + [i % 4 for i in range(nt)] * 2)
            for i in range(nt):
                bank_in(eng, c, i % 4)
                eng.tensor_copy(raw12[:, i, :], banks[:, i % 4, 0:N_SMALL]).then_inc(free_s[i % 4], 1)

        def dve_attend(eng, c, p, grp):
            nt = prompt_tiles(p)

            def row_max(i):
                bank_in(eng, c, 4 + i % 2)
                eng.tensor_reduce(soft[:, i % 2, 0:1], banks[:, 4 + i % 2, 0:MEM], AX_X, ALU.max)
                eng.drain()
                eng.tensor_scalar(soft[:, i % 2, 1:2], soft[:, i % 2, 0:1], -1.0, None, ALU.mult).then_inc(p_max, 1)

            def normalise(i):
                eng.wait_ge(p_exp, c.p_exp.next())
                eng.reciprocal(soft[:, i % 2, 3:4], soft[:, i % 2, 2:3])
                eng.drain()
                eng.tensor_scalar(pr[:, i % 2, :], pr[:, i % 2, :], soft[:, i % 2, 3:4], None, ALU.mult)
                eng.drain().then_inc(p_done, 1)

            for i in range(nt + 1):
                if i < nt:
                    row_max(i)
                if i > 0:
                    normalise(i - 1)
            skip(c.full, [6 + i % 2 for i in range(nt)])
            if p == len(PASSES) - 1:
                for b in range(4, 8):
                    bank_in(eng, c, b)
                s = banks[0:SEQ_LEN, 4:8, :].rearrange("p b (s m) -> p (b s) m", s=2)
                w = prs[0:SEQ_LEN]
                top, total, inv = (softs[0:SEQ_LEN, j, :] for j in range(3))
                eng.tensor_reduce(top, s, AX_X, ALU.max)
                eng.drain()
                eng.tensor_tensor(w, s, top.unsqueeze(2).to_broadcast([SEQ_LEN, SEQS, MEM]), ALU.subtract)
                for b in range(4, 8):
                    eng.drain().then_inc(free_s[b], 1)
                eng.drain().then_inc(p_max, 1)
                eng.wait_ge(p_exp, c.p_exp.next())
                eng.tensor_reduce(total, w, AX_X, ALU.add)
                eng.drain()
                eng.reciprocal(inv, total)
                eng.drain()
                eng.tensor_tensor(w, w, inv.unsqueeze(2).to_broadcast([SEQ_LEN, SEQS, MEM]), ALU.mult)
                eng.drain().then_inc(p_done, 1)
                skip(c.full, [4])

        def dve_stage_b(eng, c, p):
            grp = groups(p)
            for g, (c0, n) in enumerate(grp):
                for k in range(KD):
                    eng.wait_ge(hh_done, c.hh.next())
                    eng.tensor_tensor(hl[:, k, c0:c0 + n], x[:, k, c0:c0 + n], hh[:, k, c0:c0 + n].bitcast(F32),
                                      ALU.subtract).then_inc(hl_odd_done, 1)
            for g in range(2):
                eng.wait_ge(x_loaded[g], 16 * (1 - g + 2 * (p + 1)))
            for n in range(4):
                dve_add_columns(eng, c, 2 * n, grp)
            dve_norm(eng, c, grp, "g_cross")
            skip(c.full, banks_of_columns(grp))
            for h in range(HEADS):
                dve_attend(eng, c, p, grp)
                if h < HEADS - 1:
                    skip(c.full, banks_of_columns(grp))
                for g, (c0, n) in enumerate(grp):
                    eng.wait_ge(g_hi_done, c.g_hi.next())
                    for e in range(2):
                        b = 2 * g + e
                        bank_in(eng, c, b)
                        eng.tensor_tensor(g_lo[:, e, c0:c0 + n], banks[:, b, 0:n], g_hi[:, e, c0:c0 + n].bitcast(F32),
                                          ALU.subtract).then_inc(free_s[b], 1)
                    eng.drain().then_inc(g_lo_done, 1)
                dve_add_rows(eng, c, grp)
            dve_norm(eng, c, grp, "g_ffn")

            def times_up():
                skip(c.full, banks_of_columns(grp))
                for g, (c0, n) in enumerate(grp):
                    eng.wait_ge(gate_done, c.gate.next())
                    for mt in range(2):
                        b = 2 * g + mt
                        bank_in(eng, c, b)
                        dst = stage[0][:, mt, c0:c0 + n]
                        eng.tensor_tensor(dst, dst, banks[:, b, 0:n], ALU.mult).then_inc(free_s[b], 1)
                    eng.drain().then_inc(up_done, 1)

            times_up()
            with Loop(eng, ROUNDS - 1, [(x, 2) for x in c.full[0:4]] + [(x, 4) for x in c.full[4:8]] + [(c.gate, 2)]):
                dve_add_rows(eng, c, grp)
                times_up()
            dve_add_rows(eng, c, grp)
            c.g_hi.n += 2 * ROUNDS
            dve_norm(eng, c, grp, "g_final", final=True)

        def pool_norm(eng, c, grp, split_between=False):
            for g, (c0, n) in enumerate(grp):
                for k in range(0, KD, 2):
                    eng.wait_ge(hh_done, c.hh.next())
                    c.hh.next()
                    eng.tensor_tensor(hl[:, k, c0:c0 + n], hf[:, 0, 0:n], hh[:, k, c0:c0 + n].bitcast(F32),
                                      ALU.subtract).then_inc(hl_even_done, 1)
                if split_between and g == 0:
                    split_lo_a(eng, c, 1)

        def pool_stage_kv(eng, c):
            for s in range(2):
                split_lo_a(eng, c, s)
            pool_norm(eng, c, ((0, MEM),))
            for n in range(6):
                split_lo_a(eng, c, n % 2)

        def pool_stage_a(eng, c, p):
            split_lo_a(eng, c, 0)
            pool_norm(eng, c, groups(p), split_between=True)
            with Loop(eng, 4, [(x, 1) for x in c.a_hi]):
                for s in range(2):
                    split_lo_a(eng, c, s)
            split_lo_a(eng, c, 0)

        def pool_stage_b(eng, c, p):
            grp = groups(p)
            for s in range(2):
                split_lo_a(eng, c, s)
            c.hh.n += KD * len(grp)
            for n in range(4):
                split_lo_a(eng, c, n % 2)
            split_lo_b(eng, c)
            pool_norm(eng, c, grp)
            for h in range(HEADS):
                split_lo_a(eng, c, h % 2)
                split_lo_b(eng, c)
            pool_norm(eng, c, grp)
            c.g_hi.n += HEADS * len(grp)

            def up():
                for g, (c0, n) in enumerate(grp):
                    eng.wait_ge(g_hi_done, c.g_hi.next())
                    eng.tensor_tensor(g_lo[:, :, c0:c0 + n], stage[0][:, :, c0:c0 + n],
                                      g_hi[:, :, c0:c0 + n].bitcast(F32), ALU.subtract).then_inc(g_lo_done, 1)

            split_lo_a(eng, c, 0)
            up()
            split_lo_a(eng, c, 1)
            with Loop(eng, ROUNDS - 2, [(x, 1) for x in c.a_hi] + [(c.b_hi, 1), (c.g_hi, 2)]):
                split_lo_a(eng, c, 0)
                split_lo_b(eng, c)
                up()
                split_lo_a(eng, c, 1)
            split_lo_b(eng, c)
            up()

        def sp_stage_kv(eng, c):
            eng.dma_start(x[:, :, 0:MEM], t["mem_t"]).then_inc(x_loaded[0], 16)

            def store(n):
                slot = n % 2
                eng.wait_ge(stage_full[slot], c.stage[slot].next())
                c.stage_stored[slot].n += 1
                if n < 4:
                    dst = t["p_mem_kt"].rearrange("(t p) m -> p t m", p=P)[:, 2 * n:2 * n + 2, :]
                    eng.dma_start(dst, stage[slot][:, :, 0:MEM]).then_inc(stage_stored[slot], 16)
                else:
                    j = (n - 4) * 256
                    dst = t["p_mem_v"].rearrange("(t p) e -> p t e", p=P)[:, :, j:j + 256]
                    src = stage[slot][:].rearrange("p a b -> p (a b)")[:, 0:512].rearrange("p (t e) -> p t e", t=2)
                    eng.dma_start(dst, src).then_inc(stage_stored[slot], 16)

            for n in range(8):
                load_a(eng, c, n % 2, t["w_kv"][n])
                if n >= 3:
                    store(n - 3)
            for n in range(5, 8):
                store(n)
            for s in range(2):
                eng.wait_ge(stage_stored[s], c.stage_stored[s].value())

        def sp_stage_a(eng, c, p):
            t0, nt = PASSES[p][0] * P, PASSES[p][1] - PASSES[p][0]
            n = nt * P
            for g, (c0, gn) in enumerate(groups(p)):
                if p:
                    eng.wait_ge(out_stored[g], 16 * p)
                eng.dma_start(x[:, :, c0:c0 + gn], t["x_t"][:, :, t0 + c0:t0 + c0 + gn]).then_inc(x_loaded[g], 16)
                load_a(eng, c, g, t["w_in"][g])
            eng.dma_start(ws[:], t["w_small"]).then_inc(ws_loaded, 16)

            def store(i, slot, tokens=None):
                eng.wait_ge(stage_full[slot], c.stage[slot].next())
                c.stage_stored[slot].n += 1
                if tokens is None:
                    dst = u_dram[:, bass.ds(i * 2, 2), 3 + t0:3 + t0 + n]
                    src = stage[slot][:, :, 0:n]
                else:
                    dst = z_dram[t0:t0 + n, tokens * 256:tokens * 256 + 256].rearrange("(t p) c -> p t c", p=P)
                    src = stage[slot][:].rearrange("p a b -> p (a b)")[:, 0:nt * 256].rearrange("p (t c) -> p t c", t=nt)
                eng.dma_start(dst, src).then_inc(stage_stored[slot], 16)

            load_a(eng, c, 0, t["w_in"][2])
            with Loop(eng, 4, [(x, 1) for x in c.a_lo + c.stage + c.stage_stored]) as i:
                for s in range(2):
                    store(i * 2 + s, s)
                    load_a(eng, c, 1 - s, t["w_in"][bass.ds(i * 2 + (s + 3), 1)].rearrange("a p n -> p (a n)"))
            store(8, 0)
            store(None, 1, tokens=0)
            store(None, 0, tokens=1)
            for s in range(2):
                eng.wait_ge(stage_stored[s], c.stage_stored[s].value())

        def sp_stage_b(eng, c, p):
            t0, nt = PASSES[p][0] * P, PASSES[p][1] - PASSES[p][0]
            n = nt * P
            sample = p == len(PASSES) - 1
            eng.wait_ge(ms["y_out"], 1 + 16 * PASSES[p][1])
            for g, (c0, gn) in enumerate(groups(p)):
                eng.dma_start(x[:, :, c0:c0 + gn], y_dram[:, :, t0 + c0:t0 + c0 + gn]).then_inc(y_loaded[g], 16)
                load_a(eng, c, g, t["w_a"][g])
            eng.dma_start(ident[:], t["mixc"][:, MIX["ident"][0]:MIX["ident"][0] + P]).then_inc(ident_loaded, 16)
            norms_groups = 1 + 2 * (p + 1) + 2 * 2 * p
            for g, (c0, gn) in enumerate(groups(p)):
                eng.wait_ge(hl_odd_done, KD // 2 * norms_groups + 2 * KD * p + KD * (g + 1))
                eng.wait_ge(hh_done, KD * norms_groups + 2 * KD * p + KD * (g + 1))
                eng.dma_start(x[:, :, c0:c0 + gn], t["x_t"][:, :, t0 + c0:t0 + c0 + gn]).then_inc(x_loaded[g], 16)

            def load_kv(h):
                slot = h % 2
                if h >= 2:
                    eng.wait_ge(av_done, HEADS * p + h - 1)
                k = t["p_mem_kt"].rearrange("(h e p) m -> h p e m", h=HEADS, p=P)[h]
                v = t["p_mem_v"].rearrange("(t p) (h e) -> h p t e", p=P, h=HEADS)[h]
                eng.dma_start(kv[:, slot, 0, :].rearrange("p (e m) -> p e m", e=2), k).then_inc(kv_loaded[slot], 16)
                eng.dma_start(kv[:, slot, 1, :].rearrange("p (t e) -> p t e", t=2), v).then_inc(kv_loaded[slot], 16)

            for s in (2, 3, 4, 5):
                load_a(eng, c, s % 2, t["w_a"][s])
            for h in range(HEADS):
                load_kv(h)
                load_b(eng, c, t["w_b"][h])
                load_a(eng, c, h % 2, t["w_a"][6 + h])
                if sample:
                    for name in ("k_cache_t", "v_cache"):
                        for s in range(SEQS):
                            c.kvs_used[s % KVS].next()
                            eng.wait_ge(kvs_used[s % KVS], c.kvs_used[s % KVS].value(1))
                            eng.dma_start(kvs[:, s % KVS, :], t[name][h, s]).then_inc(kvs_loaded[s % KVS], 16)
            load_b(eng, c, t["w_b"][4])
            with Loop(eng, ROUNDS - 1, [(x, 1) for x in c.a_lo] + [(c.b_lo, 1)]) as i:
                for s in range(2):
                    load_a(eng, c, s, t["w_a"][bass.ds(i * 2 + (10 + s), 1)].rearrange("a p n -> p (a n)"))
                load_b(eng, c, t["w_b"][bass.ds(i + 5, 1)].rearrange("a p n -> p (a n)"))
            for g, (c0, gn) in enumerate(groups(p)):
                eng.wait_ge(out_ready, 2 * p + g + 1)
                eng.dma_start(t["y_t"][:, :, t0 + c0:t0 + c0 + gn], x[:, :, c0:c0 + gn]).then_inc(out_stored[g], 16)
            if sample:
                for g in range(2):
                    eng.wait_ge(out_stored[g], 16 * len(PASSES))

        per_chunk = dict(
            u_in=1, z_in=1, turned=3, turned_sb=4, kq=1, kq_dec=2, share=2, share_sb=2, tap0=3, conv=3, sz=1,
            bu=2, bu_sb=2, cs=2,
            lg=1, dec_g=1, dec_s=1, dec_x=2, dec_m=2, score=1,
            gates=1, th=1, n2=1, nr=1, scaled=1, ch=2, cht=2, ml=6, cur=1,
            rot_p=1, sc=1, ssdy=1, yo=1, xw=1, ssdst=1, xsd=2, la=1, lm=1, lsq=1, gg=1,
            xs5=1, s5yb=1, s5ys=1, gelu_gate=2, glu=1, uw=1, uw_sb=1, ws_b=1, delta=1, ob=1, gst=1,
            rot_z=1, rot_q=1, y3=1, ss=1, rs=1, gz=1, gsq=1, grs=1, ytm=2, ytr=2, ych=2, y_out=1, s5done=1,
            lruy=1, osum=1, sel=8, stp=8, x0=6, x1=6, y0=6, y1=6, tri_t=2, sx0=6, sx1=6, ss0=7, ss1=7, tri_t_sb=2)
        ms = {k: sem("m_" + k) for k in per_chunk}
        prep_in, tok_pe, tok_act, tok_dve = sem("prep_in"), sem("tok_pe"), sem("tok_act"), sem("tok_dve")
        sample_in = sem("sample_in")
        SAMPLE_LOADS = U_TILES + 5
        SAMPLE_ONLY = ("sel", "stp", "share", "share_sb", "osum")
        finals_stored = sem("finals_stored")

        def v3(ap, a):
            return ap.rearrange("p (a b) -> p a b", a=a)

        def mc(name, j=0, w=None):
            o, n = MIX[name]
            return mixc[:, o + j:o + j + (n if w is None else w)]

        class Chunk:

            def __init__(self, eng, base, i, sample):
                self.eng, self.base, self.i, self.sample = eng, base, i, sample
                self.seqs, self.len = (SEQS, SEQ_LEN) if sample else (1, P)

            def need(self, name, k=1):
                if self.sample and name == "u_in":
                    self.eng.wait_ge(sample_in, 16 * SAMPLE_LOADS)
                    return
                n, unit = per_chunk[name], 16 if name in ("u_in", "z_in", "y_out") else 1
                v = (k if name in SAMPLE_ONLY else self.base * n + k) * unit
                if name in ("y_out", "gg", "xsd", "ych"):
                    v += 1
                self.eng.wait_ge(ms[name], v if self.i is None else self.i * (n * unit) + v)

            def first_token(self):
                return PROMPT if self.sample else self.i * P + self.base * P

            def window(self, tile, j=3):
                w = self.len + 3
                return u_buf[:, tile, 0:self.seqs * w].rearrange("p (s w) -> p s w", w=w)[:, :, j:j + self.len]

            def by_seq(self, ap):
                return v3(ap, self.seqs)

        u_buf = m["u"][:].rearrange("p (t w) -> p t w", t=U_TILES)
        cv = v3(m["cv"][:], N_CONV)
        cur = m["cur"]
        dec, lg = v3(m["dec"][:], 8), v3(m["lg"][:], 8)
        chT = v3(m["chT"][:], 8)
        bre, bim, p1, p2, p3, p4 = (m[k] for k in ("bre", "bim", "p1", "p2", "p3", "p4"))
        ych = v3(m["ych"][:], 8)

        def tri(pair, transposed, h):
            o = pair * 512 + transposed * 256 + h * P
            return m["ST"][:, o:o + P]

        levels_of = lambda sample: 3 if sample else 6
        GROUPS = ((8, 14), (2, 8), (0, 2))

        def heads(ap, n=4):
            return v3(ap, n)

        def per_head(ap, n, w=64):
            return ap.unsqueeze(2).to_broadcast([P, n, w])

        def pe_tokens_scalars(eng, c, p):
            npr = prompt_tiles(p)
            eng.wait_ge(tok_dve, 2 * p + 2)
            g = m["tmp8"][:, 0:npr * 8]
            eng.matmul(banks[:, 0, 0:npr * 8], mc("U"), g, start=True, stop=True)
            eng.matmul(banks[:, 0, 64:64 + npr * 8], mc("L"), g, start=True, stop=True)
            last = eng.matmul(banks[:, 0, 128:128 + npr * 8], mc("ones"), g, start=True, stop=True)
            if p == len(PASSES) - 1:
                g = m["tmp8"][:, npr * 8:npr * 8 + 8]
                eng.matmul(banks[:, 1, 0:8], mc("Us"), g, start=True, stop=True)
                eng.matmul(banks[:, 1, 8:16], mc("Ls"), g, start=True, stop=True)
                last = eng.matmul(banks[:, 1, 64:128], mc("ones"), m["tmp8"][:, 64:128], start=True, stop=True)
            last.then_inc(tok_pe, 1)

        def pe_chunk(eng, k):
            s_ = k.sample

            k.need("u_in")
            for part in range(2):
                for s in range(8):
                    b = 3 + 2 * part + s // 4
                    last = eng.matmul(k.by_seq(banks[:, b, s % 4 * P:s % 4 * P + P]), mprep[:, part, s, :],
                                      k.window(DU + s // 4), start=True, stop=True)
                last.then_inc(ms["bu"], 1)

            def turn(bank, col, tiles):
                for j, src in enumerate(tiles):
                    last = eng.transpose(banks[:, bank, col + j * P:col + j * P + P], src, mc("ident"))
                return last

            k.need("cs", 1)
            k.need("ych", 0)
            turn(1, 0, [cv[:, j, :] for j in (8, 9, 10, 11)]).then_inc(ms["turned"], 1)
            turn(2, 0, [cv[:, j, :] for j in (12, 13)]).then_inc(ms["turned"], 1)
            k.need("lg")
            k.need("bu_sb", 1)
            for h in range(8):
                b = 3 if h < 4 else 4
                last = eng.matmul(banks[:, b, h % 4 * P:h % 4 * P + P], lg[:, h, :], mc("Us" if s_ else "U"),
                                  start=True, stop=True)
                if h % 4 == 3:
                    last.then_inc(ms["dec_s" if h < 4 else "dec_g"], 1)
            k.need("cs", 2)
            turn(0, 0, [cv[:, j, :] for j in (2, 3, 4, 5)]).then_inc(ms["turned"], 1)
            k.need("turned_sb", 3)
            for g in range(2):
                last = eng.matmul(banks[:, 2, 256 + g * P:256 + g * P + P], cv[:, 4 + g, :], cv[:, 6 + g, :],
                                  start=True, stop=True)
            last.then_inc(ms["score"], 1)
            k.need("conv", 3)
            for w, name in enumerate(("w_r", "w_i")):
                for j in range(2):
                    last = eng.matmul(banks[:, 7, (2 * w + j) * P:(2 * w + j + 1) * P], mc(name, j * P, P), cv[:, j, :],
                                      start=True, stop=True)
            last.then_inc(ms["gates"], 1)
            k.need("scaled")
            k.need("turned_sb", 4)
            qkn = m["qkn"]
            turn(0, 0, [qkn[:, j * P:j * P + P] for j in range(4)]).then_inc(ms["ch"], 1)
            turn(1, 0, [m["kb"][:, 0:P], m["kb"][:, P:256], m["qd"][:, 0:P], m["qd"][:, P:256]]).then_inc(ms["ch"], 1)
            k.need("cht", 2)
            for o, right in ((0, 4), (2, 0)):
                for h in range(4):
                    r = slice(h % 2 * 64, h % 2 * 64 + 64)
                    j = (o + h // 2) * P
                    eng.matmul(banks[:, 5 + h % 2, j:j + P], chT[r, 2 + h // 2, :], chT[r, right + h // 2, :],
                               start=True, stop=True)
            eng.drain().then_inc(ms["kq"], 1)
            k.need("sc")
            k.need("th")
            for h in range(4):
                last = eng.matmul(banks[:, 7, h * 64:h * 64 + 64], m["sc"][:, h * P:h * P + P],
                                  m["xdt"][:, h * 64:h * 64 + 64], start=True, stop=True)
            if s_:
                for g in range(2):
                    for s in range(SEQS):
                        cols = slice(s * SEQ_LEN, (s + 1) * SEQ_LEN)
                        last = eng.matmul(banks[:, 7, 256 + g * P + s * SEQ_LEN:256 + g * P + (s + 1) * SEQ_LEN],
                                          ssd_hs[:, s, g * P:g * P + P], cv[:, 6 + g, cols], start=True, stop=True)
            else:
                for g in range(2):
                    last = eng.matmul(banks[:, 7, 256 + g * P:256 + g * P + P], cv[:, 6 + g, :],
                                      ssd_h[:, g * P:g * P + P], start=True, stop=True)
            last.then_inc(ms["ssdy"], 1)
            top = levels_of(s_)
            k.need("sc")
            k.need("turned_sb", 3)
            for pr_ in range(2):
                k.need(f"ss{pr_}", 1)
                for h in range(2):
                    last = eng.transpose(banks[:, (0, 2)[pr_], 256 + h * P:256 + h * P + P], tri(pr_, 0, h), mc("ident"))
                last.then_inc(ms["tri_t"], 1)
            for lv in range(top):
                for pr_ in range(2):
                    bx = (0, 2)[pr_]
                    if lv == 0:
                        k.need("tri_t_sb", pr_ + 1)
                    else:
                        k.need(f"ss{pr_}", lv + 1)
                    k.need("ml", lv + 1)
                    for h in range(2):
                        o = (2 * pr_ + h) * P
                        last = eng.matmul(banks[:, bx, h * P:h * P + P],
                                          m["ML"][:, (lv + 1) * 512 + o:(lv + 1) * 512 + o + P],
                                          tri(pr_, 1, h), start=True, stop=True)
                    last.then_inc(ms[f"x{pr_}"], 1)
                for pr_ in range(2):
                    by = (1, 3)[pr_]
                    k.need(f"sx{pr_}", lv + 1)
                    if lv == 0 and pr_ == 1:
                        k.need("dec_x", 2)
                    for h in range(2):
                        X = m["X"][:, (2 * pr_ + h) * P:(2 * pr_ + h + 1) * P]
                        last = eng.matmul(banks[:, by, h * P:h * P + P], X, tri(pr_, 0, h), start=True, stop=True)
                        if lv < top - 1:
                            last = eng.matmul(banks[:, by, 256 + h * P:256 + h * P + P], tri(pr_, 0, h), X,
                                              start=True, stop=True)
                    last.then_inc(ms[f"y{pr_}"], 1)
                if lv == 1 and not s_:
                    k.need("kq_dec", 2)
                    k.need("xw")
                    for g in range(2):
                        last = eng.matmul(banks[:, 6, g * P:g * P + P], m["tok_x"][:, 256 + g * P:256 + g * P + P],
                                          m["xw"][:, g * P:g * P + P], start=True, stop=True)
                    last.then_inc(ms["ssdst"], 1)
            if s_:
                k.need("share_sb", 1)
                turn(6, 0, [m["yo"][:, 0:P], m["yo"][:, P:256]]).then_inc(ms["share"], 1)

            def s5_out(j):
                for n in range(8):
                    s, part = 4 * j + n // 2, n % 2
                    src = (p1, p3)[part]
                    last = eng.matmul(banks[:, 4, j * P:j * P + P], mc(("ct_re", "ct_im")[part], s * P, P),
                                      src[:, s * P:s * P + P], start=n == 0, stop=n == 7)
                return last

            k.need("kq_dec", 1)
            k.need("ss0", top + 1)
            k.need("ss1", top + 1)
            for h in range(4):
                S = tri(h // 2, 0, h % 2)
                eng.matmul(banks[:, 5, h * 64:h * 64 + 64], S, m["vb"][:, h * 64:h * 64 + 64], start=True, stop=True)
            for h in range(4):
                r = slice(h % 2 * 64, h % 2 * 64 + 64)
                last = eng.matmul(banks[r, 5, 256 + h // 2 * P:256 + h // 2 * P + P], m["wk"][:, h * 64:h * 64 + 64],
                                  tri(h // 2, 0, h % 2), start=True, stop=True)
            last.then_inc(ms["uw"], 1)
            wT, delta = m["wT"], m["delta"]
            k.need("xs5")
            k.need("dec_x", 2)
            s5_out(0)
            k.need("uw_sb")
            if s_:
                s5_out(1).then_inc(ms["s5yb"], 1)
                pe_gdn_sample(eng, k)
                return
            for j in range(2):
                last = eng.matmul(banks[:, 3, 256 + j * P:256 + j * P + P], wT[:, j * P:j * P + P], gdn_s[:, j, :],
                                  start=True, stop=True)
            last.then_inc(ms["ws_b"], 1)
            s5_out(1).then_inc(ms["s5yb"], 1)
            k.need("delta")
            for j in range(2):
                eng.matmul(banks[:, 6, 256 + j * P:256 + j * P + P], chT[:, 6 + j, :], gdn_s[:, j, :],
                           start=True, stop=False, skip_group_check=True)
                for h in (2 * j, 2 * j + 1):
                    last = eng.matmul(banks[:, 6, 256 + h * 64:256 + h * 64 + 64], m["qkd"][:, h * P:h * P + P],
                                      delta[:, h * 64:h * 64 + 64], start=False, stop=h == 2 * j + 1, skip_group_check=True)
            last.then_inc(ms["ob"], 1)
            k.need("yo")
            k.need("y3")
            for j in range(2):
                last = eng.matmul(banks[:, 7, j * P:j * P + P], m["kd"][:, j * P:j * P + P], delta[:, j * P:j * P + P],
                                  start=True, stop=True)
            last.then_inc(ms["gst"], 1)
            pe_glu(eng, k)
            pe_chunk_end(eng, k)

        def pe_gdn_sample(eng, k):
            for j in range(2):
                for s in range(SEQS):
                    cols = slice(j * P + s * SEQ_LEN, j * P + (s + 1) * SEQ_LEN)
                    out = slice(256 + cols.start, 256 + cols.stop)
                    eng.matmul(banks[:, 3, out], gdn_ss[:, s, j, :], m["wT"][:, cols], start=True, stop=True)
                    last = eng.matmul(banks[:, 6, out], gdn_ss[:, s, j, :],
                                      chT[:, 6 + j, s * SEQ_LEN:(s + 1) * SEQ_LEN], start=True, stop=True)
            last.then_inc(ms["share"], 1)
            k.need("share_sb", 2)
            for j in range(4):
                last = eng.transpose(banks[:, 0, j * P:j * P + P], m["X"][:, j * P:j * P + P], mc("ident"))
            last.then_inc(ms["ws_b"], 1)
            k.need("delta")
            for h in range(4):
                last = eng.matmul(banks[:, 6, 256 + h * 64:256 + h * 64 + 64], m["qkd"][:, h * P:h * P + P],
                                  m["delta"][:, h * 64:h * 64 + 64], start=True, stop=True)
            last.then_inc(ms["ob"], 1)
            pe_glu(eng, k)
            k.need("yo")
            k.need("y3")
            for s in range(SEQS):
                k.need("sel", s + 1)
                for j in range(2):
                    eng.matmul(banks[:, 7, j * P:j * P + P], m["kb"][:, j * P:j * P + P],
                               m["delta"][:, j * P:j * P + P], start=True, stop=True)
                for g in range(2):
                    last = eng.matmul(banks[:, 7, 256 + g * P:256 + g * P + P],
                                      m["tok_x"][:, 256 + g * P:256 + g * P + P], m["qd"][:, g * P:g * P + P],
                                      start=True, stop=True)
                last.then_inc(ms["stp"], 1)
            pe_chunk_end(eng, k)

        def pe_glu(eng, k):
            k.need("gelu_gate", 1)
            for d in range(2):
                for j in range(2):
                    last = eng.matmul(banks[:, 4, 256 + d * P:256 + d * P + P], mc("glu", j * 256 + d * P, P),
                                      m["s5t"][:, j * P:j * P + P], start=j == 0, stop=j == 1)
            last.then_inc(ms["glu"], 1)

        def pe_chunk_end(eng, k):
            k.need("gelu_gate", 2)
            for n in range(2):
                k.need("ytm", n + 1)
                for j in range(2):
                    last = eng.transpose(banks[:, n, j * P:j * P + P], m["ytm"][:, (2 * n + j) * P:(2 * n + j + 1) * P],
                                         mc("ident"))
                last.then_inc(ms["ytr"], 1)

        def pe_stage_m(eng, c, p):
            eng.wait_ge(prep_in, 32 * (p + 1))
            pe_tokens_scalars(eng, c, p)
            chunks(eng, c, p, pe_chunk)

        def chunks(eng, c, p, body, loads=False):
            first, n = PASSES[p][0], prompt_tiles(p)
            if loads:
                c.pass_by()
            else:
                eng.wait_ge(prep_in, 32 * (p + 1))
                c.meet()
            with Loop(eng, n, []) as i:
                body(eng, Chunk(eng, first, i, False))
            if p == len(PASSES) - 1:
                c.meet()
                body(eng, Chunk(eng, TILES - 1, None, True))
                c.meet()

        def act_chunk(eng, k):
            s_ = k.sample
            top = levels_of(s_)
            for part, dst in enumerate((bre, bim)):
                k.need("bu", part + 1)
                src = banks[:, 3 + 2 * part:5 + 2 * part, :].rearrange("p b c -> p (b c)")
                eng.activation(dst[:], src, ACT.Copy).then_inc(ms["bu_sb"], 1)
            k.need("conv", 1)
            eng.activation(cv[:, 8:14, :], cv[:, 8:14, :], ACT.Silu).then_inc(ms["cs"], 1)
            k.need("turned", 1)
            eng.activation(m["tok_qk"][:], banks[:, 1, :], ACT.Copy).then_inc(ms["turned_sb"], 1)
            eng.activation(m["sqk"][:], banks[:, 1, :], ACT.Square).then_inc(ms["turned_sb"], 1)
            k.need("turned", 2)
            eng.activation(m["tok_v"][:], banks[:, 2, 0:256], ACT.Copy).then_inc(ms["turned_sb"], 1)
            k.need("z_in")
            eng.activation(m["sz"][:], m["z"][:], ACT.Silu).then_inc(ms["sz"], 1)
            k.need("conv", 2)
            eng.activation(cv[:, 2:8, :], cv[:, 2:8, :], ACT.Silu).then_inc(ms["cs"], 1)
            k.need("n2")
            eng.activation(m["n8"][:, 0:8], m["n8"][:, 0:8], ACT.Sqrt, bias=eps[:]).then_inc(ms["nr"], 1)
            for b, name, o in ((4, "dec_g", 4), (3, "dec_s", 0)):
                k.need(name)
                eng.activation(dec[:, o:o + 4, :].rearrange("p h t -> p (h t)"), banks[:, b, :],
                               ACT.Exp).then_inc(ms["dec_x"], 1)
            k.need("turned", 3)
            eng.activation(m["tok_x"][:], banks[:, 0, :], ACT.Copy).then_inc(ms["turned_sb"], 1)
            for b in range(2):
                k.need("ch", b + 1)
                eng.activation(chT[:, 4 * b:4 * b + 4, :].rearrange("p a t -> p (a t)"), banks[:, b, :],
                               ACT.Copy).then_inc(ms["cht"], 1)
            for j in range(2):
                eng.activation(k.by_seq(m["gg"][:, j * P:j * P + P]), k.window(GATE + j), ACT.Gelu_apprx_tanh)
            k.need("gates")
            for j in range(4):
                eng.activation(m["th"][:, j * P:j * P + P], banks[:, 7, j * P:j * P + P], ACT.Tanh,
                               bias=half_b[:, j:j + 1], scale=0.5)
            eng.drain().then_inc(ms["th"], 1)
            eng.drain().then_inc(ms["gg"], 1)
            for j in range(2):
                th = m["th"][:, j * P:j * P + P]
                for dst, o, f in ((m["la"], 0, ACT.Exp), (m["lt"], 2, ACT.Tanh)):
                    eng.activation(dst[:, j * P:j * P + P], th, f, bias=lru_c[:, o + j:o + j + 1],
                                   scale=lru_c[:, o + j:o + j + 1])
            eng.drain().then_inc(ms["la"], 1)

            def yo():
                if s_:
                    k.need("share", 1)
                else:
                    k.need("ssdy")
                b, o = (6, 0) if s_ else (7, 256)
                for h in range(4):
                    eng.activation(m["yo"][:, h * 64:h * 64 + 64], banks[:, b, o + h * 64:o + h * 64 + 64], ACT.Copy,
                                   scale=cur[:, EGC + h:EGC + h + 1])
                eng.drain().then_inc(ms["yo"], 1)

            for pr_, b in ((0, 0), (1, 2)):
                k.need("tri_t", pr_ + 1)
                eng.activation(m["ST"][:, pr_ * 512 + 256:pr_ * 512 + 512], banks[:, b, 256:512],
                               ACT.Copy).then_inc(ms["tri_t_sb"], 1)
            for lv in range(top):
                for pr_, b in ((0, 0), (1, 2)):
                    k.need(f"x{pr_}", lv + 1)
                    eng.activation(m["X"][:, pr_ * 256:pr_ * 256 + 256], banks[:, b, 0:256],
                                   ACT.Copy).then_inc(ms[f"sx{pr_}"], 1)
                if lv == 0:
                    if s_:
                        k.need("ssdy")
                        eng.activation(m["yo"][:], banks[:, 7, 256:512], ACT.Copy).then_inc(ms["share_sb"], 1)
                    else:
                        yo()
                if lv == 1:
                    k.need("lm")
                    eng.activation(m["lb"][:], m["lb"][:], ACT.Sqrt, scale=0.25).then_inc(ms["lsq"], 1)
            if s_:
                yo()
            k.need("uw")
            eng.activation(m["wT"][:], banks[:, 5, 256:512], ACT.Copy)
            eng.activation(m["uu"][:], banks[:, 5, 0:256], ACT.Copy)
            eng.drain().then_inc(ms["uw_sb"], 1)
            k.need("y3")
            for g in range(2):
                eng.activation(m["sqk"][:, g * P:g * P + P], m["ys"][:, g * P:g * P + P], ACT.Square,
                               accum_out=m["n8"][:, g:g + 1])
            eng.drain()
            eng.activation(m["n8"][:, 0:2], m["n8"][:, 0:2], ACT.Sqrt, bias=eps[:], scale=1.0 / P).then_inc(ms["rs"], 1)
            if s_:
                k.need("share", 2)
                eng.activation(m["X"][:, 0:256], banks[:, 3, 256:512], ACT.Copy)
                eng.activation(m["X"][:, 256:512], banks[:, 6, 256:512], ACT.Copy)
                eng.drain().then_inc(ms["share_sb"], 1)
            k.need("s5ys")
            eng.activation(m["s5t"][:], m["s5y"][:], ACT.Gelu_apprx_tanh).then_inc(ms["gelu_gate"], 1)
            k.need("osum" if s_ else "ob")
            o = m["uu"][:] if s_ else banks[:, 6, 256:512]
            eng.activation(m["sqk"][:, 0:256], o, ACT.Square).then_inc(ms["gsq"], 1)
            k.need("glu")
            for d in range(2):
                eng.activation(m["sqk"][:, 256 + d * P:256 + d * P + P], banks[:, 4, 256 + d * P:256 + d * P + P],
                               ACT.Tanh, bias=half_b[:, 4 + d:5 + d], scale=0.5)
            eng.drain().then_inc(ms["gelu_gate"], 1)
            k.need("ss")
            eng.activation(m["n8"][:, 8:12], m["n8"][:, 8:12], ACT.Sqrt, bias=eps[:], scale=1.0 / 64).then_inc(ms["grs"], 1)
            k.need("y_out", 0)
            for n in range(2):
                k.need("ytr", n + 1)
                eng.activation(ych[:, 2 + 2 * n:4 + 2 * n, :], v3(banks[:, n, 0:256], 2), ACT.Copy).then_inc(ms["ych"], 1)
            k.need("lruy")
            k.need("s5done")
            k.need("ych", 2)
            eng.dma_start(y_dram[:, :, bass.ds(k.first_token(), P)], ych).then_inc(ms["y_out"], 16)

        def act_stage_m(eng, c, p):
            n, npr = PASSES[p][1] - PASSES[p][0], prompt_tiles(p)
            eng.wait_ge(tok_dve, 2 * p + 1)
            tk = m["tk"]
            eng.activation(tk[:, 2 * 64:2 * 64 + n * 8], tk[:, 64:64 + n * 8], ACT.Exp)
            eng.activation(v3(tk[:, 4 * 64:4 * 64 + n * 4], n), raw12[:, 0:n, 8:12], ACT.Tanh, scale=0.5)
            eng.drain().then_inc(tok_act, 1)
            eng.wait_ge(tok_pe, p + 1)
            for o, col in ((EGC, 0), (EGE, 64), (ETOT, 128)):
                eng.activation(tsc[:, 0:npr, o:o + 8], v3(banks[:, 0, col:col + npr * 8], npr), ACT.Exp)
            if npr < n:
                eng.activation(tsc[:, npr, EGC:EGC + 16], banks[:, 1, 0:16], ACT.Exp)
                eng.activation(m["etotb"][:], banks[:, 1, 64:128], ACT.Exp)
            chunks(eng, c, p, act_chunk)

        def dve_tokens_scalars(eng, p):
            n, npr = PASSES[p][1] - PASSES[p][0], prompt_tiles(p)
            w = n * 8
            tk = m["tk"]
            x8, na, e, sp, th, z, z2, acc = (tk[:, j * 64:j * 64 + w] for j in range(8))
            th = tk[:, 4 * 64:4 * 64 + n * 4]
            eng.tensor_tensor(v3(x8, n), raw12[:, 0:n, 0:8], pcol("bias8", 0, 8).unsqueeze(1).to_broadcast([P, n, 8]), ALU.add)
            eng.drain()
            eng.scalar_tensor_tensor(na, x8, -1.0, x8, ALU.mult, ALU.min)
            eng.drain().then_inc(tok_dve, 1)
            eng.wait_ge(tok_act, p + 1)
            eng.tensor_scalar(z, e, 2.0, None, ALU.add)
            eng.drain()
            eng.reciprocal(z, z)
            eng.drain()
            eng.tensor_tensor(z, z, e, ALU.mult)
            eng.drain()
            eng.tensor_tensor(z2, z, z, ALU.mult)
            artanh(eng, acc, z2)
            eng.drain()
            eng.tensor_tensor(acc, acc, z, ALU.mult)
            eng.drain()
            eng.tensor_scalar(acc, acc, 2.0, None, ALU.mult)
            eng.drain()
            eng.scalar_tensor_tensor(sp, x8, 0.0, acc, ALU.max, ALU.add)
            eng.drain()
            sp3 = v3(sp, n)
            eng.tensor_tensor(tsc[:, 0:n, G8:G8 + 8], sp3, nea8[:].unsqueeze(1).to_broadcast([P, n, 8]), ALU.mult)
            eng.tensor_tensor(v3(m["tmp8"][:, 0:w], n), sp3, nea8[:].unsqueeze(1).to_broadcast([P, n, 8]), ALU.mult)
            eng.tensor_copy(tsc[:, 0:n, DT:DT + 4], sp3[:, :, 0:4])
            eng.tensor_scalar(tsc[:, 0:n, BETA:BETA + 4], v3(th, n), 0.5, 0.5, ALU.mult, ALU.add)
            if npr < n:
                eng.wait_ge(prep_in, 32 * (p + 1))
                eng.drain()
                g = m["tmp8"][:, npr * 8:npr * 8 + 8]
                eng.tensor_tensor(v3(m["tmp8"][:, 64:128], SEQS), mc("seqsel").unsqueeze(2).to_broadcast([P, SEQS, 8]),
                                  g.unsqueeze(1).to_broadcast([P, SEQS, 8]), ALU.mult)
            eng.drain().then_inc(tok_dve, 1)

        def artanh(eng, acc, z2):
            eng.memset(acc, 1.0 / 17)
            for d in (15, 13, 11, 9, 7, 5, 3, 1):
                eng.drain()
                eng.tensor_tensor(acc, acc, z2, ALU.mult)
                eng.drain()
                eng.tensor_scalar(acc, acc, 1.0 / d, None, ALU.add)

        def v4(k, ap):
            return ap.rearrange("p (t s l) -> p t s l", t=8, s=k.seqs)

        def rotation(k, part):
            tab = mprep[:, 2 + part, :, 0:k.len]
            return tab.unsqueeze(2).to_broadcast([P, 8, k.seqs, k.len])

        def dve_chunk(eng, k):
            s_, top = k.sample, levels_of(k.sample)
            tt, stt = eng.tensor_tensor, eng.scalar_tensor_tensor
            s5_state = s5_xs if s_ else s5_x[:].unsqueeze(3)
            decay5, c5 = m["decay5"], m["c5"]
            tile_in_pass = TILES - 1 - PASSES[-1][0] if s_ else k.i
            eng.tensor_copy(cur[:], tsc[:, bass.ds(tile_in_pass, 1), :].rearrange("p a c -> p (a c)")).then_inc(ms["cur"], 1)
            k.need("u_in")

            def conv(n):
                k.need("tap0", n + 1)
                for tap in (1, 2, 3):
                    for j in range(*GROUPS[n]):
                        out = k.by_seq(cv[:, j, :])
                        last = stt(out, k.window(CONV + j, tap), pcol("conv_w", tap * N_CONV + j), out, ALU.mult, ALU.add)
                    if tap < 3:
                        eng.drain()
                last.then_inc(ms["conv"], 1)

            conv(0)
            conv(1)
            conv(2)
            k.need("turned_sb", 2)
            eng.tensor_reduce(m["n8"][:, 0:8], v3(m["sqk"][:], 8), AX_X, ALU.add).then_inc(ms["n2"], 1)
            k.need("bu_sb", 2)
            tt(v4(k, p1[:]), v4(k, bre[:]), rotation(k, 0), ALU.mult)
            tt(v4(k, p3[:]), v4(k, bim[:]), rotation(k, 0), ALU.mult)
            for part in range(2):
                tt(v3(c5[:, part * 64:part * 64 + 8 * k.seqs], 8), s5_state[:, part],
                   mag[:].unsqueeze(2).to_broadcast([P, 8, k.seqs]), ALU.mult)
            k.need("nr")
            eng.reciprocal(m["n8"][:, 0:8], m["n8"][:, 0:8])
            eng.drain()
            eng.tensor_scalar(m["n8"][:, 0:4], m["n8"][:, 0:4], 0.125, None, ALU.mult)
            eng.drain()
            k.need("turned_sb", 1)
            k.need("turned_sb", 3)
            qkn = m["qkn"]
            tt(v3(qkn[:], 8), v3(m["tok_qk"][:], 8), per_head(m["n8"][:, 0:8], 8), ALU.mult)
            beta, egc = cur[:, BETA:BETA + 4], cur[:, EGC + 4:EGC + 8]
            eng.drain()
            tt(heads(m["kb"][:]), heads(qkn[:, 256:512]), per_head(beta, 4), ALU.mult)
            tt(heads(m["qd"][:]), heads(qkn[:, 0:256]), per_head(egc, 4), ALU.mult)
            eng.drain().then_inc(ms["scaled"], 1)
            tt(heads(m["vb"][:]), heads(m["tok_v"][:]), per_head(beta, 4), ALU.mult)
            tt(heads(m["kd"][:]), heads(qkn[:, 256:512]), per_head(cur[:, EGE + 4:EGE + 8], 4), ALU.mult)
            tt(heads(m["wk"][:]), heads(m["kb"][:]), per_head(egc, 4), ALU.mult)
            k.need("rot_p")
            tt(p1[:], p1[:], p2[:], ALU.add)
            tt(p3[:], p3[:], p4[:], ALU.subtract)
            if s_:
                eng.memset(v4(k, decay5[:])[:, :, :, 0:1], 0.0)
            eng.drain()
            for part, src in enumerate((p1, p3)):
                first = v4(k, src[:])[:, :, :, 0]
                tt(first, first, v3(c5[:, part * 64:part * 64 + 8 * k.seqs], 8), ALU.add)
            k.need("turned_sb", 4)
            tt(heads(m["xdt"][:]), heads(m["tok_x"][:, 0:256]), per_head(cur[:, DT:DT + 4], 4), ALU.mult)
            k.need("dec_m", 2)
            k.need("score")
            for g in range(2):
                tt(v3(m["sc"][:, g * 256:g * 256 + 256], 2), dec[:, 2 * g:2 * g + 2, :],
                   banks[:, 2, 256 + g * P:256 + g * P + P].unsqueeze(1).to_broadcast([P, 2, P]), ALU.mult)
            eng.drain().then_inc(ms["sc"], 1)
            k.need("kq")

            def by_pair(ap):
                return ap.rearrange("p (j h t) -> p j h t", j=2, h=2)

            kq = banks[:, 5:7, :].rearrange("p h (w j t) -> p w j h t", w=2, j=2)
            tt(by_pair(m["MT"][:]), kq[:, 0], by_pair(m["decs"][:]), ALU.mult).then_inc(ms["kq_dec"], 1)
            tt(by_pair(m["qkd"][:]), kq[:, 1], dec[:, 4:8, :].rearrange("p (j h) t -> p j h t", j=2),
               ALU.mult).then_inc(ms["kq_dec"], 1)
            eng.drain()
            lm = mc("levels", 0, P).unsqueeze(1).to_broadcast([P, 4, P])
            tt(v3(m["ML"][:, 0:512], 4), v3(m["MT"][:], 4), lm, ALU.mult)
            eng.drain()
            for pr_ in range(2):
                o = slice(pr_ * 256, pr_ * 256 + 256)
                tt(v3(m["ST"][:, pr_ * 512:pr_ * 512 + 256], 2), mc("ident").unsqueeze(1).to_broadcast([P, 2, P]), v3(m["ML"][:, o], 2),
                   ALU.subtract).then_inc(ms[f"ss{pr_}"], 1)
            tt(heads(m["xw"][:]), heads(m["xdt"][:]), per_head(cur[:, EGE:EGE + 4], 4), ALU.mult).then_inc(ms["xw"], 1)
            k.need("la")
            tt(m["lb"][:], m["la"][:], m["la"][:], ALU.mult)
            eng.drain()
            stt(m["lb"][:], m["lb"][:], 1.0, m["lt"][:], ALU.add, ALU.mult).then_inc(ms["lm"], 1)

            def ssd_y():
                k.need("ssdy")
                k.need("yo")
                k.need("xsd")
                k.need("sz")
                ys = m["ys"][:]
                tt(ys, banks[:, 7, 0:256], m["yo"][:], ALU.add)
                eng.drain()
                tt(ys, ys, m["xsd"][:], ALU.add)
                eng.drain()
                tt(ys, ys, m["sz"][:, 0:256], ALU.mult).then_inc(ms["y3"], 1)

            def s5_forward(part):
                if part == 0:
                    k.need("rot_q")
                    tt(p1[:], p1[:], p2[:], ALU.subtract)
                    return
                tt(p3[:], p3[:], p4[:], ALU.add)
                eng.drain().then_inc(ms["xs5"], 1)
                for part, src in enumerate((p1, p3)):
                    eng.tensor_copy(s5_state[:, part], v4(k, src[:])[:, :, :, k.len - 1])

            for lv in range(top):
                if lv == 0:
                    eng.drain()
                    stt(m["lt"][:], m["th"][:, 256:512], 1.0, cv[:, 0:2, :].rearrange("p a t -> p (a t)"), ALU.add, ALU.mult)
                    for part, src, dst in ((0, p1, bre), (1, p3, bim)):
                        eng.tensor_tensor_scan(dst[:], decay5[:], src[:], 0.0, ALU.mult, ALU.add)
                    eng.drain().then_inc(ms["rot_z"], 1)
                if lv == 1:
                    tt(v4(k, p1[:]), v4(k, bre[:]), rotation(k, 0), ALU.mult)
                    tt(v4(k, p3[:]), v4(k, bim[:]), rotation(k, 0), ALU.mult)
                if lv == 2:
                    eng.drain()
                    k.need("lsq")
                    tt(m["lt"][:], m["lt"][:], m["lb"][:], ALU.mult)
                    eng.drain()
                    for j in range(2):
                        for s in range(k.seqs):
                            w = slice(j * P + s * k.len, j * P + (s + 1) * k.len)
                            first = lru_hs[:, j, s:s + 1] if s_ else lru_h[:, j:j + 1]
                            eng.tensor_tensor_scan(m["hs"][:, w], m["la"][:, w], m["lt"][:, w], first, ALU.mult, ALU.add)
                    eng.drain()
                    dst = lru_hs if s_ else lru_h[:].unsqueeze(2)
                    eng.tensor_copy(dst, m["hs"][:].rearrange("p (t s l) -> p t s l", t=2, s=k.seqs)[:, :, :, k.len - 1])
                if lv == 3:
                    ssd_y()
                if lv == 4:
                    k.need("ssdst")
                    for h in range(4):
                        o = slice(h * 64, h * 64 + 64)
                        stt(ssd_h[:, o], ssd_h[:, o], cur[:, ETOT + h:ETOT + h + 1], banks[:, 6, o], ALU.mult, ALU.add)
                    s5_forward(0)
                if lv == 5:
                    s5_forward(1)
                for pr_, b in ((0, 1), (1, 3)):
                    k.need(f"y{pr_}", lv + 1)
                    w = 512 if lv < top - 1 else 256
                    o = slice(pr_ * 512, pr_ * 512 + w)
                    tt(m["ST"][:, o], m["ST"][:, o], banks[:, b, 0:w], ALU.subtract).then_inc(ms[f"ss{pr_}"], 1)
            if s_:
                s5_forward(0)
                s5_forward(1)
                ssd_y()
            k.need("uw_sb")
            k.need("ws_b")
            uu = m["uu"]
            if s_:
                tt(m["delta"][:], uu[:], banks[:, 0, 0:256], ALU.subtract)
                eng.drain()
                eng.tensor_copy(uu[:], banks[:, 0, 256:512])
                eng.drain().then_inc(ms["delta"], 1)
            else:
                tt(m["delta"][:], uu[:], banks[:, 3, 256:512], ALU.subtract).then_inc(ms["delta"], 1)
            k.need("s5yb")
            k.need("xsd", 2)
            tt(m["s5y"][:], m["s5y"][:], banks[:, 4, 0:256], ALU.add).then_inc(ms["s5ys"], 1)
            k.need("rs")
            eng.reciprocal(m["n8"][:, 0:2], m["n8"][:, 0:2])
            eng.drain()
            for g in range(2):
                o = slice(g * P, g * P + P)
                stt(m["ytm"][:, o], m["ys"][:, o], m["n8"][:, g:g + 1], mc("ssd_norm", g * P, P), ALU.mult, ALU.mult)
            eng.drain().then_inc(ms["ytm"], 1)
            k.need("gg")
            k.need("y_out", 0)
            tt(ych[:, 0:2, :].rearrange("p a t -> p (a t)"), m["hs"][:], m["gg"][:], ALU.mult).then_inc(ms["lruy"], 1)
            k.need("ob")
            if s_:
                tt(uu[:], uu[:], banks[:, 6, 256:512], ALU.add).then_inc(ms["osum"], 1)
            k.need("gsq")
            eng.tensor_reduce(m["n8"][:, 8:12], heads(m["sqk"][:, 0:256]), AX_X, ALU.add).then_inc(ms["ss"], 1)

            def gdn_state(j, state, total):
                for half in range(2):
                    r = slice(half * 64, half * 64 + 64)
                    h = 2 * j + half
                    stt(state[r, j, r], state[r, j, r], total[r, 4 + h:5 + h],
                        banks[r, 7, j * P + half * 64:j * P + half * 64 + 64], ALU.mult, ALU.add)

            if not s_:
                k.need("gst")
                for j in range(2):
                    gdn_state(j, gdn_s, cur[:, ETOT:ETOT + 8])
            s5_gate(eng, k)
            k.need("grs")
            eng.reciprocal(m["n8"][:, 8:12], m["n8"][:, 8:12])
            eng.drain()
            o = uu[:] if s_ else banks[:, 6, 256:512]
            tt(heads(m["yo"][:]), heads(o), per_head(m["n8"][:, 8:12], 4), ALU.mult)
            eng.drain()
            k.need("gz")
            tt(m["ytm"][:, 256:512], m["yo"][:], m["gz"][:], ALU.mult).then_inc(ms["ytm"], 1)
            if s_:
                for s in range(SEQS):
                    if s:
                        k.need("stp", s)
                    sel = mc("seqsel", s, 1)
                    eng.tensor_scalar(m["kb"][:], m["kd"][:], sel, None, ALU.mult)
                    eng.tensor_scalar(m["qd"][:], m["xw"][:], sel, None, ALU.mult)
                    eng.drain().then_inc(ms["sel"], 1)
                    k.need("stp", s + 1)
                    for j in range(2):
                        gdn_state(j, gdn_ss[:, s], etotb[:, s, :])
                    for h in range(4):
                        o = slice(h * 64, h * 64 + 64)
                        stt(ssd_hs[:, s, o], ssd_hs[:, s, o], etotb[:, s, h:h + 1],
                            banks[:, 7, 256 + h * 64:256 + h * 64 + 64], ALU.mult, ALU.add)
                    eng.drain()
                tails = u_buf[:, CONV:CONV + N_CONV, 0:SEQS * (SEQ_LEN + 3)].rearrange("p t (s w) -> p t s w", s=SEQS)
                eng.tensor_copy(m["tail"][:].rearrange("p (t s w) -> p t s w", t=N_CONV, s=SEQS), tails[:, :, :, SEQ_LEN:])

        def s5_gate(eng, k):
            k.need("gelu_gate", 2)
            g = m["sqk"][:, 256:512]
            eng.tensor_scalar(g, g, 0.5, 0.5, ALU.mult, ALU.add)
            eng.drain()
            eng.tensor_tensor(ych[:, 6:8, :].rearrange("p a t -> p (a t)"), m["s5t"][:], g, ALU.mult).then_inc(ms["s5done"], 1)

        def dve_stage_m(eng, c, p):
            dve_tokens_scalars(eng, p)
            eng.wait_ge(prep_in, 32 * (p + 1))
            eng.tensor_scalar(mc("ct_im"), mc("ct_im"), -1.0, None, ALU.mult)
            eng.tensor_copy(v3(m["decay5"][:], 8), mag[:].unsqueeze(2).to_broadcast([P, 8, P]))
            eng.drain()
            eng.memset(v3(m["decay5"][:], 8)[:, :, 0:1], 0.0)
            chunks(eng, c, p, dve_chunk)

        def pool_chunk(eng, k):
            s_ = k.sample
            tt = eng.tensor_tensor
            k.need("u_in")
            for grp in GROUPS:
                for j in range(*grp):
                    out, src = k.by_seq(cv[:, j, :]), k.window(CONV + j, 0)
                    if j == GROUPS[0][0]:
                        tt(out, src, pcol("conv_w", j).unsqueeze(2).to_broadcast([P, k.seqs, k.len]), ALU.mult)
                    else:
                        last = eng.tensor_scalar(out, src, pcol("conv_w", j), pcol("conv_b", j), ALU.mult, ALU.add)
                last.then_inc(ms["tap0"], 1)
            k.need("cur")
            later = mc("Ls" if s_ else "L")
            tt(lg[:, 0, :], later, cur[:, G8:G8 + 1].to_broadcast([P, P]), ALU.mult)
            for h in range(1, 8):
                eng.tensor_scalar(lg[:, h, :], later, cur[:, G8 + h:G8 + h + 1], None, ALU.mult)
            eng.drain().then_inc(ms["lg"], 1)
            k.need("bu_sb", 2)
            tt(v4(k, p2[:]), v4(k, bim[:]), rotation(k, 1), ALU.mult)
            tt(v4(k, p4[:]), v4(k, bre[:]), rotation(k, 1), ALU.mult)
            eng.drain().then_inc(ms["rot_p"], 1)
            k.need("dec_x", 1)
            mask = mc("Us" if s_ else "U").unsqueeze(1).to_broadcast([P, 4, P])
            strict = mc("stricts" if s_ else "strict").unsqueeze(1).to_broadcast([P, 4, P])
            tt(dec[:, 4:8, :], dec[:, 4:8, :], mask, ALU.mult)
            eng.drain()
            tt(v3(m["decs"][:], 4), dec[:, 4:8, :], strict, ALU.mult)
            eng.drain().then_inc(ms["dec_m"], 1)
            k.need("dec_x", 2)
            tt(dec[:, 0:4, :], dec[:, 0:4, :], mask, ALU.mult).then_inc(ms["dec_m"], 1)
            k.need("kq_dec", 1)
            for b in range(1, levels_of(s_) + 1):
                lm = mc("levels", b * P, P).unsqueeze(1).to_broadcast([P, 4, P])
                tt(v3(m["ML"][:, b * 512:b * 512 + 512], 4), v3(m["MT"][:], 4), lm, ALU.mult).then_inc(ms["ml"], 1)
                if b == 2:
                    k.need("turned_sb", 4)
                    tt(m["xsd"][:], m["tok_x"][:, 0:256], mc("ssd_d"), ALU.mult).then_inc(ms["xsd"], 1)
                if b == 3:
                    k.need("rot_z")
                    tt(v4(k, p2[:]), v4(k, bim[:]), rotation(k, 1), ALU.mult)
                    tt(v4(k, p4[:]), v4(k, bre[:]), rotation(k, 1), ALU.mult)
                    eng.drain().then_inc(ms["rot_q"], 1)
            for j in range(2):
                last = tt(k.by_seq(m["s5y"][:, j * P:j * P + P]), k.window(DU + j),
                          pcol("s5_d", j).unsqueeze(2).to_broadcast([P, k.seqs, k.len]), ALU.mult)
            last.then_inc(ms["xsd"], 1)
            k.need("sz")
            tt(m["gz"][:], m["sz"][:, 256:512], mc("gdn_norm"), ALU.mult).then_inc(ms["gz"], 1)
            k.need("ssdy")

        def pool_stage_m(eng, c, p):
            chunks(eng, c, p, pool_chunk)

        def sp_chunk(eng, k):
            t0 = k.first_token()
            k.need("gg", 0)
            k.need("xsd", 0)
            if k.sample:
                for tile in range(U_TILES):
                    eng.dma_start(k.window(tile), k.by_seq(u_dram[:, tile, 3 + t0:3 + t0 + P])).then_inc(sample_in, 16)
                halo = u_buf[:, CONV:CONV + N_CONV, 0:SEQS * (SEQ_LEN + 3)].rearrange("p t (s w) -> p (t s) w", s=SEQS)
                eng.dma_start(halo[:, :, 0:3], t["conv_caches"]).then_inc(sample_in, 16)
                for name in ("ssd_hs", "gdn_ss", "s5_xs", "lru_hs"):
                    eng.dma_start(m[name][:], t[name]).then_inc(sample_in, 16)
            else:
                eng.dma_start(u_buf[:, :, 0:P + 3], u_dram[:, :, bass.ds(t0, P + 3)]).then_inc(ms["u_in"], 16)
            eng.dma_start(m["z"][:], z_dram[bass.ds(t0, P), :]).then_inc(ms["z_in"], 16)

        def sp_stage_m(eng, c, p):
            eng.dma_start(mixc[:], t["mixc"]).then_inc(prep_in, 16)
            eng.dma_start(mprep[:].rearrange("p a b c -> p (a b c)"), prep_dram).then_inc(prep_in, 16)
            chunks(eng, c, p, sp_chunk, loads=True)
            if p == len(PASSES) - 1:
                outs = [("p_ssd", ssd_h[:]), ("p_gdn", gdn_s[:].rearrange("p a b -> p (a b)")),
                        ("p_s5", s5_x[:].rearrange("p a b -> p (a b)")), ("p_lru", lru_h[:]),
                        ("p_tail", u_dram[:, CONV:CONV + N_CONV, PROMPT:PROMPT + 3]),
                        ("s_tail", m["tail"][:]), ("s_ssd", m["ssd_hs"][:]), ("s_gdn", m["gdn_ss"][:]),
                        ("s_s5", m["s5_xs"][:]), ("s_lru", m["lru_hs"][:])]
                for name, src in outs:
                    eng.dma_start(t[name], src).then_inc(finals_stored, 16)
                eng.wait_ge(finals_stored, 16 * len(outs))

        are, aim, ldt = (s5p[:, j, :] for j in range(3))
        (w_step, w_mag, w_ang, w_k, w_r, w_sin, w_half, w_cos, w_den, w_fr, w_fi, w_t1, w_t2, w_t3) = (w[:] for w in sw)
        prep_flat = prep[:].rearrange("p a b c -> p (a b c)")

        def act_setup(eng, c):
            eng.wait_ge(par_loaded, 16 * 4)
            eng.activation(w_step, ldt, ACT.Exp)
            eng.activation(sm[:, 2:4], pcol("lam", 0, 2), ACT.Abs)
            eng.drain()
            eng.activation(sm[:, 4:6], sm[:, 2:4], ACT.Exp, scale=-1.0)
            eng.activation(nea8[:], pcol("alog8", 0, 8), ACT.Exp)
            eng.drain().then_inc(setup_act, 1)
            eng.wait_ge(setup_dve, 1)
            eng.activation(w_mag, w_t1, ACT.Exp)
            eng.drain().then_inc(setup_act, 1)
            eng.wait_ge(setup_dve, 2)
            eng.activation(w_sin, w_r, ACT.Sin)
            eng.activation(w_half, w_r, ACT.Sin, scale=0.5)
            eng.drain().then_inc(setup_act, 1)
            bank_in(eng, c, 3)
            eng.activation(prep_flat[:, 0:2048], banks[:, 0:4, :].rearrange("p b c -> p (b c)"), ACT.Copy).then_inc(setup_act, 1)

        def pe_setup(eng, c):
            eng.wait_ge(setup_dve, 3)
            for part in range(2):
                for s in range(8):
                    j = (part * 8 + s) * P
                    last = eng.transpose(banks[:, j // 512, j % 512:j % 512 + P], bb[:, part, s, :], ident_s[:])
            last.then_inc(full_s[3], 1)

        def exp_exact(eng, out, src):
            n, r, e = ex[:, 0], ex[:, 1], ex[:, 2]
            eng.tensor_scalar(n, src, float(1 / np.log(2)), ROUND_MAGIC, ALU.mult, ALU.add)
            eng.drain()
            eng.tensor_scalar(n, n, ROUND_MAGIC, -126.0, ALU.subtract, ALU.max)
            eng.drain()
            eng.tensor_scalar(n, n, 127.0, None, ALU.min)
            eng.drain()
            eng.scalar_tensor_tensor(r, n, -LN2_HI, src, ALU.mult, ALU.add)
            eng.drain()
            eng.scalar_tensor_tensor(r, n, -LN2_LO, r, ALU.mult, ALU.add)
            eng.memset(e, 1.0 / 9)
            for d in range(8, 0, -1):
                eng.drain()
                eng.tensor_tensor(e, e, r, ALU.mult)
                eng.drain()
                eng.tensor_scalar(e, e, 1.0, 1.0 / d, ALU.add, ALU.mult)
            eng.drain()
            eng.tensor_tensor(e, e, r, ALU.mult)
            eng.tensor_scalar(exi[:], n, 127.0, 8388608.0, ALU.add, ALU.mult)
            eng.drain()
            eng.tensor_scalar(e, e, 1.0, None, ALU.add)
            eng.drain()
            eng.tensor_tensor(out, e, exi[:].bitcast(F32), ALU.mult)

        def dve_setup(eng):
            tt, ts, stt = eng.tensor_tensor, eng.tensor_scalar, eng.scalar_tensor_tensor
            eng.memset(ones[:], 1.0)
            eng.memset(eps[:], EPS)
            eng.memset(ssd_h[:], 0.0)
            eng.memset(gdn_s[:], 0.0)
            eng.memset(s5_x[:], 0.0)
            eng.memset(lru_h[:], 0.0)
            eng.memset(zero3[:], 0.0)
            for s in free_s:
                eng.sem_inc(s, 1)
            for name in ("y_out", "gg", "xsd", "ych"):
                eng.sem_inc(ms[name], 1)
            eng.wait_ge(setup_act, 1)
            exp_exact(eng, w_step, ldt)
            eng.drain()
            tt(w_t1, are, w_step, ALU.mult).then_inc(setup_dve, 1)
            tt(w_ang, aim, w_step, ALU.mult)
            eng.drain()
            ts(w_k, w_ang, float(1 / (2 * np.pi)), ROUND_MAGIC, ALU.mult, ALU.add)
            eng.drain()
            ts(w_k, w_k, ROUND_MAGIC, None, ALU.subtract)
            eng.drain()
            stt(w_r, w_k, -TWO_PI_HI, w_ang, ALU.mult, ALU.add)
            eng.drain()
            stt(w_r, w_k, -TWO_PI_MID, w_r, ALU.mult, ALU.add)
            eng.drain()
            stt(w_r, w_k, -float(TWO_PI_LO), w_r, ALU.mult, ALU.add)
            eng.drain().then_inc(setup_dve, 1)
            tt(w_t2, are, are, ALU.mult)
            tt(w_t3, aim, aim, ALU.mult)
            eng.drain()
            tt(w_den, w_t2, w_t3, ALU.add)
            eng.drain()
            eng.reciprocal(w_den, w_den)
            z, z2, acc = sm[:, 6:8], sm[:, 8:10], sm[:, 10:12]
            e = sm[:, 4:6]
            ts(z, e, 2.0, None, ALU.add)
            eng.drain()
            eng.reciprocal(z, z)
            eng.drain()
            tt(z, z, e, ALU.mult)
            eng.drain()
            tt(z2, z, z, ALU.mult)
            artanh(eng, acc, z2)
            eng.drain()
            tt(acc, acc, z, ALU.mult)
            ts(sm[:, 0:2], pcol("lam", 0, 2), -1.0, 0.0, ALU.mult, ALU.max)
            eng.drain()
            stt(sm[:, 0:2], acc, 2.0, sm[:, 0:2], ALU.mult, ALU.add)
            eng.drain()
            ts(lru_c[:, 0:2], sm[:, 0:2], -4.0, None, ALU.mult)
            ts(lru_c[:, 2:4], sm[:, 0:2], 4.0, None, ALU.mult)
            for j, name in enumerate(("b_r", "b_i", "b_glu")):
                ts(half_b[:, 2 * j:2 * j + 2], pcol(name, 0, 2), 0.5, None, ALU.mult)
            ts(nea8[:], nea8[:], -1.0, None, ALU.mult)
            eng.wait_ge(setup_act, 3)
            tt(w_t2, w_half, w_half, ALU.mult)
            eng.drain()
            ts(w_cos, w_t2, -2.0, 1.0, ALU.mult, ALU.add)
            exp_exact(eng, mag[:], w_t1)
            eng.drain()
            tt(w_t1, w_mag, w_cos, ALU.mult)
            tt(w_t2, w_mag, w_sin, ALU.mult)
            eng.drain()
            ts(w_t1, w_t1, -1.0, None, ALU.add)
            eng.drain()
            tt(w_fr, w_t1, are, ALU.mult)
            tt(w_t3, w_t2, aim, ALU.mult)
            eng.drain()
            tt(w_fr, w_fr, w_t3, ALU.add)
            tt(w_fi, w_t2, are, ALU.mult)
            eng.drain()
            tt(w_t3, w_t1, aim, ALU.mult)
            tt(w_fr, w_fr, w_den, ALU.mult)
            eng.drain()
            tt(w_fi, w_fi, w_t3, ALU.subtract)
            eng.drain()
            tt(w_fi, w_fi, w_den, ALU.mult)
            eng.drain()
            fr, fi = (f.unsqueeze(2).to_broadcast([P, 8, P]) for f in (w_fr, w_fi))
            b_re, b_im, t2, t3 = v3(s5b[:, 0, :], 8), v3(s5b[:, 1, :], 8), v3(bt[:, 0, :], 8), v3(bt[:, 1, :], 8)
            tt(bb[:, 0], fr, b_re, ALU.mult)
            tt(t2, fi, b_im, ALU.mult)
            tt(bb[:, 1], fr, b_im, ALU.mult)
            tt(t3, fi, b_re, ALU.mult)
            eng.drain()
            tt(bb[:, 0], bb[:, 0], t2, ALU.subtract)
            tt(bb[:, 1], bb[:, 1], t3, ALU.add)
            eng.drain().then_inc(setup_dve, 1)
            cos, sin = prep[:, 2], prep[:, 3]
            eng.tensor_copy(cos[:, :, 0], w_cos)
            eng.tensor_copy(sin[:, :, 0], w_sin)
            eng.drain()
            n = 1
            while n < P:
                cn = cos[:, :, n - 1:n].to_broadcast([P, 8, n])
                sn = sin[:, :, n - 1:n].to_broadcast([P, 8, n])
                ta, tb = v3(bt[:, 0, 0:8 * n], 8), v3(bt[:, 1, 0:8 * n], 8)
                tt(ta, sin[:, :, 0:n], sn, ALU.mult)
                tt(tb, cos[:, :, 0:n], sn, ALU.mult)
                tt(cos[:, :, n:2 * n], cos[:, :, 0:n], cn, ALU.mult)
                tt(sin[:, :, n:2 * n], sin[:, :, 0:n], cn, ALU.mult)
                eng.drain()
                tt(cos[:, :, n:2 * n], cos[:, :, n:2 * n], ta, ALU.subtract)
                tt(sin[:, :, n:2 * n], sin[:, :, n:2 * n], tb, ALU.add)
                eng.drain()
                n *= 2
            eng.drain().then_inc(setup_dve, 1)

        def sp_setup(eng):
            eng.dma_start(par[:], t["par"]).then_inc(par_loaded, 16)
            eng.dma_start(s5p[:], t["s5p"]).then_inc(par_loaded, 16)
            eng.dma_start(s5b[:], t["s5b"]).then_inc(par_loaded, 16)
            eng.dma_start(ident_s[:], t["mixc"][:, MIX["ident"][0]:MIX["ident"][0] + P]).then_inc(par_loaded, 16)
            eng.wait_ge(setup_dve, 4)
            eng.wait_ge(setup_act, 4)
            eng.dma_start(u_dram[:, :, 0:3], zero3[:]).then_inc(par_loaded, 16)
            eng.dma_start(prep_dram, prep_flat).then_inc(par_loaded, 16)
            eng.wait_ge(par_loaded, 16 * 6)

        block = ctx.enter_context(nc.Block())

        @block.tensor
        def _(pe):
            c = Counts(pe)
            pe_setup(pe, c)
            c.meet()
            pe_stage_kv(pe, c)
            c.meet()
            for p in range(len(PASSES)):
                pe_stage_a(pe, c, p)
                c.meet()
                pe_stage_m(pe, c, p)
                c.meet()
                pe_stage_b(pe, c, p)
                c.meet()

        @block.scalar
        def _(act):
            c = Counts(act)
            act_setup(act, c)
            c.meet()
            act_stage_kv(act, c)
            c.meet()
            for p in range(len(PASSES)):
                act_stage_a(act, c, p)
                c.meet()
                act_stage_m(act, c, p)
                c.meet()
                act_stage_b(act, c, p)
                c.meet()

        @block.vector
        def _(dve):
            c = Counts(dve)
            dve_setup(dve)
            c.full[3].n += 1
            c.meet()
            dve_stage_kv(dve, c)
            c.meet()
            for p in range(len(PASSES)):
                dve_stage_a(dve, c, p)
                c.meet()
                dve_stage_m(dve, c, p)
                c.meet()
                dve_stage_b(dve, c, p)
                c.meet()

        @block.gpsimd
        def _(pool):
            c = Counts(pool)
            c.meet()
            pool_stage_kv(pool, c)
            c.meet()
            for p in range(len(PASSES)):
                pool_stage_a(pool, c, p)
                c.meet()
                pool_stage_m(pool, c, p)
                c.meet()
                pool_stage_b(pool, c, p)
                c.meet()

        @block.sync
        def _(sp):
            c = Counts(sp)
            sp_setup(sp)
            c.meet()
            sp_stage_kv(sp, c)
            c.meet()
            for p in range(len(PASSES)):
                sp_stage_a(sp, c, p)
                c.meet()
                sp_stage_m(sp, c, p)
                c.meet()
                sp_stage_b(sp, c, p)
                c.meet()


def channel_major(a, tiles):
    return np.ascontiguousarray(a.reshape(a.shape[0], tiles, P).transpose(2, 1, 0))


def column_slab(w):
    return w.reshape(KD, P, 256).transpose(1, 0, 2).reshape(P, SLAB)


def row_slab(w):
    return w.reshape(2, P, D).transpose(1, 0, 2).reshape(P, SLAB)


def by_channel(v):
    return v.reshape(-1, P).T


def rows(v):
    return np.tile(v.reshape(1, -1), (P, 1))


def lay_out(a):
    f = np.float32
    a = {k: np.asarray(v) for k, v in a.items()}
    o = {}
    tokens = np.concatenate([a["x_prompt"][0], a["x_sample"].reshape(SEQS * SEQ_LEN, D)])
    o["x_t"] = channel_major(tokens, KD)
    o["mem_t"] = channel_major(a["mem_prompt"][0], KD)
    w = a["w_in"][0]
    starts = [0, 256] + [768 + 256 * j for j in range(3)] + [1540 + 256 * j for j in range(3)] + [2572, 512, 2308]
    o["w_in"] = np.stack([column_slab(w[:, s:s + 256]) for s in starts])
    small = np.concatenate([w[:, 1536:1540], w[:, 2568:2572], w[:, 2564:2568]], axis=1)
    o["w_small"] = small.reshape(KD, P, N_SMALL).transpose(1, 0, 2).reshape(P, -1)
    cols = lambda w, n: [column_slab(w[:, j * 256:j * 256 + 256]) for j in range(n)]
    rws = lambda w, n: [row_slab(w[j * 256:j * 256 + 256]) for j in range(n)]
    o["w_kv"] = np.stack(cols(a["w_ck"][0], 4) + cols(a["w_cv"][0], 4))
    gate, up = cols(a["w_ffn_gate"][0], ROUNDS), cols(a["w_ffn_up"][0], ROUNDS)
    o["w_a"] = np.stack(cols(a["w_out"][0], 4) + cols(a["w_cq"][0], 4) + [s for pair in zip(gate, up) for s in pair])
    o["w_b"] = np.stack(rws(a["w_co"][0], 4) + rws(a["w_ffn_down"][0], ROUNDS))
    o["k_cache_t"] = (a["cache_mem_k"][0].transpose(2, 0, 3, 1).reshape(HEADS, SEQS, 2, P, MEM)
                      .transpose(0, 1, 3, 2, 4).reshape(HEADS, SEQS, P, 512))
    o["v_cache"] = (a["cache_mem_v"][0].transpose(2, 0, 1, 3).reshape(HEADS, SEQS, 2, P, HD)
                    .transpose(0, 1, 3, 2, 4).reshape(HEADS, SEQS, P, 512))

    def fill(table, parts, width):
        out = np.zeros((P, width), f)
        for name, v in parts.items():
            c0, n = table[name]
            out[:, c0:c0 + n] = v
        return out

    t_ = np.arange(P)
    same = (t_[:, None] // SEQ_LEN) == (t_[None, :] // SEQ_LEN)
    upper, strict, lower = t_[:, None] <= t_[None, :], t_[:, None] < t_[None, :], t_[:, None] > t_[None, :]
    lev = [((t_[:, None] // (2 * b)) == (t_[None, :] // (2 * b))) & (t_[None, :] // b % 2 == 1)
           & (t_[:, None] // b % 2 == 0) for b in LEVELS]
    ct = {}
    for part in ("re", "im"):
        c = np.zeros((P, 8, P), f)
        for g in range(16):
            ch = g * 16 % P
            c[g % 2 * 64:g % 2 * 64 + 64, g // 2, ch:ch + 16] = a["s5_c_" + part][0][g].T
        ct[part] = c.reshape(P, -1)
    lru = {}
    for name in ("w_r", "w_i"):
        c = np.zeros((P, 2, P), f)
        for b in range(4):
            r = slice(b % 2 * 64, b % 2 * 64 + 64)
            c[r, b // 2, r] = a["lru_" + name][0][b]
        lru[name] = c.reshape(P, -1)
    o["mixc"] = fill(MIX, dict(
        U=upper, L=lower, strict=strict, Us=upper & same, Ls=lower & same, stricts=strict & same, ident=np.eye(P),
        ones=1.0, levels=np.stack(lev, 1).reshape(P, -1), seqsel=t_[:, None] // SEQ_LEN == np.arange(SEQS)[None, :],
        ct_re=ct["re"], ct_im=ct["im"], glu=a["s5_w_glu"][0].reshape(2, P, 256).transpose(1, 0, 2).reshape(P, 512),
        w_r=lru["w_r"], w_i=lru["w_i"], ssd_norm=rows(a["ssd_norm_g"][0]), gdn_norm=rows(np.tile(a["gdn_norm_g"][0], 4)),
        ssd_d=rows(np.repeat(a["ssd_d"][0], 64))), MIX_COLS)
    conv_w = np.concatenate([a["lru_conv_w"][0], a["ssd_conv_w"][0], a["gdn_conv_w"][0]], axis=1)
    conv_b = np.concatenate([a["lru_conv_b"][0], a["ssd_conv_b"][0], np.zeros(768, f)])
    o["par"] = fill(PAR, dict(
        conv_w=np.concatenate([by_channel(conv_w[j]) for j in range(4)], axis=1), conv_b=by_channel(conv_b),
        s5_d=by_channel(a["s5_d"][0]), b_glu=by_channel(a["s5_b_glu"][0]), b_r=by_channel(a["lru_b_r"][0]),
        b_i=by_channel(a["lru_b_i"][0]), lam=by_channel(a["lru_lambda"][0]),
        bias8=rows(np.concatenate([a["ssd_dt_bias"][0], a["gdn_dt_bias"][0]])),
        alog8=rows(np.concatenate([a["ssd_a_log"][0], a["gdn_a_log"][0]])),
        g_mix=by_channel(a["norm_mix_g"][0]), g_mem=by_channel(a["norm_mem_g"][0]),
        g_cross=by_channel(a["norm_cross_g"][0]), g_ffn=by_channel(a["norm_ffn_g"][0]),
        g_final=by_channel(a["norm_final_g"])), PAR_COLS)
    states = [a["s5_a_re"][0].reshape(-1), a["s5_a_im"][0].reshape(-1), np.repeat(a["s5_log_dt"][0], 64)]
    o["s5p"] = np.stack([by_channel(v) for v in states], axis=1)
    s5b = np.zeros((P, 2, 8, P), f)
    for part, name in enumerate(("s5_b_re", "s5_b_im")):
        for g in range(16):
            ch = g * 16 % P
            s5b[g % 2 * 64:g % 2 * 64 + 64, part, g // 2, ch:ch + 16] = a[name][0][g]
    o["s5b"] = s5b.reshape(P, 2, 1024)
    caches = np.concatenate([a["cache_lru_conv"][0], a["cache_ssd_conv"][0], a["cache_gdn_conv"][0]], axis=2)
    o["conv_caches"] = (caches.transpose(2, 0, 1).reshape(N_CONV, P, SEQS, 3).transpose(1, 0, 2, 3)
                        .reshape(P, N_CONV * SEQS, 3))
    o["ssd_hs"] = a["state_ssd"][0].transpose(3, 0, 1, 2).reshape(P, -1)
    g = np.zeros((2, 64, SEQS, 2, 2, 64), f)
    s = a["state_gdn"][0].reshape(SEQS, 2, 2, 64, 64)
    for half in range(2):
        g[half, :, :, :, half] = s[:, :, half].transpose(2, 0, 1, 3)
    o["gdn_ss"] = g.reshape(P, -1)
    o["s5_xs"] = np.concatenate([a["state_s5_" + part][0].reshape(SEQS, 8, P).transpose(2, 1, 0).reshape(P, -1)
                                 for part in ("re", "im")], axis=1)
    o["lru_hs"] = a["state_lru_h"][0].reshape(SEQS, 2, P).transpose(2, 1, 0).reshape(P, -1)
    return {k: np.ascontiguousarray(v, dtype=f) for k, v in o.items()}


OUTPUTS = dict(y_t=[P, KD, TOKENS], p_mem_kt=[D, MEM], p_mem_v=[MEM, D], p_ssd=[P, 256], p_gdn=[P, 256],
               p_s5=[P, 16], p_lru=[P, 2], p_tail=[P, N_CONV, 3], s_tail=[P, N_CONV * SEQS * 3],
               s_ssd=[P, SEQS * 256], s_gdn=[P, SEQS * 256], s_s5=[P, 16 * SEQS], s_lru=[P, 2 * SEQS])


def unpack(r):
    y = r["y_t"].transpose(2, 1, 0).reshape(TOKENS, D)

    def states(lru, tail, ssd, gdn, s5, n):
        conv = tail.reshape(P, N_CONV, n, 3).transpose(2, 3, 1, 0).reshape(n, 3, N_CONV * P)
        g = gdn.reshape(2, 64, n, 2, 2, 64)
        g = np.stack([g[half, :, :, :, half] for half in range(2)])
        s5 = s5.reshape(P, 2, 8, n).transpose(1, 3, 2, 0).reshape(2, n, 16, 64)
        out = (lru.reshape(P, 2, n).transpose(2, 1, 0).reshape(n, 256), conv[:, :, 0:256],
               ssd.reshape(P, n, 4, 64).transpose(1, 2, 3, 0), conv[:, :, 256:1024],
               g.transpose(2, 3, 0, 1, 4).reshape(n, 4, 64, 64), conv[:, :, 1024:1792], s5[0], s5[1])
        return tuple(np.ascontiguousarray(v)[None] for v in out)

    mem_k = np.ascontiguousarray(r["p_mem_kt"].T).reshape(1, 1, MEM, HEADS, HD)
    mem_v = r["p_mem_v"].reshape(1, 1, MEM, HEADS, HD)
    return ((np.ascontiguousarray(y[:PROMPT])[None], np.ascontiguousarray(y[PROMPT:]).reshape(SEQS, SEQ_LEN, D))
            + states(r["p_lru"], r["p_tail"], r["p_ssd"], r["p_gdn"], r["p_s5"], 1) + (mem_k, mem_v)
            + states(r["s_lru"], r["s_tail"], r["s_ssd"], r["s_gdn"], r["s_s5"], SEQS))


def kernel(**inputs):
    from concourse import bacc
    from concourse.bass_utils import run_bass_kernel_spmd

    nc = bacc.Bacc("TRN2", target_bir_lowering=False, num_devices=1)
    arrays = lay_out(inputs)
    t = {name: nc.dram_tensor(name, list(a.shape), F32, kind="ExternalInput").ap() for name, a in arrays.items()}
    t.update((name, nc.dram_tensor(name, shape, F32, kind="ExternalOutput").ap()) for name, shape in OUTPUTS.items())
    program(nc, t)
    r = run_bass_kernel_spmd(nc, [arrays], core_ids=[0])
    return unpack(r.results[0])
```
